# Optimizing a Trainium2 kernel written in Bass

```python
import math
import jax, jax.numpy as jnp
from jax import lax
import numpy as np
import math, functools

D_MODEL = 1024
BATCH = 1
SEQ = 256
DEPTH = 2

HEAD_DIM = 64
H_SB = 4
H_FOX = 4
H_MLA = 4
H_DIL = 4
N_HEADS_OUT = H_SB + H_FOX + H_MLA + H_DIL
D_MIX = N_HEADS_OUT * HEAD_DIM
Q_BLOCK = 128
ROPE_THETA = 10000.0
MLA_Q_LORA = 256
MLA_KV_LORA = 128
MLA_NOPE = 64
MLA_ROPE = 32
MLA_V = HEAD_DIM
DIL_BRANCHES = ((128, 1), (512, 4), (2048, 16))
N_BR = len(DIL_BRANCHES)
N_SB = 3 * H_SB * HEAD_DIM
N_FOX = 3 * H_FOX * HEAD_DIM + H_FOX
N_MLA = MLA_Q_LORA + MLA_KV_LORA + MLA_ROPE
N_DIL = 3 * N_BR * H_DIL * HEAD_DIM
N_IN = N_SB + N_FOX + N_MLA + N_DIL
N_GROUPS = 4
EXPERTS_PER_GROUP = 4
N_EXPERTS = N_GROUPS * EXPERTS_PER_GROUP
TOP_K = 2
D_EXPERT = 512
MOE_BLOCK = 256
LN_EPS = 1e-5
RMS_EPS = 1e-6


def _layernorm(x, g, b):
    xf = x.astype(jnp.float32)
    mu = jnp.mean(xf, -1, keepdims=True)
    var = jnp.mean(jnp.square(xf - mu), -1, keepdims=True)
    return ((xf - mu) * lax.rsqrt(var + LN_EPS) * g + b).astype(x.dtype)

def _rmsnorm(x, g):
    xf = x.astype(jnp.float32)
    return (xf * lax.rsqrt(jnp.mean(jnp.square(xf), -1, keepdims=True) + RMS_EPS) * g).astype(x.dtype)

def _rope(x, pos):
    half = x.shape[-1] // 2
    inv_freq = ROPE_THETA ** (-jnp.arange(half, dtype=jnp.float32) / half)
    ang = pos.astype(jnp.float32)[:, None] * inv_freq[None, :]
    cos = jnp.cos(ang)[None, :, None, :]
    sin = jnp.sin(ang)[None, :, None, :]
    xf = x.astype(jnp.float32)
    x1, x2 = xf[..., :half], xf[..., half:]
    return jnp.concatenate([x1 * cos - x2 * sin, x2 * cos + x1 * sin], -1).astype(x.dtype)

def _sweep(block_fn, seq):
    out = lax.map(block_fn, jnp.arange(seq // Q_BLOCK, dtype=jnp.int32) * Q_BLOCK)
    nb, b, h, blk, dv = out.shape
    return out.transpose(1, 2, 0, 3, 4).reshape(b, h, nb * blk, dv)

def _causal_softmax_sweep(logits_fn, v):
    seq = v.shape[2]
    kpos = jnp.arange(seq)

    def block(t0):
        logits = logits_fn(t0)
        qpos = t0 + jnp.arange(Q_BLOCK)
        mask = kpos[None, :] <= qpos[:, None]
        p = jax.nn.softmax(jnp.where(mask, logits, -jnp.inf), axis=-1)
        return jnp.einsum('bhqk,bhkd->bhqd', p.astype(v.dtype), v)

    return _sweep(block, seq)

def _stick_breaking_attention(q, k, v):
    seq = q.shape[2]
    scale = q.shape[-1] ** -0.5
    kpos = jnp.arange(seq)

    def block(t0):
        qb = lax.dynamic_slice_in_dim(q, t0, Q_BLOCK, axis=2)
        z = jnp.einsum('bhqd,bhkd->bhqk', qb, k).astype(jnp.float32) * scale
        qpos = t0 + jnp.arange(Q_BLOCK)
        before = kpos[None, :] < qpos[:, None]
        log_keep = jnp.where(before, jax.nn.log_sigmoid(-z), 0.0)
        log_after = lax.cumsum(log_keep, axis=3, reverse=True) - log_keep
        w = jnp.where(before, jnp.exp(jax.nn.log_sigmoid(z) + log_after), 0.0)
        return jnp.einsum('bhqk,bhkd->bhqd', w.astype(v.dtype), v)

    return _sweep(block, seq)

def _forgetting_attention(q, k, v, log_f):
    scale = q.shape[-1] ** -0.5
    c = jnp.cumsum(log_f, axis=-1)

    def logits(t0):
        qb = lax.dynamic_slice_in_dim(q, t0, Q_BLOCK, axis=2)
        cb = lax.dynamic_slice_in_dim(c, t0, Q_BLOCK, axis=2)
        s = jnp.einsum('bhqd,bhkd->bhqk', qb, k).astype(jnp.float32) * scale
        return s + cb[..., :, None] - c[..., None, :]

    return _causal_softmax_sweep(logits, v)

def _mla_attention(q_nope, q_rope, k_nope, k_rope, v):
    scale = (q_nope.shape[-1] + q_rope.shape[-1]) ** -0.5

    def logits(t0):
        qn = lax.dynamic_slice_in_dim(q_nope, t0, Q_BLOCK, axis=2)
        qr = lax.dynamic_slice_in_dim(q_rope, t0, Q_BLOCK, axis=2)
        s = (jnp.einsum('bhqd,bhkd->bhqk', qn, k_nope).astype(jnp.float32)
             + jnp.einsum('bhqr,bkr->bhqk', qr, k_rope).astype(jnp.float32))
        return s * scale

    return _causal_softmax_sweep(logits, v)

def _dilated_attention(qs, ks, vs):
    seq = qs[0].shape[1]
    scale = qs[0].shape[-1] ** -0.5

    def block(t0):
        qpos = t0 + jnp.arange(Q_BLOCK)
        outs, lses = [], []
        for (window, dil), q, k, v in zip(DIL_BRANCHES, qs, ks, vs):
            n_keys = window // dil + 1
            idx = qpos[:, None] - dil * jnp.arange(n_keys)[None, :]
            valid = idx >= 0
            idx = jnp.maximum(idx, 0)
            qb = lax.dynamic_slice_in_dim(q, t0, Q_BLOCK, axis=1)
            kb = jnp.take(k, idx, axis=1)
            vb = jnp.take(v, idx, axis=1)
            z = jnp.einsum('bqhd,bqnhd->bhqn', qb, kb).astype(jnp.float32) * scale
            z = jnp.where(valid[None, None], z, -jnp.inf)
            m = jnp.max(z, -1, keepdims=True)
            p = jnp.exp(z - m)
            den = jnp.sum(p, -1, keepdims=True)
            outs.append(jnp.einsum('bhqn,bqnhd->bhqd', (p / den).astype(v.dtype), vb).astype(jnp.float32))
            lses.append(m + jnp.log(den))
        mix = jax.nn.softmax(jnp.stack(lses), axis=0)
        return jnp.sum(mix * jnp.stack(outs), axis=0).astype(vs[0].dtype)

    return _sweep(block, seq)

def _mixing(x, w_in, b_forget, g_cq, g_ckv, w_uq, w_ukv, g_head, w_out):
    bsz, seq, _ = x.shape
    pos = jnp.arange(seq)
    proj = x @ w_in
    p_sb, p_fox, p_mla, p_dil = jnp.split(proj, [N_SB, N_SB + N_FOX, N_SB + N_FOX + N_MLA], axis=-1)

    def heads(t, n):
        return t.reshape(bsz, seq, n, -1).transpose(0, 2, 1, 3)

    q, k, v = jnp.split(p_sb, 3, axis=-1)
    o_sb = _stick_breaking_attention(heads(q, H_SB), heads(k, H_SB), heads(v, H_SB))

    hd = H_FOX * HEAD_DIM
    q, k, v, f = jnp.split(p_fox, [hd, 2 * hd, 3 * hd], axis=-1)
    log_f = jax.nn.log_sigmoid((f + b_forget).astype(jnp.float32)).transpose(0, 2, 1)
    o_fox = _forgetting_attention(heads(q, H_FOX), heads(k, H_FOX), heads(v, H_FOX), log_f)

    c_q, c_kv, k_r = jnp.split(p_mla, [MLA_Q_LORA, MLA_Q_LORA + MLA_KV_LORA], axis=-1)
    q = (_rmsnorm(c_q, g_cq) @ w_uq).reshape(bsz, seq, H_MLA, MLA_NOPE + MLA_ROPE)
    kv = (_rmsnorm(c_kv, g_ckv) @ w_ukv).reshape(bsz, seq, H_MLA, MLA_NOPE + MLA_V)
    q_rope = _rope(q[..., MLA_NOPE:], pos)
    k_rope = _rope(k_r[:, :, None, :], pos)[:, :, 0]
    tr = lambda a: a.transpose(0, 2, 1, 3)
    o_mla = _mla_attention(tr(q[..., :MLA_NOPE]), tr(q_rope), tr(kv[..., :MLA_NOPE]), k_rope,
                           tr(kv[..., MLA_NOPE:]))

    q, k, v = jnp.split(p_dil, 3, axis=-1)
    br = lambda a: a.reshape(bsz, seq, N_BR, H_DIL, HEAD_DIM)
    flat = lambda a: a.reshape(bsz, seq, N_BR * H_DIL, HEAD_DIM)
    q = br(_rope(flat(q), pos))
    k = br(_rope(flat(k), pos))
    v = br(v)
    o_dil = _dilated_attention([q[:, :, i] for i in range(N_BR)],
                               [k[:, :, i] for i in range(N_BR)],
                               [v[:, :, i] for i in range(N_BR)])

    o = jnp.concatenate([o_sb, o_fox, o_mla, o_dil], axis=1)
    o = _rmsnorm(o, g_head[None, :, None, :])
    return o.transpose(0, 2, 1, 3).reshape(bsz, seq, D_MIX) @ w_out

def _hier_moe(x, w_group, b_group, w_expert, b_expert, w1, w3, w2):
    n_tok, d = x.shape
    xf = x.astype(jnp.float32)
    g_logits = xf @ w_group.astype(jnp.float32) + b_group.astype(jnp.float32)
    g_sel = jnp.argmax(g_logits, axis=-1)
    g_w = jnp.take_along_axis(jax.nn.softmax(g_logits, -1), g_sel[:, None], axis=-1)
    e_logits = (xf @ w_expert.astype(jnp.float32) + b_expert.astype(jnp.float32)).reshape(
        n_tok, N_GROUPS, EXPERTS_PER_GROUP)
    e_in_group = jnp.take_along_axis(e_logits, g_sel[:, None, None], axis=1)[:, 0]
    top_logit, top_idx = lax.top_k(e_in_group, TOP_K)
    gate = jax.nn.softmax(top_logit, -1) * g_w
    expert_id = (g_sel[:, None] * EXPERTS_PER_GROUP + top_idx).reshape(-1).astype(jnp.int32)

    n_assign = n_tok * TOP_K
    n_slots = n_assign + N_EXPERTS * MOE_BLOCK
    n_chunks = n_slots // MOE_BLOCK
    tok_id = jnp.repeat(jnp.arange(n_tok, dtype=jnp.int32), TOP_K)
    order = jnp.argsort(expert_id)
    e_sorted = expert_id[order]
    counts = jnp.bincount(expert_id, length=N_EXPERTS)
    start = jnp.cumsum(counts) - counts
    padded = (counts + MOE_BLOCK - 1) // MOE_BLOCK * MOE_BLOCK
    pad_end = jnp.cumsum(padded)
    pad_start = pad_end - padded
    dest = pad_start[e_sorted] + jnp.arange(n_assign) - start[e_sorted]
    slot_tok = jnp.full((n_slots,), n_tok, jnp.int32).at[dest].set(tok_id[order])
    slot_gate = jnp.zeros((n_slots,), jnp.float32).at[dest].set(gate.reshape(-1)[order])
    chunk_expert = jnp.minimum(
        jnp.searchsorted(pad_end, jnp.arange(n_chunks) * MOE_BLOCK, side='right'), N_EXPERTS - 1)
    x_pad = jnp.concatenate([x, jnp.zeros((1, d), x.dtype)], axis=0)
    xs = x_pad[slot_tok].reshape(n_chunks, MOE_BLOCK, d)

    def expert_block(args):
        xb, e = args
        h = jax.nn.silu(xb @ w1[e]) * (xb @ w3[e])
        return h @ w2[e]

    ys = lax.map(expert_block, (xs, chunk_expert)).reshape(n_slots, d)
    ys = ys * slot_gate[:, None].astype(ys.dtype)
    return jax.ops.segment_sum(ys, slot_tok, num_segments=n_tok + 1)[:n_tok]

def first_inputs(seed: int = 0) -> dict:
    key = jax.random.key(seed)
    ks = jax.random.split(key, 20)
    L = DEPTH
    beta = (8.0 * DEPTH) ** -0.25
    f32 = jnp.float32

    def normal(k, shape, scale):
        return jax.random.normal(k, shape, f32) * scale

    return {
        'x': normal(ks[0], (BATCH, SEQ, D_MODEL), 1.0),
        'w_in': normal(ks[1], (L, D_MODEL, N_IN), D_MODEL ** -0.5),
        'b_forget': normal(ks[2], (L, H_FOX), 0.1),
        'g_cq': 1.0 + normal(ks[3], (L, MLA_Q_LORA), 0.02),
        'g_ckv': 1.0 + normal(ks[4], (L, MLA_KV_LORA), 0.02),
        'w_uq': normal(ks[5], (L, MLA_Q_LORA, H_MLA * (MLA_NOPE + MLA_ROPE)), MLA_Q_LORA ** -0.5),
        'w_ukv': normal(ks[6], (L, MLA_KV_LORA, H_MLA * (MLA_NOPE + MLA_V)), MLA_KV_LORA ** -0.5),
        'g_head': 1.0 + normal(ks[7], (L, N_HEADS_OUT, HEAD_DIM), 0.02),
        'w_out': normal(ks[8], (L, D_MIX, D_MODEL), beta * D_MIX ** -0.5),
        'ln1_g': 1.0 + normal(ks[9], (L, D_MODEL), 0.02),
        'ln1_b': normal(ks[10], (L, D_MODEL), 0.02),
        'w_group': normal(ks[11], (L, D_MODEL, N_GROUPS), D_MODEL ** -0.5),
        'b_group': normal(ks[12], (L, N_GROUPS), 0.01),
        'w_expert': normal(ks[13], (L, D_MODEL, N_EXPERTS), D_MODEL ** -0.5),
        'b_expert': normal(ks[14], (L, N_EXPERTS), 0.01),
        'w1': normal(ks[15], (L, N_EXPERTS, D_MODEL, D_EXPERT), D_MODEL ** -0.5),
        'w3': normal(ks[16], (L, N_EXPERTS, D_MODEL, D_EXPERT), D_MODEL ** -0.5),
        'w2': normal(ks[17], (L, N_EXPERTS, D_EXPERT, D_MODEL), beta * D_EXPERT ** -0.5),
        'ln2_g': 1.0 + normal(ks[18], (L, D_MODEL), 0.02),
        'ln2_b': normal(ks[19], (L, D_MODEL), 0.02),
    }

def first_block(x, w_in, b_forget, g_cq, g_ckv, w_uq, w_ukv, g_head, w_out, ln1_g, ln1_b,
              w_group, b_group, w_expert, b_expert, w1, w3, w2, ln2_g, ln2_b):
    alpha = (2.0 * DEPTH) ** 0.25
    bsz, seq, d = x.shape
    for l in range(DEPTH):
        h = _mixing(x, w_in[l], b_forget[l], g_cq[l], g_ckv[l], w_uq[l], w_ukv[l], g_head[l], w_out[l])
        x = _layernorm(alpha * x + h, ln1_g[l], ln1_b[l])
        m = _hier_moe(x.reshape(bsz * seq, d), w_group[l], b_group[l], w_expert[l], b_expert[l],
                      w1[l], w3[l], w2[l]).reshape(bsz, seq, d)
        x = _layernorm(alpha * x + m, ln2_g[l], ln2_b[l])
    return x


D_FF = ((8 * D_MODEL // 3 + 127) // 128) * 128
FFN_HALF = 0.5
N_SUB = 3

ML_HEADS = 4
ML_QK = D_MODEL // 2
ML_V = D_MODEL
ML_DK = ML_QK // ML_HEADS
ML_DV = ML_V // ML_HEADS
ML_CHUNK = 64
ML_IN = 2 * ML_QK + 2 * ML_V + 2 * ML_HEADS

MB_EXPAND = 2
MB_DI = MB_EXPAND * D_MODEL
MB_HEADDIM = 64
MB_HEADS = MB_DI // MB_HEADDIM
MB_GROUPS = 4
MB_HPG = MB_HEADS // MB_GROUPS
MB_STATE = 128
MB_CONV = 4
MB_CHUNK = 128
MB_CONV_DIM = MB_DI + 2 * MB_GROUPS * MB_STATE
MB_IN = 2 * MB_DI + 2 * MB_GROUPS * MB_STATE + MB_HEADS

N_MLSTM_LAYERS = (DEPTH + 1) // 2
N_MAMBA_LAYERS = DEPTH // 2
EPS = 1e-6


def rms_norm(x, g):
    xf = x.astype(jnp.float32)
    y = xf * lax.rsqrt(jnp.mean(xf * xf, axis=-1, keepdims=True) + EPS)
    return (y * g.astype(jnp.float32)).astype(x.dtype)

def _to_chunks(t, L):
    B, S = t.shape[:2]
    return jnp.moveaxis(t.reshape(B, S // L, L, *t.shape[2:]), 1, 0)

def _mlstm_chunk(carry, xs):
    C, n, m = carry
    q, k, v, ig, lf = xs
    L = q.shape[2]
    causal = jnp.tril(jnp.ones((L, L), dtype=bool))
    b = jnp.cumsum(lf, axis=-1)
    log_d = jnp.where(causal, b[..., :, None] - b[..., None, :] + ig[..., None, :], -jnp.inf)
    m_inter = b + m[..., None]
    m_t = jnp.maximum(jnp.max(log_d, axis=-1), m_inter)
    s = jnp.einsum('bhtd,bhsd->bhts', q, k) * jnp.exp(log_d - m_t[..., None])
    inter = jnp.exp(m_inter - m_t)
    num = jnp.einsum('bhts,bhsv->bhtv', s, v) + inter[..., None] * jnp.einsum('bhtd,bhdv->bhtv', q, C)
    den = jnp.sum(s, axis=-1) + inter * jnp.einsum('bhtd,bhd->bht', q, n)
    h = num / jnp.maximum(jnp.abs(den), jnp.exp(-m_t))[..., None]
    b_last = b[..., -1]
    log_w = b_last[..., None] - b + ig
    m_new = jnp.maximum(b_last + m, jnp.max(log_w, axis=-1))
    w = jnp.exp(log_w - m_new[..., None])
    decay = jnp.exp(b_last + m - m_new)
    C_new = decay[..., None, None] * C + jnp.einsum('bhs,bhsd,bhsv->bhdv', w, k, v)
    n_new = decay[..., None] * n + jnp.einsum('bhs,bhsd->bhd', w, k)
    return (C_new, n_new, m_new), h

def mlstm_mixer(h, w_in, b_gate, norm_w, w_out):
    B, S, _ = h.shape
    proj = h @ w_in
    q, k, v, o, gates = jnp.split(proj, [ML_QK, 2 * ML_QK, 2 * ML_QK + ML_V, 2 * ML_QK + 2 * ML_V], axis=-1)
    f32 = jnp.float32
    q = q.reshape(B, S, ML_HEADS, ML_DK).astype(f32)
    k = k.reshape(B, S, ML_HEADS, ML_DK).astype(f32) * (ML_DK ** -0.5)
    v = v.reshape(B, S, ML_HEADS, ML_DV).astype(f32)
    gates = gates.astype(f32) + b_gate.astype(f32)
    ig, fg = jnp.split(gates, 2, axis=-1)
    lf = jax.nn.log_sigmoid(fg)
    xs = tuple(jnp.swapaxes(_to_chunks(t, ML_CHUNK), 2, 3) for t in (q, k, v, ig, lf))
    carry0 = (jnp.zeros((B, ML_HEADS, ML_DK, ML_DV), f32),
              jnp.zeros((B, ML_HEADS, ML_DK), f32),
              jnp.zeros((B, ML_HEADS), f32))
    _, hs = lax.scan(_mlstm_chunk, carry0, xs)
    hs = jnp.moveaxis(jnp.swapaxes(hs, 2, 3), 0, 1).reshape(B, S, ML_HEADS, ML_DV)
    hs = hs * lax.rsqrt(jnp.mean(hs * hs, axis=-1, keepdims=True) + EPS)
    hs = hs.reshape(B, S, ML_V) * norm_w.astype(f32) * jax.nn.sigmoid(o.astype(f32))
    return hs.astype(h.dtype) @ w_out

def _ssd_chunk(state, xs, A):
    x, dt, Bc, Cc = xs
    Q = x.shape[1]
    causal = jnp.tril(jnp.ones((Q, Q), dtype=bool))
    a = jnp.cumsum(dt * A, axis=1)
    seg = jnp.where(causal[None, :, :, None, None], a[:, :, None] - a[:, None, :], -jnp.inf)
    w = jnp.einsum('btgn,bsgn->btsg', Cc, Bc)[..., None] * jnp.exp(seg) * dt[:, None]
    y = (jnp.einsum('btsgh,bsghp->btghp', w, x)
         + jnp.exp(a)[..., None] * jnp.einsum('btgn,bghpn->btghp', Cc, state))
    a_last = a[:, -1]
    ws = jnp.exp(a_last[:, None] - a) * dt
    state_new = (jnp.exp(a_last)[..., None, None] * state
                 + jnp.einsum('bsgn,bsgh,bsghp->bghpn', Bc, ws, x))
    return state_new, y

def mamba2_mixer(h, w_in, conv_w, conv_b, dt_bias, A_log, D_skip, norm_w, w_out):
    B, S, _ = h.shape
    f32 = jnp.float32
    proj = h @ w_in
    z, xbc, dt = jnp.split(proj, [MB_DI, MB_DI + MB_CONV_DIM], axis=-1)
    xbc = lax.conv_general_dilated(xbc, conv_w[:, None, :].astype(xbc.dtype), window_strides=(1,),
                                   padding=[(MB_CONV - 1, 0)], dimension_numbers=('NWC', 'WIO', 'NWC'),
                                   feature_group_count=MB_CONV_DIM)
    xbc = jax.nn.silu((xbc + conv_b).astype(f32))
    xs, Bm, Cm = jnp.split(xbc, [MB_DI, MB_DI + MB_GROUPS * MB_STATE], axis=-1)
    xs = xs.reshape(B, S, MB_GROUPS, MB_HPG, MB_HEADDIM)
    Bm = Bm.reshape(B, S, MB_GROUPS, MB_STATE)
    Cm = Cm.reshape(B, S, MB_GROUPS, MB_STATE)
    dt = jax.nn.softplus(dt.astype(f32) + dt_bias.astype(f32)).reshape(B, S, MB_GROUPS, MB_HPG)
    A = -jnp.exp(A_log.astype(f32)).reshape(MB_GROUPS, MB_HPG)
    chunks = tuple(_to_chunks(t, MB_CHUNK) for t in (xs, dt, Bm, Cm))
    state0 = jnp.zeros((B, MB_GROUPS, MB_HPG, MB_HEADDIM, MB_STATE), f32)
    _, ys = lax.scan(functools.partial(_ssd_chunk, A=A), state0, chunks)
    y = jnp.moveaxis(ys, 0, 1).reshape(B, S, MB_GROUPS, MB_HPG, MB_HEADDIM)
    y = y + D_skip.astype(f32).reshape(MB_GROUPS, MB_HPG)[..., None] * xs
    y = y.reshape(B, S, MB_DI) * jax.nn.silu(z.astype(f32))
    y = y.reshape(B, S, MB_GROUPS, MB_DI // MB_GROUPS)
    y = y * lax.rsqrt(jnp.mean(y * y, axis=-1, keepdims=True) + EPS)
    y = y.reshape(B, S, MB_DI) * norm_w.astype(f32)
    return y.astype(h.dtype) @ w_out

def swiglu(h, w1, w3, w2):
    return (jax.nn.silu(h @ w1) * (h @ w3)) @ w2

def sublayer(x, fn, g_pre, g_post, shift, scale, gate, weight):
    hmod = rms_norm(x, g_pre) * (1 + scale[:, None, :]) + shift[:, None, :]
    y = rms_norm(fn(hmod), g_post)
    return x + weight * gate[:, None, :] * y

def second_inputs(seed: int = 0) -> dict:
    key = jax.random.key(seed)
    ks = jax.random.split(key, 24)
    D = D_MODEL
    nrm = lambda k, shape, fan_in: jax.random.normal(k, shape, jnp.float32) * (fan_in ** -0.5)
    u_dt = jax.random.uniform(ks[17], (N_MAMBA_LAYERS, MB_HEADS), jnp.float32)
    dt0 = jnp.exp(u_dt * (math.log(0.1) - math.log(1e-3)) + math.log(1e-3))
    ig_b = 0.5 * jax.random.normal(ks[12], (N_MLSTM_LAYERS, ML_HEADS), jnp.float32)
    fg_b = 3.0 + 3.0 * jax.random.uniform(ks[13], (N_MLSTM_LAYERS, ML_HEADS), jnp.float32)
    return {
        "x": jax.random.normal(ks[0], (BATCH, SEQ, D), jnp.float32),
        "c": jax.random.normal(ks[1], (BATCH, D), jnp.float32),
        "ada_w": 0.5 * nrm(ks[2], (DEPTH, D, 3 * N_SUB * D), D),
        "ada_b": 0.02 * jax.random.normal(ks[3], (DEPTH, 3 * N_SUB * D), jnp.float32),
        "norm_pre": 1.0 + 0.1 * jax.random.normal(ks[4], (DEPTH, N_SUB, D), jnp.float32),
        "norm_post": 1.0 + 0.1 * jax.random.normal(ks[5], (DEPTH, N_SUB, D), jnp.float32),
        "ffn_w1": nrm(ks[6], (DEPTH, 2, D, D_FF), D),
        "ffn_w3": nrm(ks[7], (DEPTH, 2, D, D_FF), D),
        "ffn_w2": nrm(ks[8], (DEPTH, 2, D_FF, D), D_FF),
        "ml_w_in": nrm(ks[9], (N_MLSTM_LAYERS, D, ML_IN), D),
        "ml_b_gate": jnp.concatenate([ig_b, fg_b], axis=-1),
        "ml_norm_w": 1.0 + 0.1 * jax.random.normal(ks[10], (N_MLSTM_LAYERS, ML_V), jnp.float32),
        "ml_w_out": nrm(ks[11], (N_MLSTM_LAYERS, ML_V, D), ML_V),
        "mb_w_in": nrm(ks[14], (N_MAMBA_LAYERS, D, MB_IN), D),
        "mb_conv_w": nrm(ks[15], (N_MAMBA_LAYERS, MB_CONV, MB_CONV_DIM), MB_CONV),
        "mb_conv_b": 0.02 * jax.random.normal(ks[16], (N_MAMBA_LAYERS, MB_CONV_DIM), jnp.float32),
        "mb_dt_bias": dt0 + jnp.log(-jnp.expm1(-dt0)),
        "mb_A_log": jnp.log(jax.random.uniform(ks[18], (N_MAMBA_LAYERS, MB_HEADS), jnp.float32, 1.0, 16.0)),
        "mb_D": 1.0 + 0.1 * jax.random.normal(ks[19], (N_MAMBA_LAYERS, MB_HEADS), jnp.float32),
        "mb_norm_w": 1.0 + 0.1 * jax.random.normal(ks[20], (N_MAMBA_LAYERS, MB_DI), jnp.float32),
        "mb_w_out": nrm(ks[21], (N_MAMBA_LAYERS, MB_DI, D), MB_DI),
    }

def second_block(x, c, ada_w, ada_b, norm_pre, norm_post, ffn_w1, ffn_w3, ffn_w2,
              ml_w_in, ml_b_gate, ml_norm_w, ml_w_out,
              mb_w_in, mb_conv_w, mb_conv_b, mb_dt_bias, mb_A_log, mb_D, mb_norm_w, mb_w_out):
    B = x.shape[0]
    c_act = jax.nn.silu(c)
    for i in range(DEPTH):
        mod = (c_act @ ada_w[i] + ada_b[i]).reshape(B, N_SUB, 3, D_MODEL)
        j = i // 2
        if i % 2 == 0:
            mixer = lambda h, j=j: mlstm_mixer(h, ml_w_in[j], ml_b_gate[j], ml_norm_w[j], ml_w_out[j])
        else:
            mixer = lambda h, j=j: mamba2_mixer(h, mb_w_in[j], mb_conv_w[j], mb_conv_b[j], mb_dt_bias[j],
                                                mb_A_log[j], mb_D[j], mb_norm_w[j], mb_w_out[j])
        fns = (lambda h, i=i: swiglu(h, ffn_w1[i, 0], ffn_w3[i, 0], ffn_w2[i, 0]),
               mixer,
               lambda h, i=i: swiglu(h, ffn_w1[i, 1], ffn_w3[i, 1], ffn_w2[i, 1]))
        weights = (FFN_HALF, 1.0, FFN_HALF)
        for s in range(N_SUB):
            x = sublayer(x, fns[s], norm_pre[i, s], norm_post[i, s],
                         mod[:, s, 0], mod[:, s, 1], mod[:, s, 2], weights[s])
    return x


def setup_inputs(seed=0):
    out = dict(first_inputs(seed))
    for name, value in second_inputs(seed + 1).items():
        if name != "x":
            out[name + "_2"] = value
    return out


def reference(
    x, w_in, b_forget, g_cq, g_ckv, w_uq, w_ukv, g_head, w_out, ln1_g, ln1_b, w_group, b_group,
    w_expert, b_expert, w1, w3, w2, ln2_g, ln2_b, c_2, ada_w_2, ada_b_2, norm_pre_2,
    norm_post_2, ffn_w1_2, ffn_w3_2, ffn_w2_2, ml_w_in_2, ml_b_gate_2, ml_norm_w_2, ml_w_out_2,
    mb_w_in_2, mb_conv_w_2, mb_conv_b_2, mb_dt_bias_2, mb_A_log_2, mb_D_2, mb_norm_w_2,
    mb_w_out_2,
):
    x = first_block(
        x, w_in, b_forget, g_cq, g_ckv, w_uq, w_ukv, g_head, w_out, ln1_g, ln1_b, w_group,
        b_group, w_expert, b_expert, w1, w3, w2, ln2_g, ln2_b,
    )
    return second_block(
        x, c_2, ada_w_2, ada_b_2, norm_pre_2, norm_post_2, ffn_w1_2, ffn_w3_2, ffn_w2_2,
        ml_w_in_2, ml_b_gate_2, ml_norm_w_2, ml_w_out_2, mb_w_in_2, mb_conv_w_2, mb_conv_b_2,
        mb_dt_bias_2, mb_A_log_2, mb_D_2, mb_norm_w_2, mb_w_out_2,
    )


_drawn_inputs = setup_inputs


def setup_inputs(seed=0):
    import zlib

    import numpy as np

    out = dict(_drawn_inputs(seed))
    spreads = {}
    factors = {'b_forget': 3.361,
     'g_cq': 7.152,
     'g_ckv': 5.346,
     'g_head': 4.293,
     'b_group': 8.0,
     'b_expert': 8.0,
     'mb_conv_b_2': 8.0,
     'mb_D_2': 3.714}
    for name, (base, spread) in spreads.items():
        noise = np.random.default_rng([zlib.crc32(name.encode()), seed]).standard_normal(out[name].shape)
        drawn = base * np.exp(spread * noise) if base else spread * noise
        out[name] = __import__('jax').numpy.asarray(drawn.astype(out[name].dtype))
    for name, factor in factors.items():
        out[name] = (out[name] * factor).astype(out[name].dtype)
    return out
```

```python
from contextlib import ExitStack, contextmanager

import numpy as np

import concourse.bass as bass
from concourse import mybir

F32 = mybir.dt.float32
ALU = mybir.AluOpType
ACT = mybir.ActivationFunctionType
AX = mybir.AxisListType.X

P = 128
SLOTS = 3
CHUNK = 4096
NEG = -1e30
LOG1P_SERIES_BELOW = 0.03


class Tally:

    def __init__(self):
        self.count, self.around = 0, []

    def at(self, more=0, times=1, per=1):
        value = times * ((self.count + more) // per)
        for i, n in self.around:
            value = i * (n * times // per) + value
        return value

    def add(self, n=1):
        self.count += n


TALLIES = ("chunk", "proj", "tr_act", "tr_dve", "row", "y", "y_early", "mlp",
           "pe_step", "act_step", "dve_step", "head", "mod_act", "mod_dve")


class Tallies:

    def __init__(self):
        self.chunk, self.proj, self.tr_act, self.tr_dve = Tally(), Tally(), Tally(), Tally()
        self.row, self.y, self.y_early, self.mlp = Tally(), Tally(), Tally(), Tally()
        self.pe_step, self.act_step, self.dve_step = Tally(), Tally(), Tally()
        self.head, self.mod_act, self.mod_dve = Tally(), Tally(), Tally()
        self.all = (self.chunk, self.proj, self.tr_act, self.tr_dve, self.row, self.y, self.y_early,
                    self.mlp, self.pe_step, self.act_step, self.dve_step, self.head, self.mod_act,
                    self.mod_dve)

    def counts(self):
        return tuple(x.count for x in self.all)

    def add(self, **more):
        for name, n in more.items():
            self.all[TALLIES.index(name)].add(n)

    @contextmanager
    def loop(self, engine, n, per):
        before = self.counts()
        with engine.Fori(0, n) as i:
            for tally, k in zip(self.all, per):
                if k:
                    tally.around.append((i, k))
            yield i
            for tally, k in zip(self.all, per):
                if k:
                    tally.around.pop()
        added = tuple(b - a for a, b in zip(before, self.counts()))
        assert added == tuple(per), f"one iteration adds {added}, not {tuple(per)}"
        for tally, k in zip(self.all, per):
            tally.add((n - 1) * k)


def shape_constants(S):
    pos = np.arange(S)
    q, k = pos[:, None], pos[None, :]

    def row_layout(valid):
        bias = np.where(valid, 0.0, NEG).astype(np.float32)
        return np.concatenate([bias[:P, :P], bias[P:, :]], axis=1)

    def column_layout(valid):
        bias = np.where(valid, 0.0, NEG).astype(np.float32).T
        return np.concatenate([bias[:P, :], bias[P:, P:]], axis=1)

    dist = q - k
    masks = [row_layout(dist >= 0)]
    for window, dil in ((128, 1), (512, 4), (2048, 16)):
        masks.append(row_layout((dist >= 0) & (dist <= window) & (dist % dil == 0)))
    masks.append(column_layout(dist > 0))
    masks.append(column_layout(dist >= 0))

    def rope(half):
        freq = np.float32(10000.0) ** (-np.arange(half, dtype=np.float32) / np.float32(half))
        ang = pos.astype(np.float32)[:, None] * freq.astype(np.float32)[None, :]
        return np.concatenate([np.cos(ang), np.sin(ang)], axis=1).astype(np.float32)

    cum = (q <= k).astype(np.float32)
    mid = np.where(k >= P, (q >= P) & (q <= k), 0) - np.where(k < P, (q > k) & (q < P), 0)
    tok = lambda a: np.ascontiguousarray(a.reshape(S // P, P, -1).transpose(1, 0, 2))
    return {
        "c_masks": np.stack(masks, axis=1).astype(np.float32),
        "c_rope64": tok(rope(32)),
        "c_rope32": tok(rope(16)),
        "c_cum": tok(cum),
        "c_mid": tok(mid.astype(np.float32)),
        "c_ident": np.eye(P, dtype=np.float32),
        "c_later": (q[:P] >= k[:, :P]).astype(np.float32),
        "c_rank": np.broadcast_to(16.0 - np.arange(16, dtype=np.float32), (P, 16)).copy(),
    }


def build(nc, A, out):
    S, D = A["x"].shape[1:]
    L = A["w_in"].shape[0]
    NT = S // P
    KD = D // P
    E, FE = A["w1"].shape[1], A["w1"].shape[3]
    DFF = A["ffn_w1_2"].shape[3]
    HD = 64
    ALPHA = (2.0 * L) ** 0.25
    N_IN = A["w_in"].shape[2]
    FOX, MLA, DIL = 768, 1540, 1956
    DQ, DKV, DR = 256, 128, 32
    ML_HEADS, ML_DK, ML_DV = 4, 128, 256
    MB_DI, MB_G, MB_H = 2048, 4, 32
    ROWS = 19
    LN1G, LN1B, LN2G, LN2B, PRE, POST, ADAB = 0, 1, 2, 3, 4, 7, 10
    assert (S, D, L, NT, CHUNK) == (256, 1024, 2, 2, KD * 512)

    ctx = ExitStack()
    with ctx:
        def sb(name, shape):
            return ctx.enter_context(nc.sbuf_tensor(name, shape, F32))

        def sem(name):
            return ctx.enter_context(nc.semaphore(name))

        ring = sb("ring", [P, SLOTS, CHUNK])
        X = sb("X", [P, NT, D])
        Y = sb("Y", [P, NT, D])
        XT = sb("XT", [P, KD, S])
        proj = sb("proj", [P, NT, N_IN])
        feat = sb("feat", [P, 28, S])
        wide = sb("wide", [P, 4096])
        temp = sb("temp", [P, 3072])
        heads = sb("heads", [P, 6, 384])
        kv = sb("kv", [P, NT, 512])
        masks = sb("masks", [P, 6, 384])
        rope64 = sb("rope64", [P, NT, 64])
        rope32 = sb("rope32", [P, NT, 32])
        cum = sb("cum", [P, NT, S])
        mid = sb("mid", [P, NT, S])
        ident = sb("ident", [P, P])
        later = sb("later", [P, P])
        ones = sb("ones", [P, P])
        rank = sb("rank", [P, 16])
        rows = sb("rows", [P, L, D])
        rowT = sb("rowT", [32, 2, S])
        b_forget = sb("b_forget", [P, L, 4])
        b_router = sb("b_router", [P, L, 20])
        w_router = sb("w_router", [P, L, KD, 20])
        g_cq = sb("g_cq", [P, L, 2])
        g_ckv = sb("g_ckv", [P, L])
        g_head = sb("g_head", [P, L, KD])
        b_gate = sb("b_gate", [P, 8])
        ml_norm = sb("ml_norm", [P, KD])
        mb_norm = sb("mb_norm", [P, 16])
        conv_w = sb("conv_w", [P, 4, 24])
        conv_b = sb("conv_b", [P, 24])
        mb_head = sb("mb_head", [P, 3, 32])
        c_feat = sb("c_feat", [P, KD])
        stats = sb("stats", [P, NT, 2, 6])
        mv = sb("mv", [P, NT, 2])
        rs = sb("rs", [P, 3, 32])
        gate = sb("gate", [P, NT, 16])
        small = sb("small", [P, 12, 64])
        lse = sb("lse", [P, 5, 8])
        nmax = sb("nmax", [P, 24, NT])
        den = sb("den", [P, 24, NT])
        rden = sb("rden", [P, 24, NT])
        ps = ctx.enter_context(nc.psum_tensor("ps", [P, 8, 512], F32))

        mlp_silu = proj[:, :, 0:512]
        mlp_h = proj[:, :, 512:1024]
        mlp_hT = proj[:, :, 1024:1536]
        heads_out = wide[:, 0:2048].rearrange("p (t h d) -> p t h d", t=NT, h=16)
        dil_out = wide[:, 2048:3584].rearrange("p (b t h d) -> p b t h d", b=3, t=NT, h=4)

        loaded = sem("constants_loaded")
        x_loaded = sem("x_loaded")
        chunk_ready = [sem(f"chunk_ready{i}") for i in range(SLOTS)]
        chunk_done = sem("chunk_done")
        proj_act = sem("proj_moved_by_act")
        proj_dve = sem("proj_moved_by_dve")
        tr_to_act = sem("transposed_for_act")
        tr_to_dve = sem("transposed_for_dve")
        tr_act = sem("transposed_moved_by_act")
        tr_dve = sem("transposed_moved_by_dve")
        row_ready = sem("row_ready")
        row_used = sem("row_used")
        silu_done = sem("silu_done")
        h_ready = sem("h_ready")
        hT_psum = sem("hT_in_psum")
        hT_ready = sem("hT_ready")
        y_ready = sem("y_ready")
        y_used = sem("y_used")
        pe_did = sem("pe_did")
        act_did = sem("act_did")
        dve_did = sem("dve_did")
        stored = sem("stored")
        scores_ready = sem("scores_ready")
        logits_ready = sem("logits_ready")
        probs_ready = sem("probs_ready")
        probs_turned = sem("probs_turned")
        probsT_ready = sem("probsT_ready")
        output_ready = sem("output_ready")
        output_used = sem("output_used")
        mod_act = sem("mod_moved_by_act")
        mod_dve = sem("mod_moved_by_dve")
        conv_read = sem("conv_read")
        conv_done = sem("conv_done")
        decay_row = sem("decay_row")
        decay_ready = sem("decay_ready")
        decays = sem("decays")
        weights_ready = sem("weights_ready")
        state_out = sem("state_out")
        state_used = sem("state_used")
        ones_set = sem("ones_set")
        done = {}

        N_LOADS = 37
        LAYER = (63, 15, 14, 14, 4, 64, 48, 16, 5, 13, 20, 20, 0, 0)
        SYNC_LAYER = (63, 15, 0, 0, 0, 64, 48, 16, 0, 0, 0, 0, 0, 0)
        END_STEPS = 98
        CREDIT = SLOTS

        def load_chunk(sp, t, part):
            slot = t.chunk.count % SLOTS
            sp.wait_ge(chunk_done, t.chunk.at(1))
            dst, src = part
            sp.dma_start(dst(slot), src).then_inc(chunk_ready[slot], 16)
            t.add(chunk=1)

        def columns(w, c0, n):
            blocks = w.shape[0] // P

            def dst(slot):
                return ring[:, slot, 0:blocks * n].rearrange("p (k n) -> p k n", n=n)

            return dst, w[:, c0:c0 + n].rearrange("(k p) n -> p k n", p=P)

        def slot_view(t, n):
            slot = t.chunk.count % SLOTS
            blocks = min(KD, CHUNK // n)
            return ring[:, slot, 0:blocks * n].rearrange("p (k n) -> p k n", n=n)

        def chunk_arrived(pe, t):
            pe.wait_ge(chunk_ready[t.chunk.count % SLOTS], t.chunk.at(SLOTS, 16, SLOTS))

        def products_ready(eng, t, more=1):
            eng.wait_ge(chunk_done, t.chunk.at(more + CREDIT))

        def project_sync(sp, t, w, c0, widths):
            for n in widths:
                for k0 in range(0, w.shape[0], D):
                    load_chunk(sp, t, columns(w[k0:k0 + D, :], c0, n))
                c0 += n
                t.add(proj=1)

        def project_tensor(pe, t, lhs, widths, depth=1):
            for j, n in enumerate(widths):
                pe.wait_ge(proj_act, t.proj.at(1 if j == 0 else 0))
                pe.wait_ge(proj_dve, t.proj.at(1 if j == 0 else 0))
                for k in range(depth):
                    chunk_arrived(pe, t)
                    w = slot_view(t, n)
                    for tt in range(NT):
                        for b in range(KD):
                            last = nc.tensor.matmul(
                                ps[:, 2 * (j % 2) + tt, 0:n], lhs(k * KD + b, tt), w[:, b, :],
                                start=(k == 0 and b == 0), stop=(k == depth - 1 and b == KD - 1))
                    last.then_inc(chunk_done, 1)
                    t.add(chunk=1)
                t.add(proj=1)

        def project_move(eng, t, tt, widths, take, depth=1):
            for j, n in enumerate(widths):
                products_ready(eng, t, depth)
                take(j, ps[:, 2 * (j % 2) + tt, 0:n]).then_inc(proj_act if tt == 0 else proj_dve, 1)
                t.add(chunk=depth, proj=1)

        def projected(eng, t):
            eng.wait_ge(proj_act, t.proj.at(1))
            eng.wait_ge(proj_dve, t.proj.at(1))

        def to_proj(eng, tt, c0, widths):
            starts = [c0 + sum(widths[:j]) for j in range(len(widths))]

            def take(j, src):
                dst = proj[:, tt, starts[j]:starts[j] + widths[j]]
                if tt == 0:
                    return nc.scalar.copy(dst, src)
                return nc.vector.tensor_copy(dst, src)

            return take

        def transpose_tensor(pe, t, groups):
            for g, blocks in enumerate(groups):
                bank = 4 + g % 2
                if g % 2 == 0:
                    pe.wait_ge(tr_act, t.tr_act.at(1))
                else:
                    pe.wait_ge(tr_dve, t.tr_dve.at(1))
                for n, c, src in blocks:
                    last = nc.tensor.transpose(ps[0:n, bank, c:c + src.shape[0]], src, ident[:, :])
                if g % 2 == 0:
                    last.then_inc(tr_to_act, 1)
                    t.add(tr_act=1)
                else:
                    last.then_inc(tr_to_dve, 1)
                    t.add(tr_dve=1)

        def transposed_move_scalar(act, t, groups):
            for g, moves in enumerate(groups):
                if g % 2 == 0:
                    act.wait_ge(tr_to_act, t.tr_act.at(1))
                    for dst, n, c0, c1, scale in moves:
                        if scale is None:
                            last = nc.scalar.copy(dst, ps[0:n, 4, c0:c1])
                        else:
                            last = nc.scalar.activation(dst, ps[0:n, 4, c0:c1], ACT.Copy, scale=scale)
                    last.then_inc(tr_act, 1)
                    t.add(tr_act=1)
                else:
                    t.add(tr_dve=1)

        def transposed_move_vector(dve, t, groups):
            for g, moves in enumerate(groups):
                if g % 2 == 1:
                    dve.wait_ge(tr_to_dve, t.tr_dve.at(1))
                    for dst, n, c0, c1, scale in moves:
                        if scale is None:
                            last = nc.vector.tensor_copy(dst, ps[0:n, 5, c0:c1])
                        else:
                            last = nc.vector.tensor_scalar(dst, ps[0:n, 5, c0:c1], scale, None, ALU.mult)
                    last.then_inc(tr_dve, 1)
                    t.add(tr_dve=1)
                else:
                    t.add(tr_act=1)

        def transposed(eng, t):
            eng.wait_ge(tr_act, t.tr_act.at(1))
            eng.wait_ge(tr_dve, t.tr_dve.at(1))

        def pairs(src, dst, blocks, scale=None):
            reads, moves = [], []
            for b in range(0, blocks, 2):
                got = [x for x in (b, b + 1) if x < blocks]
                reads.append([(src(x, tt).shape[1], (x - b) * S + tt * P, src(x, tt))
                              for x in got for tt in range(NT)])
                moves.append([(dst(x), src(x, 0).shape[1], (x - b) * S, (x - b + 1) * S,
                               scale(x) if scale else None) for x in got])
            return reads, moves

        def x_groups(buf):
            reads, _ = pairs(lambda b, tt: buf[:, tt, b * P:(b + 1) * P], lambda b: XT[:, b, :], KD)
            moves = [[(XT[:, 2 * g:2 * g + 2, :], P, 0, 2 * S, None)] for g in range(KD // 2)]
            return reads, moves

        def row_tensor(pe, t, layer, r):
            pe.wait_ge(row_used, t.row.at(1))
            pe.wait_ge(y_used, t.y.at(2))
            for h in range(2):
                last = nc.tensor.matmul(ps[:, 6 + h, :],
                                        ident[:, r:r + 1].to_broadcast([P, P]),
                                        rows[:, layer, h * 512:(h + 1) * 512], start=True, stop=True)
            last.then_inc(row_ready, 1)
            t.add(row=1)

        ROW = ps[:, 6:8, :].rearrange("p b n -> p (b n)")

        def rsqrt_scalar(act, t, n):
            act.wait_ge(dve_did, t.dve_step.at())
            nc.scalar.activation(rs[:, 1, 0:n], rs[:, 0, 0:n], ACT.Ln)
            act.drain()
            nc.scalar.activation(rs[:, 2, 0:n], rs[:, 1, 0:n], ACT.Exp, scale=-0.5).then_inc(act_did, 1)
            t.add(act_step=1)

        def softplus_vector(dve, t, n):
            u, e, l, s, m, o = (small[:, i, 0:n] for i in (0, 1, 2, 3, 4, 5))
            nc.vector.scalar_tensor_tensor(s, u, -1.0, u, ALU.mult, ALU.max).then_inc(dve_did, 1)
            t.add(dve_step=1, act_step=1)
            dve.wait_ge(act_did, t.act_step.at())
            nc.vector.tensor_scalar(m, e, LOG1P_SERIES_BELOW, None, ALU.is_lt)
            nc.vector.tensor_scalar(s, e, 0.2, None, ALU.mult)
            for c in (-0.25, 1.0 / 3.0, -0.5, 1.0):
                dve.drain()
                nc.vector.scalar_tensor_tensor(s, s, c, e, ALU.add, ALU.mult)
            dve.drain()
            nc.vector.tensor_tensor(s, s, l, ALU.subtract)
            dve.drain()
            nc.vector.tensor_tensor(s, s, m, ALU.mult)
            dve.drain()
            nc.vector.tensor_tensor(s, s, l, ALU.add)
            dve.drain()
            nc.vector.scalar_tensor_tensor(o, u, 0.0, s, ALU.max, ALU.add)
            dve.drain()

        def softplus_scalar(act, t, n):
            act.wait_ge(dve_did, t.dve_step.at(1))
            nc.scalar.activation(small[:, 1, 0:n], small[:, 3, 0:n], ACT.Exp, scale=-1.0)
            act.drain()
            nc.scalar.activation(small[:, 2, 0:n], small[:, 1, 0:n], ACT.Ln, bias=1.0).then_inc(act_did, 1)
            t.add(dve_step=1, act_step=1)

        def layer_norm_vector(dve, t):
            dve.drain()
            for tt in range(NT):
                for h in range(2):
                    nc.vector.bn_stats(stats[:, tt, h, :], Y[:, tt, h * 512:(h + 1) * 512])
            dve.drain()
            for tt in range(NT):
                nc.vector.bn_aggr(mv[:, tt, :], stats[:, tt, :, :].rearrange("p a b -> p (a b)"))
            dve.drain()
            nc.vector.tensor_scalar(rs[:, 0, 0:NT], mv[:, :, 1], 1e-5, None, ALU.add).then_inc(dve_did, 1)
            t.add(dve_step=1, act_step=1)
            dve.wait_ge(act_did, t.act_step.at())
            for tt in range(NT):
                nc.vector.tensor_scalar(Y[:, tt, :], Y[:, tt, :], mv[:, tt, 0:1], rs[:, 2, tt:tt + 1],
                                        ALU.subtract, ALU.mult)
            dve.drain()
            dve.wait_ge(row_ready, t.row.at(1))
            for tt in range(NT):
                last = nc.vector.tensor_tensor(Y[:, tt, :], Y[:, tt, :], ROW, ALU.mult)
            last.then_inc(row_used, 1)
            dve.drain()
            dve.wait_ge(row_ready, t.row.at(2))
            for tt in range(NT):
                last = nc.vector.tensor_tensor(X[:, tt, :], Y[:, tt, :], ROW, ALU.add)
            last.then_inc(row_used, 1)
            t.add(row=2, dve_step=1)
            dve.drain().then_inc(dve_did, 1)

        def layer_norm_scalar(act, t):
            t.add(dve_step=1)
            rsqrt_scalar(act, t, NT)
            t.add(row=2, dve_step=1)

        def layer_norm_tensor(pe, t, layer, g):
            row_tensor(pe, t, layer, g)
            row_tensor(pe, t, layer, g + 1)
            t.add(dve_step=2, act_step=1)

        def x_transpose_tensor(pe, t, buf):
            pe.wait_ge(dve_did, t.dve_step.at())
            transpose_tensor(pe, t, x_groups(buf)[0])
            transposed(pe, t)

        def up_chunks(w1, w3, n):
            return columns(w1, 0, n), columns(w3, 0, n)

        def down_chunk(w2, n):
            def dst(slot):
                return ring[:, slot, 0:n // P * D].rearrange("p (k d) -> p k d", d=D)

            return dst, w2.rearrange("(k p) d -> p k d", p=P)

        def mlp_up_tensor(pe, t, n):
            for m in range(2):
                chunk_arrived(pe, t)
                w = slot_view(t, n)
                if m == 0:
                    pe.wait_ge(h_ready, t.mlp.at(1))
                for tt in range(NT):
                    for b in range(KD):
                        last = nc.tensor.matmul(ps[:, 2 * m + tt, 0:n], XT[:, b, tt * P:(tt + 1) * P],
                                                w[:, b, :], start=(b == 0), stop=(b == KD - 1))
                last.then_inc(chunk_done, 1)
                t.add(chunk=1)

        def mlp_turn_tensor(pe, t, n):
            pe.wait_ge(h_ready, t.mlp.at(2))
            pe.wait_ge(hT_ready, t.mlp.at(1))
            for b in range(n // P):
                for tt in range(NT):
                    last = nc.tensor.transpose(ps[:, 4 + b // 2, (b % 2) * S + tt * P:(b % 2) * S + (tt + 1) * P],
                                               mlp_h[:, tt, b * P:(b + 1) * P], ident[:, :])
            last.then_inc(hT_psum, 1)
            t.add(mlp=1)

        def mlp_down_tensor(pe, t, n):
            chunk_arrived(pe, t)
            w = slot_view(t, D)
            pe.wait_ge(hT_ready, t.mlp.at(1))
            for q in range(4):
                tt, h = q // 2, q % 2
                pe.wait_ge(y_used, t.y.at(1))
                for b in range(n // P):
                    last = nc.tensor.matmul(ps[:, 6 + q % 2, :], mlp_hT[:, b // 2, (b % 2) * S + tt * P:
                                                                        (b % 2) * S + (tt + 1) * P],
                                            w[:, b, h * 512:(h + 1) * 512], start=(b == 0), stop=(b == n // P - 1))
                t.add(y=1)
                if q < 3:
                    last.then_inc(y_ready, 1)
                    t.add(y_early=1)
            last.then_inc(chunk_done, 1)
            t.add(chunk=1)

        def mlp_up_scalar(act, t, n):
            products_ready(act, t)
            act.wait_ge(h_ready, t.mlp.at(1))
            nc.scalar.activation(mlp_silu[:, :, 0:n], ps[:, 0:2, 0:n], ACT.Silu).then_inc(silu_done, 1)
            t.add(chunk=2)

        def mlp_turn_scalar(act, t, n):
            act.wait_ge(hT_psum, t.mlp.at(1))
            w = n // P // 2
            nc.scalar.copy(mlp_hT[:, 0:w, :], ps[:, 4:4 + w, :]).then_inc(hT_ready, 1)
            t.add(mlp=1)

        def mlp_down_skip(t):
            t.add(y=4, y_early=3, chunk=1)

        def mlp_up_vector(dve, t, n):
            products_ready(dve, t, 2)
            dve.wait_ge(silu_done, t.mlp.at(1))
            nc.vector.tensor_tensor(mlp_h[:, :, 0:n], mlp_silu[:, :, 0:n], ps[:, 2:4, 0:n],
                                    ALU.mult).then_inc(h_ready, 1)
            t.add(chunk=2)

        def mlp_down_vector(dve, t, weight):
            dve.drain()
            for q in range(4):
                tt, h = q // 2, q % 2
                if q < 3:
                    dve.wait_ge(y_ready, t.y_early.at(1))
                    t.add(y_early=1)
                else:
                    products_ready(dve, t)
                yy = Y[:, tt, h * 512:(h + 1) * 512]
                nc.vector.scalar_tensor_tensor(yy, ps[:, 6 + q % 2, :], weight(tt), yy,
                                               ALU.mult, ALU.add).then_inc(y_used, 1)
                t.add(y=1)
            t.add(chunk=1)

        STAGE = dict(chunk=3, mlp=1, y=4, y_early=3)
        STAGE = tuple(STAGE.get(n, 0) for n in TALLIES)

        def mlp_sync(sp, t, n, rest, w1, w3, w2, w1r=None, w3r=None, w2r=None):
            for part in up_chunks(w1(0), w3(0), 512):
                load_chunk(sp, t, part)
            t.add(mlp=1)
            with t.loop(sp, n - 1, STAGE) as i:
                for part in up_chunks(w1(i + 1), w3(i + 1), 512):
                    load_chunk(sp, t, part)
                load_chunk(sp, t, down_chunk(w2(i), 512))
                t.add(mlp=1, y=4, y_early=3)
            if rest:
                for part in up_chunks(w1r, w3r, rest):
                    load_chunk(sp, t, part)
                load_chunk(sp, t, down_chunk(w2(n - 1), 512))
                load_chunk(sp, t, down_chunk(w2r, rest))
                t.add(mlp=1, y=8, y_early=6)
            else:
                load_chunk(sp, t, down_chunk(w2(n - 1), 512))
                t.add(y=4, y_early=3)

        def mlp_tensor(pe, t, n, rest):
            pe.wait_ge(row_used, t.row.at(1))
            mlp_up_tensor(pe, t, 512)
            mlp_turn_tensor(pe, t, 512)
            with t.loop(pe, n - 1, STAGE):
                mlp_up_tensor(pe, t, 512)
                mlp_down_tensor(pe, t, 512)
                mlp_turn_tensor(pe, t, 512)
            if rest:
                mlp_up_tensor(pe, t, rest)
                mlp_down_tensor(pe, t, 512)
                mlp_turn_tensor(pe, t, rest)
                mlp_down_tensor(pe, t, rest)
            else:
                mlp_down_tensor(pe, t, 512)

        def mlp_scalar(act, t, n, rest):
            mlp_up_scalar(act, t, 512)
            mlp_turn_scalar(act, t, 512)
            with t.loop(act, n - 1, STAGE):
                mlp_up_scalar(act, t, 512)
                mlp_down_skip(t)
                mlp_turn_scalar(act, t, 512)
            if rest:
                mlp_up_scalar(act, t, rest)
                mlp_down_skip(t)
                mlp_turn_scalar(act, t, rest)
            mlp_down_skip(t)

        def mlp_vector(dve, t, n, rest, weight):
            mlp_up_vector(dve, t, 512)
            t.add(mlp=1)
            with t.loop(dve, n - 1, STAGE) as i:
                mlp_up_vector(dve, t, 512)
                mlp_down_vector(dve, t, weight(i))
                t.add(mlp=1)
            if rest:
                mlp_up_vector(dve, t, rest)
                mlp_down_vector(dve, t, weight(n - 1))
                t.add(mlp=1)
                mlp_down_vector(dve, t, weight(n))
            else:
                mlp_down_vector(dve, t, weight(n - 1))
            dve.drain()

        W_IN = [388] * 10 + [380]
        q_mla = heads[:, 0:2, :]
        k_mla = heads[:, 2:4, :]
        latent = heads[:, 4:6, :].rearrange("p a b -> p (a b)").rearrange("p (k s) -> p k s", s=S)
        CQ, CKV, KR = MLA, MLA + DQ, MLA + DQ + DKV

        def attention_sync(sp, t, l):
            project_sync(sp, t, A["w_in"][l], 0, W_IN)
            load_chunk(sp, t, columns(A["w_uq"][l], 0, 384))
            load_chunk(sp, t, columns(A["w_ukv"][l], 0, 512))
            t.add(proj=2)
            project_sync(sp, t, A["w_out"][l], 0, [512, 512])

        def input_blocks():
            def src(b, tt):
                c = b * P if b < 4 else FOX + (b - 4) * P if b < 8 else DIL + (b - 8) * P
                return proj[:, tt, c:c + P]

            reads, _ = pairs(src, lambda b: feat[:, b, :], 20)
            moves = [[(feat[:, b:b + 2, :].rearrange("p b s -> p (b s)"), P, 0, 2 * S, None)]
                     for b in range(0, 20, 2)]
            return reads, moves

        def mla_blocks():
            def src(b, tt):
                buf = q_mla if b < 4 else k_mla
                return buf[:, tt, (b % 4) * 96:(b % 4 + 1) * 96]

            reads, _ = pairs(src, lambda b: feat[0:96, 20 + b, :], 8)
            moves = [[(feat[0:96, 20 + b:22 + b, :].rearrange("p b s -> p (b s)"), 96, 0, 2 * S, None)]
                     for b in range(0, 8, 2)]
            return reads, moves

        def latent_blocks(l):
            src = lambda b, tt: proj[:, tt, CQ + b * P:CQ + (b + 1) * P]
            gain = lambda b: g_cq[:, l, b:b + 1] if b < 2 else g_ckv[:, bass.ds(l, 1)]
            return pairs(src, lambda b: latent[:, b, :], 3, gain)

        def attention_prepare_tensor(pe, t):
            x_transpose_tensor(pe, t, X)
            project_tensor(pe, t, lambda b, tt: XT[:, b, tt * P:(tt + 1) * P], W_IN)
            projected(pe, t)
            pe.wait_ge(dve_did, t.dve_step.at(2))
            for tt in range(NT):
                last = nc.tensor.matmul(ps[0:4, 0, 0:S], small[:, 6, 4 * tt:4 * tt + 4], cum[:, tt, :],
                                        start=(tt == 0), stop=(tt == NT - 1))
            last.then_inc(pe_did, 1)
            pe.wait_ge(dve_did, t.dve_step.at(4))
            transpose_tensor(pe, t, latent_blocks(0)[0])
            transposed(pe, t)
            t.add(pe_step=1, act_step=3, dve_step=4)
            pe.wait_ge(dve_did, t.dve_step.at(1))
            for j, (b0, nb, n) in enumerate(((0, 2, 384), (2, 1, 512))):
                chunk_arrived(pe, t)
                w = slot_view(t, n)
                for tt in range(NT):
                    for b in range(nb):
                        last = nc.tensor.matmul(ps[:, 2 * j + tt, 0:n], latent[:, b0 + b, tt * P:(tt + 1) * P],
                                                w[:, b, :], start=(b == 0), stop=(b == nb - 1))
                last.then_inc(chunk_done, 1)
                t.add(chunk=1, proj=1)
            transpose_tensor(pe, t, input_blocks()[0])
            pe.wait_ge(dve_did, t.dve_step.at(2))
            transpose_tensor(pe, t, mla_blocks()[0])
            transposed(pe, t)
            t.add(dve_step=2)

        def attention_prepare_scalar(act, t, l):
            transposed_move_scalar(act, t, x_groups(X)[1])
            project_move(act, t, 0, W_IN, to_proj(act, 0, 0, W_IN))
            projected(act, t)
            for i, (c, n) in enumerate(((CQ, DQ), (CKV, DKV))):
                for tt in range(NT):
                    last = nc.scalar.activation(temp[:, 0:n], proj[:, tt, c:c + n], ACT.Square,
                                                accum_out=small[:, 7, 2 * i + tt:2 * i + tt + 1])
                    act.drain()
            act.drain().then_inc(act_did, 1)
            t.add(act_step=1)
            softplus_scalar(act, t, 8)
            t.add(dve_step=2)
            rsqrt_scalar(act, t, 4)
            t.add(dve_step=1)
            transposed_move_scalar(act, t, latent_blocks(l)[1])
            t.add(pe_step=1)
            for dst, n in ((q_mla[:, 0, :], 384), (kv[:, 0, :], 512)):
                products_ready(act, t)
                nc.scalar.copy(dst, ps[:, 0 if n == 384 else 2, 0:n]).then_inc(proj_act, 1)
                t.add(chunk=1, proj=1)
            act.wait_ge(dve_did, t.dve_step.at(1))
            transposed_move_scalar(act, t, input_blocks()[1])
            transposed_move_scalar(act, t, mla_blocks()[1])
            t.add(dve_step=2)

        def rotate(dve, x1, x2, cos, sin, shape):
            n = int(np.prod(shape[1:]))
            names = "abc"[:len(shape) - 1]
            sizes = dict(zip(names, shape[1:]))
            pattern = f"p ({' '.join(names)}) -> p {' '.join(names)}"
            t1 = temp[:, 0:n].rearrange(pattern, **sizes)
            t2 = temp[:, 1536:1536 + n].rearrange(pattern, **sizes)
            nc.vector.tensor_tensor(t1, x1, sin, ALU.mult)
            nc.vector.tensor_tensor(t2, x2, sin, ALU.mult)
            dve.drain()
            nc.vector.tensor_tensor(x1, x1, cos, ALU.mult)
            nc.vector.tensor_tensor(x2, x2, cos, ALU.mult)
            dve.drain()
            nc.vector.tensor_tensor(x1, x1, t2, ALU.subtract)
            nc.vector.tensor_tensor(x2, x2, t1, ALU.add)
            dve.drain()

        def attention_prepare_vector(dve, t, l):
            transposed_move_vector(dve, t, x_groups(X)[1])
            project_move(dve, t, 1, W_IN, to_proj(dve, 1, 0, W_IN))
            projected(dve, t)
            t.add(act_step=1)
            u = small[:, 0, 0:8].rearrange("p (t h) -> p t h", t=NT)
            nc.vector.tensor_tensor(u, proj[:, :, FOX + 768:FOX + 772],
                                    b_forget[:, l, :].unsqueeze(1).to_broadcast([P, NT, 4]), ALU.add)
            dve.drain()
            nc.vector.tensor_scalar(small[:, 0, 0:8], small[:, 0, 0:8], -1.0, None, ALU.mult)
            dve.drain()
            softplus_vector(dve, t, 8)
            nc.vector.tensor_scalar(small[:, 6, 0:8], small[:, 5, 0:8], -1.0, None,
                                    ALU.mult).then_inc(dve_did, 1)
            nc.vector.tensor_scalar(rs[:, 0, 0:2], small[:, 7, 0:2], 1.0 / DQ, 1e-6, ALU.mult, ALU.add)
            nc.vector.tensor_scalar(rs[:, 0, 2:4], small[:, 7, 2:4], 1.0 / DKV, 1e-6, ALU.mult, ALU.add)
            dve.drain().then_inc(dve_did, 1)
            t.add(dve_step=2, act_step=1)
            dve.wait_ge(act_did, t.act_step.at())
            for i, (c, n) in enumerate(((CQ, DQ), (CKV, DKV))):
                for tt in range(NT):
                    nc.vector.tensor_scalar(proj[:, tt, c:c + n], proj[:, tt, c:c + n],
                                            rs[:, 2, 2 * i + tt:2 * i + tt + 1], None, ALU.mult)
            dve.drain().then_inc(dve_did, 1)
            t.add(dve_step=1)
            transposed_move_vector(dve, t, latent_blocks(l)[1])
            dve.wait_ge(pe_did, t.pe_step.at(1))
            t.add(pe_step=1)
            nc.vector.tensor_scalar(rowT[0:4, 0, :], ps[0:4, 0, 0:S], 8.0, None, ALU.mult)
            nc.vector.tensor_scalar(rowT[0:4, 1, :], ps[0:4, 0, 0:S], -8.0, None, ALU.mult)
            v = proj[:, :, DIL:DIL + 1536].rearrange("p t (h d) -> p t h d", d=HD)
            for tt in range(NT):
                rotate(dve, v[:, tt, :, 0:32], v[:, tt, :, 32:64],
                       rope64[:, tt, 0:32].unsqueeze(1).to_broadcast([P, 24, 32]),
                       rope64[:, tt, 32:64].unsqueeze(1).to_broadcast([P, 24, 32]), [P, 24, 32])
            dve.drain().then_inc(dve_did, 1)
            t.add(dve_step=1)
            for dst, n in ((q_mla[:, 1, :], 384), (kv[:, 1, :], 512)):
                products_ready(dve, t)
                nc.vector.tensor_copy(dst, ps[:, 1 if n == 384 else 3, 0:n]).then_inc(proj_dve, 1)
                t.add(chunk=1, proj=1)
            projected(dve, t)
            transposed_move_vector(dve, t, input_blocks()[1])
            kr = proj[:, :, KR:KR + DR]
            rotate(dve, kr[:, :, 0:16], kr[:, :, 16:32], rope32[:, :, 0:16], rope32[:, :, 16:32], [P, NT, 16])
            for tt in range(NT):
                qr = q_mla[:, tt, :].rearrange("p (h d) -> p h d", d=96)
                rotate(dve, qr[:, :, 64:80], qr[:, :, 80:96],
                       rope32[:, tt, 0:16].unsqueeze(1).to_broadcast([P, 4, 16]),
                       rope32[:, tt, 16:32].unsqueeze(1).to_broadcast([P, 4, 16]), [P, 4, 16])
                kc = k_mla[:, tt, :].rearrange("p (h d) -> p h d", d=96)
                nc.vector.tensor_copy(kc[:, :, 0:64], kv[:, tt, :].rearrange("p (h d) -> p h d", d=P)[:, :, 0:64])
                nc.vector.tensor_copy(kc[:, :, 64:96], kr[:, tt, :].unsqueeze(1).to_broadcast([P, 4, 32]))
            dve.drain().then_inc(dve_did, 1)
            t.add(dve_step=1)
            transposed_move_vector(dve, t, mla_blocks()[1])

        SBK = 4 * 384
        sb_z = temp[:, 0:SBK].rearrange("p (h n) -> p h n", n=384)
        sb_sp = temp[:, SBK:2 * SBK].rearrange("p (h n) -> p h n", n=384)
        sb_w = heads[:, 0:4, :]

        def pv_tensor(out_ps, pT, v):
            n = v(0).shape[-1]
            nc.tensor.matmul(out_ps[:, 0:n], pT[:, 0:P], v(0), start=True, stop=True)
            nc.tensor.matmul(out_ps[:, n:2 * n], pT[:, P:2 * P], v(0), start=True, stop=False)
            return nc.tensor.matmul(out_ps[:, n:2 * n], pT[:, 2 * P:3 * P], v(1), start=False, stop=True)

        def stick_tensor(pe, t):
            for h in range(4):
                b = (h % 2) * HD
                q, k = feat[b:b + HD, h // 2, :], feat[b:b + HD, 2 + h // 2, :]
                nc.tensor.matmul(ps[:, h, 0:S], k[:, 0:P], q, start=True, stop=True)
                last = nc.tensor.matmul(ps[:, h, S:384], k[:, P:S], q[:, P:S], start=True, stop=True)
            last.then_inc(pe_did, 1)
            pe.wait_ge(dve_did, t.dve_step.at(2))
            for h in range(4):
                nc.tensor.matmul(ps[:, 4 + h, 0:S], later[:, :], sb_sp[:, h, 0:S], start=True, stop=False)
                nc.tensor.matmul(ps[:, 4 + h, P:S], ones[:, :], sb_sp[:, h, S:384], start=False, stop=True)
                last = nc.tensor.matmul(ps[:, 4 + h, S:384], later[:, :], sb_sp[:, h, S:384],
                                        start=True, stop=True)
            last.then_inc(pe_did, 1)
            pe.wait_ge(act_did, t.act_step.at(2))
            for h in range(4):
                last = pv_tensor(ps[:, 7, h * P:(h + 1) * P], sb_w[:, h, :],
                                 lambda tt: proj[:, tt, 512 + h * HD:512 + (h + 1) * HD])
            last.then_inc(pe_did, 1)
            t.add(pe_step=3, act_step=2, dve_step=3)

        def stick_scalar(act, t):
            act.wait_ge(dve_did, t.dve_step.at(1))
            nc.scalar.activation(sb_w, sb_w, ACT.Exp, scale=-1.0)
            act.drain()
            nc.scalar.activation(sb_w, sb_w, ACT.Ln, bias=1.0).then_inc(act_did, 1)
            act.wait_ge(dve_did, t.dve_step.at(3))
            nc.scalar.activation(sb_w, sb_w, ACT.Exp).then_inc(act_did, 1)
            t.add(pe_step=3, act_step=2, dve_step=3)

        def stick_vector(dve, t):
            dve.wait_ge(pe_did, t.pe_step.at(1))
            for h in range(4):
                nc.vector.scalar_tensor_tensor(sb_z[:, h, :], ps[:, h, 0:384], HD ** -0.5, masks[:, 4, :],
                                               ALU.mult, ALU.add)
            dve.drain()
            nc.vector.scalar_tensor_tensor(sb_w, sb_z, -1.0, sb_z, ALU.mult, ALU.max).then_inc(dve_did, 1)
            dve.wait_ge(act_did, t.act_step.at(1))
            nc.vector.scalar_tensor_tensor(sb_sp, sb_z, 0.0, sb_w, ALU.max, ALU.add).then_inc(dve_did, 1)
            dve.wait_ge(pe_did, t.pe_step.at(2))
            for h in range(4):
                last = nc.vector.tensor_tensor(sb_w[:, h, :], sb_z[:, h, :], ps[:, 4 + h, 0:384], ALU.subtract)
            last.then_inc(dve_did, 1)
            dve.wait_ge(pe_did, t.pe_step.at(3))
            nc.vector.tensor_copy(heads_out[:, :, 0:4, :],
                                  ps[:, 7, :].rearrange("p (h t d) -> p t h d", h=4, t=NT))
            t.add(pe_step=3, act_step=2, dve_step=3)

        def head_list():
            out = []
            for h in range(4):
                out.append(dict(q=4 + h // 2, k=6 + h // 2, base=(h % 2) * HD, n=HD, scale=HD ** -0.5, mask=0,
                                forget=h, v=lambda tt, h=h: proj[:, tt, FOX + 512 + h * HD:FOX + 512 + (h + 1) * HD],
                                out=heads_out[:, :, 4 + h, :]))
            for h in range(4):
                out.append(dict(q=20 + h, k=24 + h, base=0, n=96, scale=96 ** -0.5, mask=0, forget=None,
                                v=lambda tt, h=h: kv[:, tt, h * P + 64:(h + 1) * P],
                                out=heads_out[:, :, 8 + h, :]))
            for n in range(12):
                out.append(dict(q=8 + n // 2, k=14 + n // 2, base=(n % 2) * HD, n=HD, scale=HD ** -0.5,
                                mask=1 + n // 4, forget=None,
                                v=lambda tt, n=n: proj[:, tt, DIL + 1536 + n * HD:DIL + 1536 + (n + 1) * HD],
                                out=dil_out[:, n // 4, :, n % 4, :]))
            return out

        HEADS = head_list()
        NH = len(HEADS)
        logits = lambda i: heads[:, i % 2, :]
        probs = lambda i: heads[:, 2 + i % 2, :]
        probsT = lambda i: heads[:, 4 + i % 2, :]

        def softmax_heads_tensor(pe, t):
            def scores(i):
                hd = HEADS[i]
                if i >= 2:
                    pe.wait_ge(logits_ready, t.head.at(i - 1))
                b, n, f = hd["base"], hd["n"], hd["forget"]
                q, k = feat[b:b + n, hd["q"], :], feat[b:b + n, hd["k"], :]
                for tt, (c0, nk) in enumerate(((0, P), (P, S))):
                    out = ps[:, i % 2, c0:c0 + nk]
                    last = nc.tensor.matmul(out, q[:, tt * P:(tt + 1) * P], k[:, 0:nk],
                                            start=True, stop=(f is None))
                    if f is not None:
                        pick = ident[0:4, f:f + 1]
                        nc.tensor.matmul(out, rowT[0:4, 0, tt * P:(tt + 1) * P],
                                         pick.to_broadcast([4, nk]), start=False, stop=False)
                        last = nc.tensor.matmul(out, pick.to_broadcast([4, P]), rowT[0:4, 1, 0:nk],
                                                start=False, stop=True)
                last.then_inc(scores_ready, 1)

            def turn(i):
                pe.wait_ge(probs_ready, t.head.at(i + 1))
                if i >= 2:
                    pe.wait_ge(probsT_ready, t.head.at(i - 1))
                for c in range(3):
                    last = nc.tensor.transpose(ps[:, 2 + i % 2, c * P:(c + 1) * P],
                                               probs(i)[:, c * P:(c + 1) * P], ident[:, :])
                last.then_inc(probs_turned, 1)

            def output(i):
                pe.wait_ge(probsT_ready, t.head.at(i + 1))
                if i >= 2:
                    pe.wait_ge(output_used, t.head.at(i - 1))
                pv_tensor(ps[:, 6 + i % 2, 0:2 * HD], probsT(i), HEADS[i]["v"]).then_inc(output_ready, 1)

            scores(0)
            scores(1)
            turn(0)
            for i in range(NH):
                if i + 2 < NH:
                    scores(i + 2)
                if i + 1 < NH:
                    turn(i + 1)
                output(i)
            t.add(head=NH)

        def softmax_heads_scalar(act, t):
            def exponentials(i):
                act.wait_ge(logits_ready, t.head.at(i + 1))
                if i >= 2:
                    act.wait_ge(probs_turned, t.head.at(i - 1))
                for tt, (c0, c1) in enumerate(((0, P), (P, 384))):
                    last = nc.scalar.activation(probs(i)[:, c0:c1], logits(i)[:, c0:c1], ACT.Exp,
                                                bias=nmax[:, i, tt:tt + 1], accum_out=den[:, i, tt:tt + 1])
                last.then_inc(probs_ready, 1)

            def move(i):
                act.wait_ge(probs_turned, t.head.at(i + 1))
                if i >= 2:
                    act.wait_ge(output_ready, t.head.at(i - 1))
                nc.scalar.copy(probsT(i), ps[:, 2 + i % 2, 0:384]).then_inc(probsT_ready, 1)

            exponentials(0)
            for i in range(NH):
                if i + 1 < NH:
                    exponentials(i + 1)
                move(i)
            t.add(head=NH)

        def softmax_heads_vector(dve, t):
            def mask(i):
                dve.wait_ge(scores_ready, t.head.at(i + 1))
                if i >= 2:
                    dve.wait_ge(probs_ready, t.head.at(i - 1))
                nc.vector.scalar_tensor_tensor(logits(i), ps[:, i % 2, 0:384], HEADS[i]["scale"],
                                               masks[:, HEADS[i]["mask"], :], ALU.mult, ALU.add)
                dve.drain()
                for tt, (c0, c1) in enumerate(((0, P), (P, 384))):
                    last = nc.vector.tensor_reduce(nmax[:, i, tt:tt + 1], logits(i)[:, c0:c1], AX, ALU.max,
                                                   negate=True)
                last.then_inc(logits_ready, 1)

            def use(i):
                dve.wait_ge(output_ready, t.head.at(i + 1))
                nc.vector.reciprocal(rden[:, i, :], den[:, i, :])
                dve.drain()
                nc.vector.tensor_tensor(HEADS[i]["out"], ps[:, 6 + i % 2, 0:2 * HD].rearrange("p (t d) -> p t d", t=NT),
                                        rden[:, i, :].unsqueeze(2).to_broadcast([P, NT, HD]),
                                        ALU.mult).then_inc(output_used, 1)

            mask(0)
            mask(1)
            for i in range(NH):
                if i + 2 < NH:
                    mask(i + 2)
                use(i)
            t.add(head=NH)

        OUT = [512, 512]
        lse3 = lse[:, 0:3, :].rearrange("p b (h t) -> p b h t", t=NT)
        DIL0 = NH - 12

        def head_blocks(l):
            src = lambda b, tt: wide[:, tt * D + b * P:tt * D + (b + 1) * P]
            return pairs(src, lambda b: XT[:, b, :], KD, lambda b: g_head[:, l, b:b + 1])

        def attention_finish_tensor(pe, t, l):
            pe.wait_ge(dve_did, t.dve_step.at(5))
            transpose_tensor(pe, t, head_blocks(0)[0])
            transposed(pe, t)
            project_tensor(pe, t, lambda b, tt: XT[:, b, tt * P:(tt + 1) * P], OUT)
            t.add(act_step=4, dve_step=5)

        def attention_finish_scalar(act, t, l):
            act.drain()
            nc.scalar.activation(lse[:, 0:3, :].rearrange("p b n -> p (b n)"),
                                 den[:, DIL0:NH, :].rearrange("p h t -> p (h t)"), ACT.Ln).then_inc(act_did, 1)
            act.wait_ge(dve_did, t.dve_step.at(1))
            nc.scalar.activation(lse[:, 0:3, :], lse[:, 0:3, :], ACT.Exp).then_inc(act_did, 1)
            act.wait_ge(dve_did, t.dve_step.at(3))
            nc.scalar.activation(temp[:, 0:2048], wide[:, 0:2048], ACT.Square).then_inc(act_did, 1)
            t.add(act_step=3, dve_step=4)
            rsqrt_scalar(act, t, 32)
            t.add(dve_step=1)
            transposed_move_scalar(act, t, head_blocks(l)[1])

            def take(j, src):
                return nc.scalar.copy(Y[:, 0, j * 512:(j + 1) * 512], src)

            project_move(act, t, 0, OUT, take)

        def attention_finish_vector(dve, t, l):
            m, total = lse[:, 3, :], lse[:, 4, :]
            dve.wait_ge(act_did, t.act_step.at(1))
            nm = nmax[:, DIL0:NH, :].rearrange("p (b h) t -> p b (h t)", b=3)
            nc.vector.tensor_tensor(lse[:, 0:3, :], lse[:, 0:3, :], nm, ALU.subtract)
            dve.drain()
            nc.vector.tensor_tensor(m, lse[:, 0, :], lse[:, 1, :], ALU.max)
            dve.drain()
            nc.vector.tensor_tensor(m, m, lse[:, 2, :], ALU.max)
            dve.drain()
            nc.vector.tensor_tensor(lse[:, 0:3, :], lse[:, 0:3, :], m.unsqueeze(1).to_broadcast([P, 3, 8]),
                                    ALU.subtract).then_inc(dve_did, 1)
            dve.wait_ge(act_did, t.act_step.at(2))
            nc.vector.tensor_tensor(total, lse[:, 0, :], lse[:, 1, :], ALU.add)
            dve.drain()
            nc.vector.tensor_tensor(total, total, lse[:, 2, :], ALU.add)
            dve.drain()
            nc.vector.reciprocal(total, total)
            dve.drain()
            nc.vector.tensor_tensor(lse[:, 0:3, :], lse[:, 0:3, :], total.unsqueeze(1).to_broadcast([P, 3, 8]),
                                    ALU.mult)
            dve.drain().then_inc(dve_did, 1)
            for b in range(3):
                w = lse3[:, b, :, :].rearrange("p h t -> p t h").unsqueeze(3).to_broadcast([P, NT, 4, HD])
                nc.vector.tensor_tensor(dil_out[:, b], dil_out[:, b], w, ALU.mult)
            dve.drain()
            nc.vector.tensor_tensor(dil_out[:, 0], dil_out[:, 0], dil_out[:, 1], ALU.add)
            dve.drain()
            nc.vector.tensor_tensor(heads_out[:, :, 12:16, :], dil_out[:, 0], dil_out[:, 2], ALU.add)
            dve.drain().then_inc(dve_did, 1)
            dve.wait_ge(act_did, t.act_step.at(3))
            nc.vector.tensor_reduce(small[:, 7, 0:32], temp[:, 0:2048].rearrange("p (n d) -> p n d", d=HD),
                                    AX, ALU.add)
            dve.drain()
            nc.vector.tensor_scalar(rs[:, 0, 0:32], small[:, 7, 0:32], 1.0 / HD, 1e-6, ALU.mult,
                                    ALU.add).then_inc(dve_did, 1)
            dve.wait_ge(act_did, t.act_step.at(4))
            w3 = wide[:, 0:2048].rearrange("p (n d) -> p n d", d=HD)
            nc.vector.tensor_tensor(w3, w3, rs[:, 2, 0:32].unsqueeze(2).to_broadcast([P, 32, HD]), ALU.mult)
            dve.drain().then_inc(dve_did, 1)
            t.add(act_step=4, dve_step=5)
            transposed_move_vector(dve, t, head_blocks(l)[1])

            def take(j, src):
                s = slice(j * 512, (j + 1) * 512)
                return nc.vector.scalar_tensor_tensor(Y[:, 1, s], X[:, 1, s], ALPHA, src, ALU.mult, ALU.add)

            project_move(dve, t, 1, OUT, take)
            projected(dve, t)
            nc.vector.scalar_tensor_tensor(Y[:, 0, :], X[:, 0, :], ALPHA, Y[:, 0, :], ALU.mult, ALU.add)

        def route_tensor(pe, t, l):
            x_transpose_tensor(pe, t, X)
            for tt in range(NT):
                for b in range(KD):
                    last = nc.tensor.matmul(ps[:, tt, 0:20], XT[:, b, tt * P:(tt + 1) * P],
                                            w_router[:, l, b, :], start=(b == 0), stop=(b == KD - 1))
            last.then_inc(pe_did, 1)
            t.add(pe_step=1, act_step=2, dve_step=2)
            pe.wait_ge(dve_did, t.dve_step.at())

        def route_scalar(act, t):
            transposed_move_scalar(act, t, x_groups(X)[1])
            g = small[:, 1, 0:8]
            act.wait_ge(dve_did, t.dve_step.at(1))
            nc.scalar.activation(g, g, ACT.Exp).then_inc(act_did, 1)
            d = small[:, 2, 0:2]
            act.wait_ge(dve_did, t.dve_step.at(2))
            nc.scalar.activation(d, d, ACT.Exp).then_inc(act_did, 1)
            t.add(pe_step=1, act_step=2, dve_step=2)

        def route_vector(dve, t, l):
            transposed_move_vector(dve, t, x_groups(X)[1])
            view = lambda i, n: small[:, i, 0:NT * n].rearrange("p (t n) -> p t n", t=NT)
            lg = view(0, 20)
            glog, elog = lg[:, :, 0:4], lg[:, :, 4:20]
            gexp, d = view(1, 4), view(2, 1)
            top, first, second = view(3, 1), view(4, 1), view(5, 1)
            group = view(6, 4)
            score, one, other = view(7, 16), view(8, 16), view(9, 16)
            gsum = view(10, 1)
            wide_ = lambda a, n: a.to_broadcast([P, NT, n])
            ranks = lambda n: rank[:, 0:n].unsqueeze(1).to_broadcast([P, NT, n])
            TT, TS = nc.vector.tensor_tensor, nc.vector.tensor_scalar

            def choose(dst, values, best, n):
                TT(dst, values, wide_(best, n), ALU.is_ge)
                dve.drain()
                TT(dst, dst, ranks(n), ALU.mult)
                dve.drain()
                nc.vector.tensor_reduce(top, dst, AX, ALU.max)
                dve.drain()
                TT(dst, dst, wide_(top, n), ALU.is_equal)
                dve.drain()

            dve.wait_ge(pe_did, t.pe_step.at(1))
            TT(lg, ps[:, 0:2, 0:20], b_router[:, l, :].unsqueeze(1).to_broadcast([P, NT, 20]), ALU.add)
            dve.drain()
            nc.vector.tensor_reduce(first, glog, AX, ALU.max)
            dve.drain()
            choose(group, glog, first, 4)
            TT(gexp, glog, wide_(first, 4), ALU.subtract).then_inc(dve_did, 1)
            dve.wait_ge(act_did, t.act_step.at(1))
            nc.vector.tensor_reduce(gsum, gexp, AX, ALU.add)
            TS(group, group, -NEG, NEG, ALU.mult, ALU.add)
            dve.drain()
            for tt in range(NT):
                e = elog[:, tt, :].rearrange("p (g e) -> p g e", e=4)
                TT(e, e, group[:, tt, :].unsqueeze(2).to_broadcast([P, 4, 4]), ALU.add)
            dve.drain()
            nc.vector.tensor_reduce(first, elog, AX, ALU.max)
            dve.drain()
            choose(one, elog, first, 16)
            nc.vector.scalar_tensor_tensor(elog, one, 2 * NEG, elog, ALU.mult, ALU.add)
            dve.drain()
            nc.vector.tensor_reduce(second, elog, AX, ALU.max)
            dve.drain()
            choose(other, elog, second, 16)
            TT(d, second, first, ALU.subtract).then_inc(dve_did, 1)
            dve.wait_ge(act_did, t.act_step.at(2))
            TS(first, d, 1.0, None, ALU.add)
            dve.drain()
            TT(first, first, gsum, ALU.mult)
            dve.drain()
            nc.vector.reciprocal(first, first)
            dve.drain()
            TT(second, first, d, ALU.mult)
            dve.drain()
            TT(one, one, wide_(first, 16), ALU.mult)
            TT(other, other, wide_(second, 16), ALU.mult)
            dve.drain()
            TT(gate[:, :, :], one, other, ALU.add)
            TS(Y[:, :, :], X[:, :, :], ALPHA, None, ALU.mult)
            dve.drain()
            t.add(pe_step=1, act_step=2, dve_step=2)

        def first_layer_sync(sp, t, l):
            attention_sync(sp, t, l)
            mlp_sync(sp, t, E, 0, lambda e: A["w1"][l, e], lambda e: A["w3"][l, e], lambda e: A["w2"][l, e])

        def first_layer_tensor(pe, t, l):
            attention_prepare_tensor(pe, t)
            stick_tensor(pe, t)
            softmax_heads_tensor(pe, t)
            attention_finish_tensor(pe, t, l)
            layer_norm_tensor(pe, t, l, LN1G)
            route_tensor(pe, t, l)
            mlp_tensor(pe, t, E, 0)
            layer_norm_tensor(pe, t, l, LN2G)

        def first_layer_scalar(act, t, l):
            attention_prepare_scalar(act, t, l)
            stick_scalar(act, t)
            softmax_heads_scalar(act, t)
            attention_finish_scalar(act, t, l)
            layer_norm_scalar(act, t)
            route_scalar(act, t)
            mlp_scalar(act, t, E, 0)
            layer_norm_scalar(act, t)

        def first_layer_vector(dve, t, l):
            attention_prepare_vector(dve, t, l)
            stick_vector(dve, t)
            softmax_heads_vector(dve, t)
            attention_finish_vector(dve, t, l)
            layer_norm_vector(dve, t)
            route_vector(dve, t, l)
            mlp_vector(dve, t, E, 0, lambda e: lambda tt: gate[:, tt, bass.ds(e, 1)])
            layer_norm_vector(dve, t)

        MOD = [512] * 6
        shift, scale1, gate_row = temp[:, 0:D], temp[:, D:2 * D], temp[:, 2 * D:3 * D]
        flat = proj[:, :, :].rearrange("p t n -> p (t n)")
        post = flat[:, 2 * N_IN - D:2 * N_IN]

        def modulate_sync(sp, t, l, s):
            for j in range(6):
                load_chunk(sp, t, columns(A["ada_w_2"][l], (6 * s + j) * 512, 512))

        def modulate_tensor(pe, t, l, s):
            for j in range(6):
                bank = 2 * (j % 2)
                if j % 2 == 0:
                    pe.wait_ge(mod_act, t.mod_act.at())
                else:
                    pe.wait_ge(mod_dve, t.mod_dve.at())
                pe.wait_ge(h_ready, t.mlp.at(1))
                pe.wait_ge(dve_did, t.dve_step.at())
                chunk_arrived(pe, t)
                w = slot_view(t, 512)
                r = ADAB + 3 * s + j // 2
                nc.tensor.matmul(ps[:, bank, :], ident[:, r:r + 1].to_broadcast([P, P]),
                                 rows[:, l, (j % 2) * 512:(j % 2 + 1) * 512], start=True, stop=False)
                for b in range(KD):
                    last = nc.tensor.matmul(ps[:, bank, :], c_feat[:, b:b + 1].to_broadcast([P, P]),
                                            w[:, b, :], start=False, stop=(b == KD - 1))
                last.then_inc(chunk_done, 1)
                t.add(chunk=1)
                if j % 2 == 0:
                    t.add(mod_act=1)
                else:
                    t.add(mod_dve=1)

        def modulate_scalar(act, t):
            act.wait_ge(dve_did, t.dve_step.at())
            for j in range(6):
                products_ready(act, t)
                t.add(chunk=1)
                if j % 2 == 0:
                    nc.scalar.copy(temp[:, j * 512:(j + 1) * 512], ps[:, 0, :]).then_inc(mod_act, 1)
                    t.add(mod_act=1)
                else:
                    t.add(mod_dve=1)

        def modulate_vector(dve, t):
            for j in range(6):
                products_ready(dve, t)
                t.add(chunk=1)
                if j % 2 == 1:
                    nc.vector.tensor_copy(temp[:, j * 512:(j + 1) * 512], ps[:, 2, :]).then_inc(mod_dve, 1)
                    t.add(mod_dve=1)
                else:
                    t.add(mod_act=1)
            dve.wait_ge(mod_act, t.mod_act.at())

        def squares_scalar(act, t, buf):
            act.wait_ge(dve_did, t.dve_step.at())
            for tt in range(NT):
                nc.scalar.activation(wide[:, tt * D:(tt + 1) * D], buf[:, tt, :], ACT.Square,
                                     accum_out=small[:, 7, tt:tt + 1])
            act.drain().then_inc(act_did, 1)
            t.add(act_step=1, dve_step=1)
            rsqrt_scalar(act, t, NT)

        def root_vector(dve, t, n, width, add=1e-6):
            t.add(act_step=1)
            dve.wait_ge(act_did, t.act_step.at())
            nc.vector.tensor_scalar(rs[:, 0, 0:n], small[:, 7, 0:n], 1.0 / width, add, ALU.mult,
                                    ALU.add).then_inc(dve_did, 1)
            t.add(dve_step=1, act_step=1)
            dve.wait_ge(act_did, t.act_step.at())

        def before_tensor(pe, t, l, s):
            modulate_tensor(pe, t, l, s)
            row_tensor(pe, t, l, PRE + s)
            row_tensor(pe, t, l, POST + s)
            t.add(act_step=2, dve_step=2)
            x_transpose_tensor(pe, t, Y)

        def before_scalar(act, t):
            modulate_scalar(act, t)
            squares_scalar(act, t, X)
            t.add(dve_step=1, row=2)
            transposed_move_scalar(act, t, x_groups(Y)[1])

        def before_vector(dve, t, weight, clear):
            modulate_vector(dve, t)
            dve.wait_ge(row_ready, t.row.at(1))
            nc.vector.scalar_tensor_tensor(scale1, scale1, 1.0, ROW, ALU.add, ALU.mult).then_inc(row_used, 1)
            dve.wait_ge(row_ready, t.row.at(2))
            nc.vector.scalar_tensor_tensor(post, gate_row, weight, ROW, ALU.mult, ALU.mult).then_inc(row_used, 1)
            t.add(row=2)
            root_vector(dve, t, NT, D)
            dve.drain()
            for tt in range(NT):
                nc.vector.scalar_tensor_tensor(Y[:, tt, :], X[:, tt, :], rs[:, 2, tt:tt + 1], scale1,
                                               ALU.mult, ALU.mult)
            dve.drain()
            for tt in range(NT):
                nc.vector.tensor_tensor(Y[:, tt, :], Y[:, tt, :], shift, ALU.add)
            dve.drain().then_inc(dve_did, 1)
            t.add(dve_step=1)
            transposed_move_vector(dve, t, x_groups(Y)[1])
            transposed(dve, t)
            if clear:
                nc.vector.memset(Y[:, :, :], 0.0)
                dve.drain()

        def after_tensor(pe, t):
            t.add(act_step=2, dve_step=3)

        def after_scalar(act, t):
            t.add(dve_step=1)
            squares_scalar(act, t, Y)
            t.add(dve_step=1)

        def after_vector(dve, t):
            dve.drain().then_inc(dve_did, 1)
            t.add(dve_step=1)
            root_vector(dve, t, NT, D)
            for tt in range(NT):
                nc.vector.scalar_tensor_tensor(Y[:, tt, :], Y[:, tt, :], rs[:, 2, tt:tt + 1], post,
                                               ALU.mult, ALU.mult)
            dve.drain()
            for tt in range(NT):
                nc.vector.tensor_tensor(X[:, tt, :], X[:, tt, :], Y[:, tt, :], ALU.add)
            dve.drain().then_inc(dve_did, 1)
            t.add(dve_step=1)

        FULL, REST = DFF // 512, DFF % 512

        def ffn_sync(sp, t, l, f):
            w1, w3, w2 = A["ffn_w1_2"][l, f], A["ffn_w3_2"][l, f], A["ffn_w2_2"][l, f]
            mlp_sync(sp, t, FULL, REST, lambda i: w1[:, bass.ds(i * 512, 512)],
                     lambda i: w3[:, bass.ds(i * 512, 512)], lambda i: w2[bass.ds(i * 512, 512), :],
                     w1[:, FULL * 512:DFF], w3[:, FULL * 512:DFF], w2[FULL * 512:DFF, :])

        one_weight = lambda i: lambda tt: 1.0

        ML_QK, ML_V = ML_HEADS * ML_DK, ML_HEADS * ML_DV
        ML_W = [512] * 6 + [8]
        ML_GATE = 2 * ML_QK + 2 * ML_V
        mlp_proj = flat[:, 0:NT * (ML_GATE + 8)].rearrange("p (t n) -> p t n", t=NT)
        gates_i, gates_f, F_tok, a_tok = (small[:, 8 + i, 0:8] for i in range(4))
        by_tile = lambda a: a.rearrange("p (t h) -> p t h", t=NT)
        ml_out = wide[:, 0:2 * D].rearrange("p (t n) -> p t n", t=NT)

        def to_buffer(buf, tt, widths):
            starts = [sum(widths[:j]) for j in range(len(widths))]

            def take(j, src):
                dst = buf[:, tt, starts[j]:starts[j] + widths[j]]
                return nc.scalar.copy(dst, src) if tt == 0 else nc.vector.tensor_copy(dst, src)

            return take

        def qk_blocks():
            src = lambda b, tt: mlp_proj[:, tt, b * P:(b + 1) * P]
            reads, _ = pairs(src, lambda b: feat[:, b, :], 8)
            return reads, [[(feat[:, b:b + 2, :].rearrange("p b s -> p (b s)"), P, 0, 2 * S, None)]
                           for b in range(0, 8, 2)]

        def ml_blocks():
            return pairs(lambda b, tt: ml_out[:, tt, b * P:(b + 1) * P], lambda b: feat[:, 8 + b, :], KD,
                         lambda b: ml_norm[:, b:b + 1])

        def mlstm_sync(sp, t):
            project_sync(sp, t, A["ml_w_in_2"][0], 0, ML_W)
            project_sync(sp, t, A["ml_w_out_2"][0], 0, OUT)

        def mlstm_tensor(pe, t):
            project_tensor(pe, t, lambda b, tt: XT[:, b, tt * P:(tt + 1) * P], ML_W)
            projected(pe, t)
            transpose_tensor(pe, t, qk_blocks()[0])
            transposed(pe, t)
            pe.wait_ge(dve_did, t.dve_step.at(2))
            for tt in range(NT):
                for st in range(NT):
                    last = nc.tensor.matmul(ps[:, 0, 4 * tt:4 * tt + 4], cum[:, st, tt * P:(tt + 1) * P],
                                            small[:, 6, 4 * st:4 * st + 4], start=(st == 0), stop=(st == NT - 1))
            last.then_inc(pe_did, 1)
            pe.wait_ge(dve_did, t.dve_step.at(3))
            for tt in range(NT):
                last = nc.tensor.transpose(ps[0:4, 1, tt * P:(tt + 1) * P], a_tok[:, 4 * tt:4 * tt + 4], ident[:, :])
            last.then_inc(pe_did, 1)
            pe.wait_ge(dve_did, t.dve_step.at(4))
            t.add(pe_step=2, act_step=1, dve_step=4)
            for h in range(ML_HEADS):
                q, k = feat[:, h, :], feat[:, 4 + h, :]
                pick = ident[0:4, h:h + 1].to_broadcast([4, P])
                for tt, (c0, nk) in enumerate(((0, P), (P, S))):
                    nc.tensor.matmul(ps[:, 0, c0:c0 + nk], pick, rowT[0:4, 0, 0:nk], start=True, stop=True)
                    last = nc.tensor.matmul(ps[:, 1, c0:c0 + nk], q[:, tt * P:(tt + 1) * P], k[:, 0:nk],
                                            start=True, stop=True)
                last.then_inc(pe_did, 1)
                pe.wait_ge(dve_did, t.dve_step.at(2))
                for c in range(3):
                    last = nc.tensor.transpose(ps[:, 2, c * P:(c + 1) * P], heads[:, 2, c * P:(c + 1) * P],
                                               ident[:, :])
                last.then_inc(pe_did, 1)
                pe.wait_ge(act_did, t.act_step.at(2))
                pv_tensor(ps[:, 3, :], heads[:, 4, :],
                          lambda tt: mlp_proj[:, tt, 2 * ML_QK + h * ML_DV:2 * ML_QK + (h + 1) * ML_DV]
                          ).then_inc(pe_did, 1)
                t.add(pe_step=3, act_step=2, dve_step=3)
                pe.wait_ge(dve_did, t.dve_step.at())
            t.add(act_step=3, dve_step=3)
            pe.wait_ge(dve_did, t.dve_step.at())
            transpose_tensor(pe, t, ml_blocks()[0])
            transposed(pe, t)
            project_tensor(pe, t, lambda b, tt: feat[:, 8 + b, tt * P:(tt + 1) * P], OUT)

        def mlstm_scalar(act, t):
            project_move(act, t, 0, ML_W, to_buffer(mlp_proj, 0, ML_W))
            transposed_move_scalar(act, t, qk_blocks()[1])
            softplus_scalar(act, t, 8)
            t.add(pe_step=2, dve_step=3)
            for h in range(ML_HEADS):
                act.wait_ge(dve_did, t.dve_step.at(1))
                for tt, (c0, c1) in enumerate(((0, P), (P, 384))):
                    nc.scalar.activation(heads[:, 1, c0:c1], heads[:, 0, c0:c1], ACT.Exp,
                                         bias=nmax[:, h, tt:tt + 1])
                nc.scalar.activation(rden[:, h, :], den[:, h, :], ACT.Exp)
                act.drain().then_inc(act_did, 1)
                act.wait_ge(pe_did, t.pe_step.at(2))
                nc.scalar.copy(heads[:, 4, :], ps[:, 2, 0:384]).then_inc(act_did, 1)
                t.add(pe_step=3, act_step=2, dve_step=3)
            projected(act, t)
            act.wait_ge(dve_did, t.dve_step.at())
            o = mlp_proj[:, :, 2 * ML_QK + ML_V:ML_GATE]
            nc.scalar.activation(o, o, ACT.Sigmoid)
            nc.scalar.activation(temp[:, 0:2 * D], wide[:, 0:2 * D], ACT.Square)
            act.drain().then_inc(act_did, 1)
            t.add(act_step=1, dve_step=1)
            rsqrt_scalar(act, t, 8)
            t.add(act_step=1, dve_step=2)
            act.drain().then_inc(act_did, 1)
            transposed_move_scalar(act, t, ml_blocks()[1])
            project_move(act, t, 0, OUT, lambda j, src: nc.scalar.copy(Y[:, 0, j * 512:(j + 1) * 512], src))

        def mlstm_vector(dve, t):
            project_move(dve, t, 1, ML_W, to_buffer(mlp_proj, 1, ML_W))
            projected(dve, t)
            transposed_move_vector(dve, t, qk_blocks()[1])
            TT = nc.vector.tensor_tensor
            gates = mlp_proj[:, :, ML_GATE:ML_GATE + 8]
            for g, dst in ((0, gates_i), (1, gates_f)):
                TT(by_tile(dst), gates[:, :, 4 * g:4 * g + 4],
                   b_gate[:, 4 * g:4 * g + 4].unsqueeze(1).to_broadcast([P, NT, 4]), ALU.add)
            dve.drain()
            nc.vector.tensor_scalar(small[:, 0, 0:8], gates_f, -1.0, None, ALU.mult)
            dve.drain()
            softplus_vector(dve, t, 8)
            nc.vector.tensor_scalar(small[:, 6, 0:8], small[:, 5, 0:8], -1.0, None,
                                    ALU.mult).then_inc(dve_did, 1)
            dve.wait_ge(pe_did, t.pe_step.at(1))
            nc.vector.tensor_copy(F_tok, ps[:, 0, 0:8])
            dve.drain()
            TT(a_tok, gates_i, F_tok, ALU.subtract).then_inc(dve_did, 1)
            dve.wait_ge(pe_did, t.pe_step.at(2))
            nc.vector.tensor_copy(rowT[0:4, 0, :], ps[0:4, 1, 0:S]).then_inc(dve_did, 1)
            t.add(pe_step=2, dve_step=3)
            for h in range(ML_HEADS):
                dve.wait_ge(pe_did, t.pe_step.at(1))
                TT(heads[:, 0, :], ps[:, 0, 0:384], masks[:, 0, :], ALU.add)
                dve.drain()
                for tt, (c0, c1) in enumerate(((0, P), (P, 384))):
                    nc.vector.tensor_reduce(nmax[:, h, tt:tt + 1], heads[:, 0, c0:c1], AX, ALU.max, negate=True)
                dve.drain()
                nc.vector.tensor_scalar(nmax[:, h, :], nmax[:, h, :], 0.0, None, ALU.min)
                dve.drain()
                TT(den[:, h, :], nmax[:, h, :], by_tile(F_tok)[:, :, h], ALU.subtract)
                dve.drain().then_inc(dve_did, 1)
                dve.wait_ge(act_did, t.act_step.at(1))
                nc.vector.scalar_tensor_tensor(heads[:, 2, :], ps[:, 1, 0:384], ML_DK ** -0.5, heads[:, 1, :],
                                               ALU.mult, ALU.mult)
                dve.drain()
                for tt, (c0, c1) in enumerate(((0, P), (P, 384))):
                    nc.vector.tensor_reduce(den[:, h, tt:tt + 1], heads[:, 2, c0:c1], AX, ALU.add)
                dve.drain().then_inc(dve_did, 1)
                nc.vector.scalar_tensor_tensor(den[:, h, :], den[:, h, :], -1.0, den[:, h, :], ALU.mult, ALU.max)
                dve.drain()
                TT(den[:, h, :], den[:, h, :], rden[:, h, :], ALU.max)
                dve.drain()
                nc.vector.reciprocal(den[:, h, :], den[:, h, :])
                dve.wait_ge(pe_did, t.pe_step.at(3))
                dve.drain()
                for tt in range(NT):
                    nc.vector.tensor_scalar(ml_out[:, tt, h * ML_DV:(h + 1) * ML_DV],
                                            ps[:, 3, tt * ML_DV:(tt + 1) * ML_DV], den[:, h, tt:tt + 1], None,
                                            ALU.mult)
                dve.drain().then_inc(dve_did, 1)
                t.add(pe_step=3, act_step=2, dve_step=3)
            t.add(act_step=1)
            dve.wait_ge(act_did, t.act_step.at())
            nc.vector.tensor_reduce(small[:, 7, 0:8], temp[:, 0:2 * D].rearrange("p (n d) -> p n d", d=ML_DV),
                                    AX, ALU.add)
            dve.drain()
            nc.vector.tensor_scalar(rs[:, 0, 0:8], small[:, 7, 0:8], 1.0 / ML_DV, 1e-6, ALU.mult,
                                    ALU.add).then_inc(dve_did, 1)
            t.add(act_step=1, dve_step=1)
            dve.wait_ge(act_did, t.act_step.at())
            w3 = wide[:, 0:2 * D].rearrange("p (n d) -> p n d", d=ML_DV)
            TT(w3, w3, rs[:, 2, 0:8].unsqueeze(2).to_broadcast([P, 8, ML_DV]), ALU.mult)
            dve.drain().then_inc(dve_did, 1)
            t.add(act_step=1, dve_step=2)
            TT(ml_out, ml_out, mlp_proj[:, :, 2 * ML_QK + ML_V:ML_GATE], ALU.mult)
            dve.drain().then_inc(dve_did, 1)
            transposed_move_vector(dve, t, ml_blocks()[1])
            project_move(dve, t, 1, OUT, lambda j, src: nc.vector.tensor_copy(Y[:, 1, j * 512:(j + 1) * 512], src))
            projected(dve, t)

        MB_CB = 24
        Z_W = [512] * 4
        mb_z = flat[:, 0:NT * MB_DI].rearrange("p (t n) -> p t n", t=NT)
        xs = wide[:, :].rearrange("p (t n) -> p t n", t=NT)
        bc = temp[:, 0:4 * 384].rearrange("p (g n) -> p g n", n=384)
        conv_acc = temp[:, 1536:3072].rearrange("p (a n) -> p a n", n=S)
        dt_tok, dtA, a_mid = (small[:, 8 + i, :] for i in range(3))
        dt_bias, A_log, D_skip = (mb_head[:, i, :] for i in range(3))
        tok32 = lambda a: a.rearrange("p (t h) -> p t h", t=NT)

        def xs_blocks():
            reads, moves = [], []
            for tt in range(NT):
                for b in range(0, 16, 4):
                    reads.append([(P, i * P, feat[:, b + i, tt * P:(tt + 1) * P]) for i in range(4)])
                    moves.append([(xs[:, tt, b * P:(b + 4) * P], P, 0, 512, None)])
            return reads, moves

        def mb_blocks():
            return pairs(lambda b, tt: xs[:, tt, b * P:(b + 1) * P], lambda b: feat[:, b, :], 16,
                         lambda b: mb_norm[:, b:b + 1])

        def mamba_sync(sp, t):
            w = A["mb_w_in_2"][0]
            project_sync(sp, t, w, 0, Z_W)
            for j in range(6):
                load_chunk(sp, t, columns(w, MB_DI + j * 512, 512))
            project_sync(sp, t, w, 2 * MB_DI + 2 * MB_G * P, [32])
            project_sync(sp, t, A["mb_w_out_2"][0], 0, OUT)

        def mamba_tensor(pe, t):
            lhs = lambda b, tt: XT[:, b, tt * P:(tt + 1) * P]
            project_tensor(pe, t, lhs, Z_W)
            projected(pe, t)
            for j in range(6):
                if j >= 2:
                    pe.wait_ge(conv_read, 4 * (j - 1))
                chunk_arrived(pe, t)
                w = slot_view(t, 512)
                for i in range(4):
                    for b in range(KD):
                        last = nc.tensor.matmul(ps[:, 2 * (j % 2) + i // 2, (i % 2) * S:(i % 2 + 1) * S],
                                                w[:, b, i * P:(i + 1) * P], XT[:, b, :],
                                                start=(b == 0), stop=(b == KD - 1))
                last.then_inc(chunk_done, 1)
                t.add(chunk=1)
            pe.wait_ge(conv_read, MB_CB)
            project_tensor(pe, t, lhs, [32])
            pe.wait_ge(conv_done, MB_CB)
            transpose_tensor(pe, t, xs_blocks()[0])
            transposed(pe, t)
            projected(pe, t)
            for g in range(MB_G):
                Bg, Cg = feat[:, 16 + g, :], feat[:, 20 + g, :]
                nc.tensor.matmul(ps[:, g, 0:S], Bg[:, 0:P], Cg, start=True, stop=True)
                last = nc.tensor.matmul(ps[:, g, S:384], Bg[:, P:S], Cg[:, P:S], start=True, stop=True)
            last.then_inc(pe_did, 1)
            pe.wait_ge(dve_did, t.dve_step.at(3))
            dA = tok32(dtA)
            for tt in range(NT):
                for st in range(NT):
                    nc.tensor.matmul(ps[:, 6, 32 * tt:32 * tt + 32], mid[:, st, tt * P:(tt + 1) * P],
                                     dA[:, st, :], start=(st == 0), stop=(st == NT - 1))
            for st in range(NT):
                last = nc.tensor.matmul(ps[0:32, 7, 0:S], dA[:, st, :], mid[:, st, :],
                                        start=(st == 0), stop=(st == NT - 1))
            last.then_inc(pe_did, 1)
            pe.wait_ge(dve_did, t.dve_step.at(4))
            t.add(pe_step=2, act_step=2, dve_step=4)

            def row(h):
                if h >= 2:
                    pe.wait_ge(decay_ready, h - 1)
                nc.tensor.matmul(ps[:, h % 2, 0:S], ident[0:32, h:h + 1].to_broadcast([32, P]),
                                 rowT[0:32, 0, :], start=True, stop=True)
                nc.tensor.matmul(ps[:, h % 2, S:384], ident[0:32, h:h + 1].to_broadcast([32, P]),
                                 rowT[0:32, 0, P:S], start=True, stop=True).then_inc(decay_row, 1)

            def output(h):
                pe.wait_ge(weights_ready, h + 1)
                if h >= 2:
                    pe.wait_ge(state_used, h - 1)
                pv_tensor(ps[:, 6 + h % 2, 0:2 * HD], heads[:, 4 + h % 2, :],
                          lambda tt: xs[:, tt, h * HD:(h + 1) * HD]).then_inc(state_out, 1)

            row(0)
            for h in range(MB_H):
                if h + 1 < MB_H:
                    row(h + 1)
                output(h)
            t.add(act_step=3, dve_step=4)
            pe.wait_ge(dve_did, t.dve_step.at())
            transpose_tensor(pe, t, mb_blocks()[0])
            transposed(pe, t)
            project_tensor(pe, t, lambda b, tt: feat[:, b, tt * P:(tt + 1) * P], OUT, depth=2)

        def mamba_scalar(act, t):
            project_move(act, t, 0, Z_W, to_buffer(mb_z, 0, Z_W))
            for b in range(MB_CB):
                act.wait_ge(conv_read, b + 1)
                nc.scalar.activation(feat[:, b, :], conv_acc[:, b % 6, :], ACT.Silu,
                                     bias=conv_b[:, b:b + 1]).then_inc(conv_done, 1)
            t.add(chunk=6)
            projected(act, t)
            nc.scalar.activation(mb_z, mb_z, ACT.Silu)
            project_move(act, t, 0, [32], lambda j, src: nc.scalar.copy(tok32(dt_tok)[:, 0, :], src))
            transposed_move_scalar(act, t, xs_blocks()[1])
            softplus_scalar(act, t, 64)
            act.drain()
            nc.scalar.activation(A_log, A_log, ACT.Exp).then_inc(act_did, 1)
            t.add(pe_step=2, act_step=1, dve_step=3)
            for h in range(MB_H):
                act.wait_ge(decay_ready, h + 1)
                if h >= 2:
                    act.wait_ge(weights_ready, h - 1)
                nc.scalar.activation(heads[:, 2 + h % 2, :], heads[:, h % 2, :], ACT.Exp).then_inc(decays, 1)
            act.wait_ge(dve_did, t.dve_step.at(1))
            for i in range(NT):
                for g in range(4):
                    last = nc.scalar.activation(temp[:, 0:512], xs[:, i, g * 512:(g + 1) * 512], ACT.Square,
                                                accum_out=small[:, 7, 4 * i + g:4 * i + g + 1])
                    act.drain()
            act.drain().then_inc(act_did, 1)
            t.add(act_step=1, dve_step=2)
            rsqrt_scalar(act, t, 8)
            t.add(act_step=1, dve_step=2)
            act.drain().then_inc(act_did, 1)
            transposed_move_scalar(act, t, mb_blocks()[1])
            project_move(act, t, 0, OUT, lambda j, src: nc.scalar.copy(Y[:, 0, j * 512:(j + 1) * 512], src), depth=2)

        def mamba_vector(dve, t):
            TT, STT = nc.vector.tensor_tensor, nc.vector.scalar_tensor_tensor
            project_move(dve, t, 1, Z_W, to_buffer(mb_z, 1, Z_W))
            for j in range(6):
                products_ready(dve, t)
                for i in range(4):
                    b = 4 * j + i
                    src = ps[:, 2 * (j % 2) + i // 2, (i % 2) * S:(i % 2 + 1) * S]
                    acc = conv_acc[:, b % 6, :]
                    if b >= 6:
                        dve.wait_ge(conv_done, b - 5)
                    nc.vector.tensor_scalar(acc, src, conv_w[:, 3, b:b + 1], None, ALU.mult)
                    for d in (1, 2, 3):
                        dve.drain()
                        last = STT(acc[:, d:S], src[:, 0:S - d], conv_w[:, 3 - d, b:b + 1], acc[:, d:S],
                                   ALU.mult, ALU.add)
                    last.then_inc(conv_read, 1)
                t.add(chunk=1)
            project_move(dve, t, 1, [32], lambda j, src: nc.vector.tensor_copy(tok32(dt_tok)[:, 1, :], src))
            projected(dve, t)
            transposed_move_vector(dve, t, xs_blocks()[1])
            TT(tok32(small[:, 0, :]), tok32(dt_tok), dt_bias.unsqueeze(1).to_broadcast([P, NT, 32]), ALU.add)
            dve.drain()
            softplus_vector(dve, t, 64)
            t.add(act_step=1)
            dve.wait_ge(act_did, t.act_step.at())
            nc.vector.tensor_copy(dt_tok, small[:, 5, :])
            STT(tok32(dtA), tok32(small[:, 5, :]), -1.0, A_log.unsqueeze(1).to_broadcast([P, NT, 32]),
                ALU.mult, ALU.mult).then_inc(dve_did, 1)
            dve.wait_ge(pe_did, t.pe_step.at(1))
            nc.vector.tensor_copy(bc, ps[:, 0:4, 0:384])
            dve.drain().then_inc(dve_did, 1)
            dve.wait_ge(pe_did, t.pe_step.at(2))
            nc.vector.tensor_copy(a_mid, ps[:, 6, 0:64])
            nc.vector.tensor_copy(rowT[0:32, 0, :], ps[0:32, 7, 0:S])
            dve.drain().then_inc(dve_did, 1)
            t.add(pe_step=2, dve_step=3)
            am, dts = tok32(a_mid), tok32(dt_tok)

            def exponent(h):
                dve.wait_ge(decay_row, h + 1)
                if h >= 2:
                    dve.wait_ge(decays, h - 1)
                for st, (c0, c1) in enumerate(((0, S), (S, 384))):
                    last = STT(heads[:, h % 2, c0:c1], ps[:, h % 2, c0:c1], am[:, st, h:h + 1],
                               masks[:, 5, c0:c1], ALU.subtract, ALU.add)
                last.then_inc(decay_ready, 1)

            def weights(h):
                dve.wait_ge(decays, h + 1)
                if h >= 2:
                    dve.wait_ge(state_out, h - 1)
                for st, (c0, c1) in enumerate(((0, S), (S, 384))):
                    last = STT(heads[:, 4 + h % 2, c0:c1], heads[:, 2 + h % 2, c0:c1], dts[:, st, h:h + 1],
                               bc[:, h // (MB_H // MB_G), c0:c1], ALU.mult, ALU.mult)
                last.then_inc(weights_ready, 1)

            def use(h):
                dve.wait_ge(state_out, h + 1)
                x = xs[:, :, h * HD:(h + 1) * HD]
                STT(x, x, D_skip[:, h:h + 1], ps[:, 6 + h % 2, 0:2 * HD].rearrange("p (t d) -> p t d", t=NT),
                    ALU.mult, ALU.add).then_inc(state_used, 1)

            exponent(0)
            for h in range(MB_H):
                if h + 1 < MB_H:
                    exponent(h + 1)
                weights(h)
                if h >= 1:
                    use(h - 1)
            use(MB_H - 1)
            dve.drain()
            TT(xs, xs, mb_z, ALU.mult)
            dve.drain().then_inc(dve_did, 1)
            t.add(act_step=1, dve_step=1)
            dve.wait_ge(act_did, t.act_step.at())
            nc.vector.tensor_scalar(rs[:, 0, 0:8], small[:, 7, 0:8], 1.0 / 512, 1e-6, ALU.mult,
                                    ALU.add).then_inc(dve_did, 1)
            t.add(act_step=1, dve_step=1)
            dve.wait_ge(act_did, t.act_step.at())
            w3 = wide[:, :].rearrange("p (n d) -> p n d", d=512)
            TT(w3, w3, rs[:, 2, 0:8].unsqueeze(2).to_broadcast([P, 8, 512]), ALU.mult)
            dve.drain().then_inc(dve_did, 1)
            dve.drain().then_inc(dve_did, 1)
            t.add(act_step=1, dve_step=2)
            transposed_move_vector(dve, t, mb_blocks()[1])
            project_move(dve, t, 1, OUT, lambda j, src: nc.vector.tensor_copy(Y[:, 1, j * 512:(j + 1) * 512], src), depth=2)
            projected(dve, t)

        def loads():
            a = A
            bcast = lambda v: v.partition_broadcast(P)
            out = [
                (masks[:, :, :], a["c_masks"]), (rope64[:, :, :], a["c_rope64"]), (rope32[:, :, :], a["c_rope32"]),
                (cum[:, :, :], a["c_cum"]), (mid[:, :, :], a["c_mid"]), (ident[:, :], a["c_ident"]),
                (later[:, :], a["c_later"]), (rank[:, :], a["c_rank"]),
                (b_forget[:, :, :], bcast(a["b_forget"])),
                (b_router[:, :, 0:4], bcast(a["b_group"])), (b_router[:, :, 4:20], bcast(a["b_expert"])),
                (b_gate[:, :], bcast(a["ml_b_gate_2"][0])),
                (mb_head[:, 0, :], bcast(a["mb_dt_bias_2"][0])), (mb_head[:, 1, :], bcast(a["mb_A_log_2"][0])),
                (mb_head[:, 2, :], bcast(a["mb_D_2"][0])),
                (g_cq[:, :, :], a["g_cq"].rearrange("l (b p) -> p l b", p=P)),
                (g_ckv[:, :], a["g_ckv"].rearrange("l p -> p l")),
                (g_head[:, :, :], a["g_head"].rearrange("l (b h) d -> (h d) l b", h=2)),
                (ml_norm[:, :], a["ml_norm_w_2"][0].rearrange("(b p) -> p b", p=P)),
                (mb_norm[:, :], a["mb_norm_w_2"][0].rearrange("(b p) -> p b", p=P)),
                (conv_b[:, :], a["mb_conv_b_2"][0].rearrange("(b p) -> p b", p=P)),
                (c_feat[:, :], a["c_2"][0].rearrange("(b p) -> p b", p=P)),
            ]
            for j in range(4):
                out.append((conv_w[:, j, :], a["mb_conv_w_2"][0, j].rearrange("(b p) -> p b", p=P)))
            for l in range(L):
                out.append((w_router[:, l, :, 0:4], a["w_group"][l].rearrange("(b p) n -> p b n", p=P)))
                out.append((w_router[:, l, :, 4:20], a["w_expert"][l].rearrange("(b p) n -> p b n", p=P)))
            for i, n in enumerate(("ln1_g", "ln1_b", "ln2_g", "ln2_b")):
                out.append((rows[i:i + 1, :, :], a[n].unsqueeze(0)))
            for r, n in ((PRE, "norm_pre_2"), (POST, "norm_post_2")):
                out.append((rows[r:r + 3, :, :], a[n].rearrange("l s d -> s l d")))
            out.append((rows[ADAB:ADAB + 9, :, :], a["ada_b_2"].rearrange("l (r d) -> r l d", d=D)))
            return out

        LOADS = loads()
        assert len(LOADS) == N_LOADS, len(LOADS)
        ctx.enter_context(nc.allow_non_contiguous_dma(reason="small parameters, one feature a partition"))
        block = ctx.enter_context(nc.Block())

        SECOND = [(l, s) for l in range(L) for s in range(3)]

        @block.sync
        def _(sp):
            t = Tallies()
            with t.loop(sp, L, SYNC_LAYER) as l:
                first_layer_sync(sp, t, l)
            for l, s in SECOND:
                modulate_sync(sp, t, l, s)
                if s != 1:
                    ffn_sync(sp, t, l, s // 2)
                elif l == 0:
                    mlstm_sync(sp, t)
                else:
                    mamba_sync(sp, t)
            sp.wait_ge(dve_did, END_STEPS)
            sp.dma_start(out[0].rearrange("(t p) d -> p t d", p=P), X[:, :, :]).then_inc(stored, 16)
            sp.wait_ge(stored, 16)

        @block.gpsimd
        def _(pool):
            nc.gpsimd.memset(rows[:, :, :], 0.0).then_inc(ones_set, 1)
            nc.gpsimd.memset(ones[:, :], 1.0).then_inc(ones_set, 1)
            pool.wait_ge(ones_set, 2)
            for dst, src in LOADS:
                pool.dma_start(dst, src).then_inc(loaded, 16)

        @block.tensor
        def _(pe):
            t = Tallies()
            pe.sem_inc(chunk_done, CREDIT)
            t.add(dve_step=1, act_step=1)
            pe.wait_ge(loaded, 16 * N_LOADS)
            pe.wait_ge(ones_set, 2)
            pe.wait_ge(dve_did, 1)
            with t.loop(pe, L, LAYER) as l:
                first_layer_tensor(pe, t, l)
            for l, s in SECOND:
                before_tensor(pe, t, l, s)
                if s != 1:
                    mlp_tensor(pe, t, FULL, REST)
                elif l == 0:
                    mlstm_tensor(pe, t)
                else:
                    mamba_tensor(pe, t)
                after_tensor(pe, t)
            done["pe"] = t.counts()

        @block.scalar
        def _(act):
            t = Tallies()
            act.dma_start(X[:, :, :], A["x"][0].rearrange("(t p) d -> p t d", p=P)).then_inc(x_loaded, 16)
            for s in (proj_act, tr_act, hT_ready):
                act.sem_inc(s, 1)
            t.add(dve_step=1)
            act.wait_ge(loaded, 16 * N_LOADS)
            nc.scalar.activation(c_feat[:, :], c_feat[:, :], ACT.Silu).then_inc(act_did, 1)
            t.add(act_step=1)
            with t.loop(act, L, LAYER) as l:
                first_layer_scalar(act, t, l)
            for l, s in SECOND:
                before_scalar(act, t)
                if s != 1:
                    mlp_scalar(act, t, FULL, REST)
                elif l == 0:
                    mlstm_scalar(act, t)
                else:
                    mamba_scalar(act, t)
                after_scalar(act, t)
            done["act"] = t.counts()

        @block.vector
        def _(dve):
            t = Tallies()
            for s in (proj_dve, tr_dve, row_used, h_ready):
                dve.sem_inc(s, 1)
            dve.sem_inc(y_used, 2)
            dve.wait_ge(loaded, 16 * N_LOADS)
            dve.wait_ge(act_did, 1)
            dve.wait_ge(x_loaded, 16)
            dve.drain().then_inc(dve_did, 1)
            t.add(dve_step=1, act_step=1)
            with t.loop(dve, L, LAYER) as l:
                first_layer_vector(dve, t, l)
            for l, s in SECOND:
                before_vector(dve, t, 0.5 if s != 1 else 1.0, s != 1)
                if s != 1:
                    mlp_vector(dve, t, FULL, REST, one_weight)
                elif l == 0:
                    mlstm_vector(dve, t)
                else:
                    mamba_vector(dve, t)
                after_vector(dve, t)
            done["dve"] = t.counts()

        assert done["pe"] == done["act"] == done["dve"], done
        assert done["dve"][TALLIES.index("dve_step")] == END_STEPS, done

    return nc


def kernel(**inputs):
    import concourse.bacc as bacc
    from concourse.bass_utils import run_bass_kernel_spmd

    arrays = {name: np.ascontiguousarray(a) for name, a in inputs.items()}
    arrays.update(shape_constants(inputs["x"].shape[1]))
    nc = bacc.Bacc("TRN2", target_bir_lowering=False, num_devices=1)
    A = {name: nc.dram_tensor(f"in_{name}", a.shape, F32, kind="ExternalInput").ap()
         for name, a in arrays.items()}
    out = nc.dram_tensor("out", inputs["x"].shape, F32, kind="ExternalOutput").ap()
    build(nc, A, out)
    result = run_bass_kernel_spmd(nc, [{f"in_{name}": a for name, a in arrays.items()}], core_ids=[0])
    return result.results[0]["out"]
```

```python
from contextlib import ExitStack, contextmanager

import numpy as np

import concourse.bass as bass
from concourse import mybir

F32 = mybir.dt.float32
F32R = mybir.dt.float32r
ALU = mybir.AluOpType
ACT = mybir.ActivationFunctionType
AX = mybir.AxisListType.X

P = 128
RAW = 3
SPLIT = 2
PIECE = 2048
NEG = -1e30
LOG1P_SERIES_BELOW = 0.03


class Tally:

    def __init__(self):
        self.count, self.around = 0, []

    def at(self, more=0, times=1, per=1):
        value = times * ((self.count + more) // per)
        for i, n in self.around:
            value = i * (n * times // per) + value
        return value

    def add(self, n=1):
        self.count += n


TALLIES = ("raw", "piece", "proj", "tr_act", "tr_dve", "turn", "row", "y", "mlp", "pe_step",
           "act_step", "dve_step", "head", "ada")


class Tallies:

    def __init__(self):
        self.raw, self.piece, self.proj = Tally(), Tally(), Tally()
        self.tr_act, self.tr_dve, self.turn, self.row = Tally(), Tally(), Tally(), Tally()
        self.y, self.mlp, self.head, self.ada = Tally(), Tally(), Tally(), Tally()
        self.pe_step, self.act_step, self.dve_step = Tally(), Tally(), Tally()
        self.all = (self.raw, self.piece, self.proj, self.tr_act, self.tr_dve, self.turn, self.row,
                    self.y, self.mlp, self.pe_step, self.act_step, self.dve_step, self.head, self.ada)
        self.ahead = 0

    def counts(self):
        return tuple(x.count for x in self.all)

    def add(self, **more):
        for name, n in more.items():
            self.all[TALLIES.index(name)].add(n)

    @contextmanager
    def loop(self, engine, n, per):
        before = self.counts()
        with engine.Fori(0, n) as i:
            for tally, k in zip(self.all, per):
                if k:
                    tally.around.append((i, k))
            yield i
            for tally, k in zip(self.all, per):
                if k:
                    tally.around.pop()
        added = tuple(b - a for a, b in zip(before, self.counts()))
        assert added == tuple(per), f"one iteration adds {added}, not {tuple(per)}"
        for tally, k in zip(self.all, per):
            tally.add((n - 1) * k)


def shape_constants(S):
    pos = np.arange(S)
    q, k = pos[:, None], pos[None, :]

    def row_layout(valid):
        bias = np.where(valid, 0.0, NEG).astype(np.float32)
        return np.concatenate([bias[:P, :P], bias[P:, :]], axis=1)

    def column_layout(valid):
        bias = np.where(valid, 0.0, NEG).astype(np.float32).T
        return np.concatenate([bias[:P, :], bias[P:, P:]], axis=1)

    dist = q - k
    masks = [row_layout(dist >= 0)]
    for window, dil in ((128, 1), (512, 4), (2048, 16)):
        masks.append(row_layout((dist >= 0) & (dist <= window) & (dist % dil == 0)))
    masks.append(column_layout(dist > 0))
    masks.append(column_layout(dist >= 0))

    def rope(half):
        freq = np.float32(10000.0) ** (-np.arange(half, dtype=np.float32) / np.float32(half))
        ang = pos.astype(np.float32)[:, None] * freq.astype(np.float32)[None, :]
        return np.concatenate([np.cos(ang), np.sin(ang)], axis=1).astype(np.float32)

    cum = (q <= k).astype(np.float32)
    mid = np.where(k >= P, (q >= P) & (q <= k), 0) - np.where(k < P, (q > k) & (q < P), 0)
    tok = lambda a: np.ascontiguousarray(a.reshape(S // P, P, -1).transpose(1, 0, 2))
    return {
        "c_masks": np.stack(masks, axis=1).astype(np.float32),
        "c_rope64": tok(rope(32)),
        "c_rope32": tok(rope(16)),
        "c_cum": tok(cum),
        "c_mid": tok(mid.astype(np.float32)),
        "c_ident": np.eye(P, dtype=np.float32),
        "c_later": (q[:P] >= k[:, :P]).astype(np.float32),
        "c_rank": np.broadcast_to(16.0 - np.arange(16, dtype=np.float32), (P, 16)).copy(),
    }


def build(nc, A, out):
    S, D = A["x"].shape[1:]
    L = A["w_in"].shape[0]
    NT = S // P
    KD = D // P
    E, FE = A["w1"].shape[1], A["w1"].shape[3]
    DFF = A["ffn_w1_2"].shape[3]
    HD = 64
    ALPHA = (2.0 * L) ** 0.25
    N_IN = A["w_in"].shape[2]
    FOX, MLA, DIL = 768, 1540, 1956
    DQ, DKV, DR = 256, 128, 32
    ML_HEADS, ML_DK, ML_DV = 4, 128, 256
    MB_DI, MB_G, MB_H = 2048, 4, 32
    ROWS = 19
    LN1G, LN1B, LN2G, LN2B, PRE, POST, ADAB = 0, 1, 2, 3, 4, 7, 10
    assert (S, D, L, NT) == (256, 1024, 2, 2)

    ctx = ExitStack()
    with ctx:
        def sb(name, shape):
            return ctx.enter_context(nc.sbuf_tensor(name, shape, F32))

        def sem(name):
            return ctx.enter_context(nc.semaphore(name))

        def at(name, shape, dtype, where):
            return nc.alloc_sbuf_tensor_at(name, shape, dtype, offset=where)

        def region(name, floats):
            where = nc.sbuf_base
            whole = sb(name, [P, floats])
            return whole, where

        ring = sb("ring", [P, RAW, PIECE])
        w_hi = ctx.enter_context(nc.sbuf_tensor("w_hi", [P, SPLIT, PIECE], F32R))
        w_lo = ctx.enter_context(nc.sbuf_tensor("w_lo", [P, SPLIT, PIECE], F32R))
        X = sb("X", [P, NT, D])
        Y = sb("Y", [P, NT, D])
        proj_all, proj_at = region("proj", NT * N_IN)
        feat_all, feat_at = region("feat", 28 * S)
        wide, wide_at = region("wide", 4096)
        heads_all, heads_at = region("heads", 6 * 384)
        temp = sb("temp", [P, 3072])
        kv = sb("kv", [P, NT, 512])
        proj = proj_all[:, :].rearrange("p (t n) -> p t n", t=NT)
        feat = feat_all[:, :].rearrange("p (b s) -> p b s", s=S)
        heads = heads_all[:, :].rearrange("p (b n) -> p b n", n=384)
        K4 = 4 * KD * S
        XTh = at("XTh", [P, KD, S], F32R, wide_at)
        XTl = at("XTl", [P, KD, S], F32R, wide_at + K4)
        OTh = at("OTh", [P, KD, S], F32R, feat_at)
        OTl = at("OTl", [P, KD, S], F32R, feat_at + K4)
        MTh = at("MTh", [P, 2 * KD, S], F32R, feat_at)
        MTl = at("MTl", [P, 2 * KD, S], F32R, proj_at)
        latent_h = at("latent_h", [P, 3, S], F32R, heads_at + 4 * 4 * 384)
        latent_l = at("latent_l", [P, 3, S], F32R, heads_at + 4 * 2 * 384)
        mlp_silu = proj_all[:, 0:1024].rearrange("p (t n) -> p t n", t=NT)
        mlp_h = proj_all[:, 1024:2048].rearrange("p (t n) -> p t n", t=NT)
        hTh = at("hTh", [P, 4, S], F32R, proj_at + 4 * 2048)
        hTl = at("hTl", [P, 4, S], F32R, proj_at + 4 * 3072)
        ada_ring = feat_all[:, 0:3 * PIECE].rearrange("p (a n) -> p a n", n=PIECE)
        ada_acc = proj_all[:, 4096:4096 + 12 * S]
        masks = sb("masks", [P, 6, 384])
        rope64 = sb("rope64", [P, NT, 64])
        rope32 = sb("rope32", [P, NT, 32])
        cum = sb("cum", [P, NT, S])
        mid = sb("mid", [P, NT, S])
        ident = sb("ident", [P, P])
        later = sb("later", [P, P])
        ones = sb("ones", [P, P])
        rank = sb("rank", [P, 16])
        rows = sb("rows", [P, L, D])
        rowT = sb("rowT", [32, 2, S])
        b_forget = sb("b_forget", [P, L, 4])
        b_router = sb("b_router", [P, L, 20])
        wr_h = ctx.enter_context(nc.sbuf_tensor("wr_h", [P, L, KD, 20], F32R))
        wr_l = ctx.enter_context(nc.sbuf_tensor("wr_l", [P, L, KD, 20], F32R))
        g_cq = sb("g_cq", [P, L, 2])
        g_ckv = sb("g_ckv", [P, L])
        g_head = sb("g_head", [P, L, KD])
        b_gate = sb("b_gate", [P, 8])
        ml_norm = sb("ml_norm", [P, KD])
        mb_norm = sb("mb_norm", [P, 16])
        conv_w = sb("conv_w", [P, 4, 24])
        conv_b = sb("conv_b", [P, 24])
        mb_head = sb("mb_head", [P, 3, 32])
        c_feat = sb("c_feat", [P, KD])
        stats = sb("stats", [P, NT, 2, 6])
        mv = sb("mv", [P, NT, 2])
        rs = sb("rs", [P, 3, 32])
        gate = sb("gate", [P, NT, 16])
        small = sb("small", [P, 12, 64])
        lse = sb("lse", [P, 5, 8])
        nmax = sb("nmax", [P, 24, NT])
        den = sb("den", [P, 24, NT])
        rden = sb("rden", [P, 24, NT])
        ps = ctx.enter_context(nc.psum_tensor("ps", [P, 8, 512], F32))

        w_router = temp[:, 0:L * KD * 20].rearrange("p (l k n) -> p l k n", l=L, k=KD)
        heads_out = wide[:, 0:2048].rearrange("p (t h d) -> p t h d", t=NT, h=16)
        dil_out = wide[:, 2048:3584].rearrange("p (b t h d) -> p b t h d", b=3, t=NT, h=4)

        loaded = sem("constants_loaded")
        ident_loaded = sem("ident_loaded")
        c_loaded = sem("c_loaded")
        params_ready = sem("params_ready")
        x_loaded = sem("x_loaded")
        raw_ready = [sem(f"raw_ready{i}") for i in range(RAW)]
        raw_used = sem("raw_used")
        hi_ready = sem("hi_ready")
        piece_done = sem("piece_done")
        turned = sem("turned")
        turned_hi = sem("turned_hi")
        turned_lo = sem("turned_lo")
        proj_act = sem("proj_moved_by_act")
        proj_dve = sem("proj_moved_by_dve")
        tr_to_act = sem("transposed_for_act")
        tr_to_dve = sem("transposed_for_dve")
        tr_act = sem("transposed_moved_by_act")
        tr_dve = sem("transposed_moved_by_dve")
        row_ready = sem("row_ready")
        row_used = sem("row_used")
        silu_done = sem("silu_done")
        h_ready = sem("h_ready")
        hT_psum = sem("hT_in_psum")
        hT_ready = sem("hT_ready")
        hT_hi = sem("hT_hi")
        y_ready = sem("y_ready")
        y_used = sem("y_used")
        pe_did = sem("pe_did")
        act_did = sem("act_did")
        dve_did = sem("dve_did")
        stored = sem("stored")
        scores_ready = sem("scores_ready")
        logits_ready = sem("logits_ready")
        probs_ready = sem("probs_ready")
        probs_turned = sem("probs_turned")
        probsT_ready = sem("probsT_ready")
        output_ready = sem("output_ready")
        output_used = sem("output_used")
        ada_loaded = [sem(f"ada_loaded{j}") for j in range(3)]
        ada_read = sem("ada_read")
        ada_ready = sem("ada_ready")
        ada_psum = sem("ada_in_psum")
        ada_used = sem("ada_used")
        conv_read = sem("conv_read")
        conv_done = sem("conv_done")
        decay_row = sem("decay_row")
        decay_ready = sem("decay_ready")
        decays = sem("decays")
        weights_ready = sem("weights_ready")
        state_out = sem("state_out")
        state_used = sem("state_used")
        ones_set = sem("ones_set")
        done = {}

        N_LOADS = 35
        POOL_LAYER = (0,) * 13 + (12,)
        LAYER = (120, 120, 13, 7, 7, 14, 4, 32, 16, 5, 13, 20, 20, 12)
        SYNC_LAYER = (120, 96, 13, 0, 0, 0, 0, 32, 16, 0, 0, 0, 0, 12)
        END_STEPS = 98

        def load_piece(sp, t, source):
            slot = t.raw.count % RAW
            blocks, n = source.shape[1:]
            sp.wait_ge(raw_used, t.raw.at(1))
            sp.dma_start(ring[:, slot, 0:blocks * n].rearrange("p (k n) -> p k n", n=n),
                         source).then_inc(raw_ready[slot], 16)
            t.add(raw=1)

        def blocks_of(w):
            return w.rearrange("(k p) n -> p k n", p=P)

        def raw_arrived(eng, t, ahead):
            i = t.raw.count + ahead
            eng.wait_ge(raw_ready[i % RAW], t.raw.at(RAW + ahead, 16, RAW))

        def split_scalar(act, t, n=PIECE, raw_ahead=0):
            raw_arrived(act, t, t.ahead + raw_ahead)
            act.wait_ge(piece_done, t.piece.at(1 + t.ahead))
            i = (t.piece.count + t.ahead) % SPLIT
            j = (t.raw.count + t.ahead + raw_ahead) % RAW
            nc.scalar.copy(w_hi[:, i, 0:n], ring[:, j, 0:n]).then_inc(hi_ready, 1)
            t.ahead += 1

        def split_vector(dve, t, n=PIECE, raw_ahead=0):
            dve.wait_ge(hi_ready, t.piece.at(1 + t.ahead))
            i = (t.piece.count + t.ahead) % SPLIT
            j = (t.raw.count + t.ahead + raw_ahead) % RAW
            nc.vector.tensor_tensor(w_lo[:, i, 0:n], ring[:, j, 0:n], w_hi[:, i, 0:n].bitcast(F32),
                                    ALU.subtract).then_inc(raw_used, 1)
            t.ahead += 1

        def used(t):
            t.add(raw=1, piece=1)
            t.ahead -= 1

        def split_arrived(pe, t, raw_ahead=0):
            pe.wait_ge(raw_used, t.raw.at(RAW + 1 + raw_ahead))

        def parts(t, n):
            i = t.piece.count % SPLIT
            b = PIECE // n
            return tuple(w[:, i, 0:b * n].rearrange("p (k n) -> p k n", n=n) for w in (w_hi, w_lo))

        def product(out, stat, moving, start, stop):
            (sh, sl), (mh, ml) = stat, moving
            nc.tensor.matmul(out, sh, mh, start=start, stop=False)
            nc.tensor.matmul(out, sh, ml, start=False, stop=False)
            return nc.tensor.matmul(out, sl, mh, start=False, stop=stop)

        def products_ready(eng, t, more=1):
            eng.wait_ge(piece_done, t.piece.at(more + SPLIT))

        KH = KD // 2
        x_lhs = lambda b, tt: (XTh[:, b, tt * P:(tt + 1) * P], XTl[:, b, tt * P:(tt + 1) * P])

        def project_sync(sp, t, w, c0, widths):
            for n in widths:
                for k0 in range(0, w.shape[0], KH * P):
                    load_piece(sp, t, blocks_of(w[k0:k0 + KH * P, c0:c0 + n]))
                c0 += n
                t.add(proj=1)

        def project_tensor(pe, t, lhs, widths, depth=2):
            for j, n in enumerate(widths):
                pe.wait_ge(proj_act, t.proj.at(1 if j == 0 else 0))
                pe.wait_ge(proj_dve, t.proj.at(1 if j == 0 else 0))
                for k in range(depth):
                    split_arrived(pe, t)
                    wh, wl = parts(t, n)
                    for tt in range(NT):
                        for b in range(KH):
                            last = product(ps[:, 2 * (j % 2) + tt, 0:n], lhs(k * KH + b, tt),
                                           (wh[:, b, :], wl[:, b, :]),
                                           start=(k == 0 and b == 0), stop=(k == depth - 1 and b == KH - 1))
                    last.then_inc(piece_done, 1)
                    t.add(raw=1, piece=1)
                t.add(proj=1)

        def project_first(eng, t, split, widths):
            for _ in range(2):
                split(eng, t, KH * widths[0])

        def project_move(eng, t, split, tt, widths, take, depth=2):
            sizes = [KH * n for n in widths for _ in range(depth)][t.ahead:]
            for j, n in enumerate(widths):
                for k in range(depth):
                    if k < depth - 1:
                        if sizes:
                            split(eng, t, sizes.pop(0))
                        t.add(piece=0)
                    else:
                        if sizes:
                            split(eng, t, sizes.pop(0))
                        eng.wait_ge(piece_done, t.piece.at(1 + SPLIT + k))
                        take(j, ps[:, 2 * (j % 2) + tt, 0:n]).then_inc(proj_act if tt == 0 else proj_dve, 1)
                for k in range(depth):
                    used(t)
                t.add(proj=1)

        def projected(eng, t):
            eng.wait_ge(proj_act, t.proj.at(1))
            eng.wait_ge(proj_dve, t.proj.at(1))

        def to_proj(eng, tt, c0, widths):
            starts = [c0 + sum(widths[:j]) for j in range(len(widths))]

            def take(j, src):
                dst = proj[:, tt, starts[j]:starts[j] + widths[j]]
                if tt == 0:
                    return nc.scalar.copy(dst, src)
                return nc.vector.tensor_copy(dst, src)

            return take

        def transpose_tensor(pe, t, groups):
            for g, blocks in enumerate(groups):
                bank = 4 + g % 2
                if g % 2 == 0:
                    pe.wait_ge(tr_act, t.tr_act.at(1))
                else:
                    pe.wait_ge(tr_dve, t.tr_dve.at(1))
                for n, c, src in blocks:
                    last = nc.tensor.transpose(ps[0:n, bank, c:c + src.shape[0]], src, ident[:, :])
                if g % 2 == 0:
                    last.then_inc(tr_to_act, 1)
                    t.add(tr_act=1)
                else:
                    last.then_inc(tr_to_dve, 1)
                    t.add(tr_dve=1)

        def transposed_move_scalar(act, t, groups):
            for g, moves in enumerate(groups):
                if g % 2 == 0:
                    act.wait_ge(tr_to_act, t.tr_act.at(1))
                    for dst, n, c0, c1, scale in moves:
                        if scale is None:
                            last = nc.scalar.copy(dst, ps[0:n, 4, c0:c1])
                        else:
                            last = nc.scalar.activation(dst, ps[0:n, 4, c0:c1], ACT.Copy, scale=scale)
                    last.then_inc(tr_act, 1)
                    t.add(tr_act=1)
                else:
                    t.add(tr_dve=1)

        def transposed_move_vector(dve, t, groups):
            for g, moves in enumerate(groups):
                if g % 2 == 1:
                    dve.wait_ge(tr_to_dve, t.tr_dve.at(1))
                    for dst, n, c0, c1, scale in moves:
                        if scale is None:
                            last = nc.vector.tensor_copy(dst, ps[0:n, 5, c0:c1])
                        else:
                            last = nc.vector.tensor_scalar(dst, ps[0:n, 5, c0:c1], scale, None, ALU.mult)
                    last.then_inc(tr_dve, 1)
                    t.add(tr_dve=1)
                else:
                    t.add(tr_act=1)

        def transposed(eng, t):
            eng.wait_ge(tr_act, t.tr_act.at(1))
            eng.wait_ge(tr_dve, t.tr_dve.at(1))

        def pairs(src, dst, blocks, scale=None):
            reads, moves = [], []
            for b in range(0, blocks, 2):
                got = [x for x in (b, b + 1) if x < blocks]
                reads.append([(src(x, tt).shape[1], (x - b) * S + tt * P, src(x, tt))
                              for x in got for tt in range(NT)])
                moves.append([(dst(x), src(x, 0).shape[1], (x - b) * S, (x - b + 1) * S,
                               scale(x) if scale else None) for x in got])
            return reads, moves

        def turn_groups(src, high, low, blocks, scale=None):
            reads, moves = [], []
            for b in range(0, blocks, 2):
                got = [x for x in (b, b + 1) if x < blocks]
                reads.append([((x - b) * S + tt * P, src(x, tt)) for x in got for tt in range(NT)])
                if scale is None:
                    n = len(got)
                    join = lambda a: a[:, b:b + n, :].rearrange("p b s -> p (b s)")
                    moves.append([(join(high), join(low), 0, n * S, None)])
                else:
                    moves.append([(high[:, x, :], low[:, x, :], (x - b) * S, (x - b + 1) * S, scale(x))
                                  for x in got])
            return reads, moves

        def x_groups(buf):
            return turn_groups(lambda b, tt: buf[:, tt, b * P:(b + 1) * P], XTh, XTl, KD)

        def turn_tensor(pe, t, groups):
            for g, blocks in enumerate(groups):
                pe.wait_ge(turned_lo, t.turn.at(1))
                for c, src in blocks:
                    last = nc.tensor.transpose(ps[:, 4 + g % 2, c:c + P], src, ident[:, :])
                last.then_inc(turned, 1)
                t.add(turn=1)
            pe.wait_ge(turned_lo, t.turn.at(2))

        def turn_scalar(act, t, groups):
            for g, moves in enumerate(groups):
                act.wait_ge(turned, t.turn.at(1))
                for high, low, c0, c1, scale in moves:
                    src = ps[:, 4 + g % 2, c0:c1]
                    if scale is None:
                        last = nc.scalar.copy(high, src)
                    else:
                        last = nc.scalar.activation(high, src, ACT.Copy, scale=scale)
                last.then_inc(turned_hi, 1)
                t.add(turn=1)

        def turn_vector(dve, t, groups):
            for g, moves in enumerate(groups):
                dve.wait_ge(turned_hi, t.turn.at(1))
                for high, low, c0, c1, scale in moves:
                    src = ps[:, 4 + g % 2, c0:c1]
                    if scale is None:
                        last = nc.vector.tensor_tensor(low, src, high.bitcast(F32), ALU.subtract)
                    else:
                        last = nc.vector.scalar_tensor_tensor(low, src, scale, high.bitcast(F32), ALU.mult,
                                                              ALU.subtract)
                last.then_inc(turned_lo, 1)
                t.add(turn=1)

        def row_tensor(pe, t, layer, r):
            pe.wait_ge(row_used, t.row.at(1))
            pe.wait_ge(y_used, t.y.at(0, 2) + 2)
            for h in range(2):
                last = nc.tensor.matmul(ps[:, 6 + h, :],
                                        ident[:, r:r + 1].to_broadcast([P, P]),
                                        rows[:, layer, h * 512:(h + 1) * 512], start=True, stop=True)
            last.then_inc(row_ready, 1)
            t.add(row=1)

        ROW = ps[:, 6:8, :].rearrange("p b n -> p (b n)")

        def rsqrt_scalar(act, t, n):
            act.wait_ge(dve_did, t.dve_step.at())
            nc.scalar.activation(rs[:, 1, 0:n], rs[:, 0, 0:n], ACT.Ln)
            act.drain()
            nc.scalar.activation(rs[:, 2, 0:n], rs[:, 1, 0:n], ACT.Exp, scale=-0.5).then_inc(act_did, 1)
            t.add(act_step=1)

        def softplus_vector(dve, t, n):
            u, e, l, s, m, o = (small[:, i, 0:n] for i in (0, 1, 2, 3, 4, 5))
            nc.vector.scalar_tensor_tensor(s, u, -1.0, u, ALU.mult, ALU.max).then_inc(dve_did, 1)
            t.add(dve_step=1, act_step=1)
            dve.wait_ge(act_did, t.act_step.at())
            nc.vector.tensor_scalar(m, e, LOG1P_SERIES_BELOW, None, ALU.is_lt)
            nc.vector.tensor_scalar(s, e, 0.2, None, ALU.mult)
            for c in (-0.25, 1.0 / 3.0, -0.5, 1.0):
                dve.drain()
                nc.vector.scalar_tensor_tensor(s, s, c, e, ALU.add, ALU.mult)
            dve.drain()
            nc.vector.tensor_tensor(s, s, l, ALU.subtract)
            dve.drain()
            nc.vector.tensor_tensor(s, s, m, ALU.mult)
            dve.drain()
            nc.vector.tensor_tensor(s, s, l, ALU.add)
            dve.drain()
            nc.vector.scalar_tensor_tensor(o, u, 0.0, s, ALU.max, ALU.add)
            dve.drain()

        def softplus_scalar(act, t, n):
            act.wait_ge(dve_did, t.dve_step.at(1))
            nc.scalar.activation(small[:, 1, 0:n], small[:, 3, 0:n], ACT.Exp, scale=-1.0)
            act.drain()
            nc.scalar.activation(small[:, 2, 0:n], small[:, 1, 0:n], ACT.Ln, bias=1.0).then_inc(act_did, 1)
            t.add(dve_step=1, act_step=1)

        def layer_norm_vector(dve, t):
            dve.drain()
            for tt in range(NT):
                for h in range(2):
                    nc.vector.bn_stats(stats[:, tt, h, :], Y[:, tt, h * 512:(h + 1) * 512])
            dve.drain()
            for tt in range(NT):
                nc.vector.bn_aggr(mv[:, tt, :], stats[:, tt, :, :].rearrange("p a b -> p (a b)"))
            dve.drain()
            nc.vector.tensor_scalar(rs[:, 0, 0:NT], mv[:, :, 1], 1e-5, None, ALU.add).then_inc(dve_did, 1)
            t.add(dve_step=1, act_step=1)
            dve.wait_ge(act_did, t.act_step.at())
            for tt in range(NT):
                nc.vector.tensor_scalar(Y[:, tt, :], Y[:, tt, :], mv[:, tt, 0:1], rs[:, 2, tt:tt + 1],
                                        ALU.subtract, ALU.mult)
            dve.drain()
            dve.wait_ge(row_ready, t.row.at(1))
            for tt in range(NT):
                last = nc.vector.tensor_tensor(Y[:, tt, :], Y[:, tt, :], ROW, ALU.mult)
            last.then_inc(row_used, 1)
            dve.drain()
            dve.wait_ge(row_ready, t.row.at(2))
            for tt in range(NT):
                last = nc.vector.tensor_tensor(X[:, tt, :], Y[:, tt, :], ROW, ALU.add)
            last.then_inc(row_used, 1)
            t.add(row=2, dve_step=1)
            dve.drain().then_inc(dve_did, 1)

        def layer_norm_scalar(act, t):
            t.add(dve_step=1)
            rsqrt_scalar(act, t, NT)
            t.add(row=2, dve_step=1)

        def layer_norm_tensor(pe, t, layer, g):
            row_tensor(pe, t, layer, g)
            row_tensor(pe, t, layer, g + 1)
            t.add(dve_step=2, act_step=1)

        def x_transpose_tensor(pe, t, buf):
            pe.wait_ge(dve_did, t.dve_step.at())
            turn_tensor(pe, t, x_groups(buf)[0])

        def up_sync(sp, t, w, n):
            if n == 512:
                load_piece(sp, t, blocks_of(w[0:KH * P, :]))
                load_piece(sp, t, blocks_of(w[KH * P:D, :]))
            else:
                load_piece(sp, t, blocks_of(w))

        def mlp_up_tensor(pe, t, n):
            for m in range(2):
                k = n // 256
                for i in range(k):
                    split_arrived(pe, t)
                    wh, wl = parts(t, n)
                    if m == 0 and i == 0:
                        pe.wait_ge(h_ready, t.mlp.at(1))
                    for tt in range(NT):
                        for b in range(KD // k):
                            last = product(ps[:, 2 * m + tt, 0:n], x_lhs(i * (KD // k) + b, tt),
                                           (wh[:, b, :], wl[:, b, :]), start=(i == 0 and b == 0),
                                           stop=(i == k - 1 and b == KD // k - 1))
                    last.then_inc(piece_done, 1)
                    t.add(raw=1, piece=1)

        def mlp_turn_tensor(pe, t, n):
            pe.wait_ge(h_ready, t.mlp.at(2))
            pe.wait_ge(hT_ready, t.mlp.at(1))
            for b in range(n // P):
                for tt in range(NT):
                    c = (b % 2) * S + tt * P
                    last = nc.tensor.transpose(ps[:, 4 + b // 2, c:c + P],
                                               mlp_h[:, tt, b * P:(b + 1) * P], ident[:, :])
            last.then_inc(hT_psum, 1)
            t.add(mlp=1)

        def mlp_down_tensor(pe, t, n, ada=None):
            pe.wait_ge(hT_ready, t.mlp.at(1))
            for h in range(2):
                split_arrived(pe, t)
                wh, wl = parts(t, 512)
                for tt in range(NT):
                    pe.wait_ge(y_used, t.y.at(0, 2) + (tt + 1))
                    for b in range(n // P):
                        s = slice(tt * P, (tt + 1) * P)
                        last = product(ps[:, 6 + tt, :], (hTh[:, b, s], hTl[:, b, s]),
                                       (wh[:, b, :], wl[:, b, :]), start=(b == 0), stop=(b == n // P - 1))
                    if tt == 0:
                        last.then_inc(y_ready, 1)
                last.then_inc(piece_done, 1)
                t.add(y=1, raw=1, piece=1)
                if ada is not None and h == 0:
                    ada_tensor(pe, t, ada)

        def silu_scalar(act, t, n):
            act.wait_ge(piece_done, t.piece.at(n // 256 + SPLIT))
            act.wait_ge(h_ready, t.mlp.at(1))
            nc.scalar.activation(mlp_silu[:, :, 0:n], ps[:, 0:2, 0:n], ACT.Silu).then_inc(silu_done, 1)

        def mlp_turn_scalar(act, t, n):
            act.wait_ge(hT_psum, t.mlp.at(1))
            w = n // P
            nc.scalar.copy(hTh[:, 0:w, :].rearrange("p b s -> p (b s)"),
                           ps[:, 4:4 + w // 2, :].rearrange("p b n -> p (b n)")).then_inc(hT_hi, 1)
            t.add(mlp=1)

        def h_vector(dve, t, n):
            dve.wait_ge(silu_done, t.mlp.at(1))
            dve.wait_ge(piece_done, t.piece.at(2 * (n // 256) + SPLIT))
            nc.vector.tensor_tensor(mlp_h[:, :, 0:n], mlp_silu[:, :, 0:n], ps[:, 2:4, 0:n],
                                    ALU.mult).then_inc(h_ready, 1)

        def mlp_turn_vector(dve, t, n):
            dve.wait_ge(hT_hi, t.mlp.at())
            w = n // P
            nc.vector.tensor_tensor(hTl[:, 0:w, :].rearrange("p b s -> p (b s)"),
                                    ps[:, 4:4 + w // 2, :].rearrange("p b n -> p (b n)"),
                                    hTh[:, 0:w, :].rearrange("p b s -> p (b s)").bitcast(F32),
                                    ALU.subtract).then_inc(hT_ready, 1)

        def y_vector(dve, t, h, weight, piece):
            for tt in range(NT):
                if tt == 0:
                    dve.wait_ge(y_ready, t.y.at(1))
                else:
                    dve.wait_ge(piece_done, t.piece.at(piece + SPLIT))
                yy = Y[:, tt, h * 512:(h + 1) * 512]
                nc.vector.scalar_tensor_tensor(yy, ps[:, 6 + tt, :], weight(tt), yy,
                                               ALU.mult, ALU.add).then_inc(y_used, 1)
            t.add(y=1)

        def ada_sync(sp, t, l, a, quarter):
            sp.wait_ge(h_ready, t.mlp.at(1))
            for j in range(3):
                sp.wait_ge(ada_read, t.ada.at(0, 3) + (j + 1))
                sp.dma_start(ada_ring[:, j, :].rearrange("p (k n) -> p k n", n=S),
                             blocks_of(A["ada_w_2"][l][:, bass.ds(a * D + quarter * 256 + 3 * j * D, 256)])
                             ).then_inc(ada_loaded[j], 16)
            t.add(ada=1)

        def ada_pool(pool, t, quarter):
            pool.wait_ge(ada_used, t.ada.at(1))
            for j in range(3):
                w = ada_ring[:, j, :].rearrange("p (k n) -> p k n", n=S)
                acc = ada_acc[:, bass.ds(quarter * (3 * S) + j * S, S)]
                pool.wait_ge(ada_loaded[j], t.ada.at(1, 16))
                nc.gpsimd.tensor_tensor(w, w, c_feat[:, :].unsqueeze(2).to_broadcast([P, KD, S]), ALU.mult)
                pool.drain()
                nc.gpsimd.tensor_tensor(w[:, 0:4, :], w[:, 0:4, :], w[:, 4:8, :], ALU.add)
                pool.drain()
                nc.gpsimd.tensor_tensor(w[:, 0:2, :], w[:, 0:2, :], w[:, 2:4, :], ALU.add)
                pool.drain()
                nc.gpsimd.tensor_tensor(acc, w[:, 0, :], w[:, 1, :], ALU.add).then_inc(ada_read, 1)
            pool.drain().then_inc(ada_ready, 1)
            t.add(ada=1)

        def ada_tensor(pe, t, quarter):
            pe.wait_ge(ada_ready, t.ada.at(1))
            for j in range(3):
                last = nc.tensor.matmul(ps[:, 4 + j // 2, (j % 2) * S:(j % 2 + 1) * S], ones[:, :],
                                        ada_acc[:, bass.ds(quarter * (3 * S) + j * S, S)], start=True, stop=True)
            last.then_inc(ada_psum, 1)

        def ada_rows_vector(dve, t, l, a, quarter):
            dve.wait_ge(ada_psum, t.ada.at(1))
            for j in range(3):
                row = rows[:, l, bass.ds(quarter * 256, 256)]
                last = nc.vector.scalar_tensor_tensor(
                    row, ps[:, 4 + j // 2, (j % 2) * S:(j % 2 + 1) * S],
                    ident[:, bass.ds(a + (ADAB + 3 * j), 1)], row, ALU.mult, ALU.add)
                dve.drain()
            dve.drain().then_inc(ada_used, 1)
            t.add(ada=1)

        def stage_sync(sp, t, w1, w3, w2, n, ada=None):
            up_sync(sp, t, w1, n)
            up_sync(sp, t, w3, n)
            if ada is not None:
                ada_sync(sp, t, *ada)
            load_piece(sp, t, blocks_of(w2[:, 0:512]))
            load_piece(sp, t, blocks_of(w2[:, 512:D]))
            t.add(mlp=1, y=2, piece=2 * (n // 256) + 2)

        def stage_tensor(pe, t, ada=None):
            mlp_up_tensor(pe, t, 512)
            mlp_down_tensor(pe, t, 512, ada)
            if ada is not None:
                pe.wait_ge(ada_used, t.ada.at(5))
                t.add(ada=1)
            mlp_turn_tensor(pe, t, 512)

        def stage_scalar(act, t, ada=False):
            split_scalar(act, t)
            silu_scalar(act, t, 512)
            for _ in range(5):
                split_scalar(act, t)
            for _ in range(6):
                used(t)
            t.add(y=2, ada=1 * ada)
            mlp_turn_scalar(act, t, 512)

        def stage_vector(dve, t, weight, ada=None):
            mlp_turn_vector(dve, t, 512)
            split_vector(dve, t)
            split_vector(dve, t)
            split_vector(dve, t)
            h_vector(dve, t, 512)
            split_vector(dve, t)
            y_vector(dve, t, 0, weight, 5)
            split_vector(dve, t)
            if ada is not None:
                ada_rows_vector(dve, t, *ada)
            y_vector(dve, t, 1, weight, 6)
            split_vector(dve, t)
            for _ in range(6):
                used(t)
            t.add(mlp=1)

        def per_stage(ada):
            adds = dict(raw=6, piece=6, mlp=1, y=2, ada=1 if ada else 0)
            return tuple(adds.get(n, 0) for n in TALLIES)

        def mlp_first(eng, t, split):
            split(eng, t)
            split(eng, t)

        def mlp_sync(sp, t, n, rest, w1, w3, w2, w1r=None, w3r=None, w2r=None, ada=None):
            up_sync(sp, t, w1(0), 512)
            up_sync(sp, t, w3(0), 512)
            t.add(mlp=1, piece=4)
            if ada is None:
                with t.loop(sp, n - 1, per_stage(False)) as i:
                    stage_sync(sp, t, w1(i + 1), w3(i + 1), w2(i), 512)
            else:
                with ada_loop(sp, t, 3, 4) as (a, q):
                    i = a * 4 + q
                    stage_sync(sp, t, w1(i + 1), w3(i + 1), w2(i), 512, (ada, a, q))
                with t.loop(sp, n - 13, per_stage(False)) as i:
                    stage_sync(sp, t, w1(i + 13), w3(i + 13), w2(i + 12), 512)
            if rest:
                stage_sync(sp, t, w1r, w3r, w2(n - 1), rest)
                load_piece(sp, t, blocks_of(w2r[:, 0:512]))
                load_piece(sp, t, blocks_of(w2r[:, 512:D]))
            else:
                load_piece(sp, t, blocks_of(w2(n - 1)[:, 0:512]))
                load_piece(sp, t, blocks_of(w2(n - 1)[:, 512:D]))
            t.add(y=2, piece=2)

        @contextmanager
        def ada_loop(eng, t, na, nq, adds=None):
            inner = tuple(adds.get(n, 0) for n in TALLIES) if adds else per_stage(True)
            with t.loop(eng, na, tuple(nq * k for k in inner)) as a:
                with t.loop(eng, nq, inner) as q:
                    yield a, q

        def mlp_tensor(pe, t, n, rest, ada=False):
            pe.wait_ge(row_used, t.row.at(1))
            mlp_up_tensor(pe, t, 512)
            mlp_turn_tensor(pe, t, 512)
            if ada:
                stage_tensor(pe, t)
                with ada_loop(pe, t, 3, 4) as (a, q):
                    stage_tensor(pe, t, q)
            with t.loop(pe, n - 1 - 13 * ada, per_stage(False)):
                stage_tensor(pe, t)
            if rest:
                mlp_up_tensor(pe, t, rest)
                mlp_down_tensor(pe, t, 512)
                mlp_turn_tensor(pe, t, rest)
                mlp_down_tensor(pe, t, rest)
            else:
                mlp_down_tensor(pe, t, 512)

        def mlp_scalar(act, t, n, rest, ada=False):
            split_scalar(act, t)
            silu_scalar(act, t, 512)
            split_scalar(act, t)
            split_scalar(act, t)
            split_scalar(act, t)
            for _ in range(4):
                used(t)
            mlp_turn_scalar(act, t, 512)
            if ada:
                stage_scalar(act, t)
                with ada_loop(act, t, 3, 4):
                    stage_scalar(act, t, True)
            with t.loop(act, n - 1 - 13 * ada, per_stage(False)):
                stage_scalar(act, t)
            if rest:
                split_scalar(act, t)
                silu_scalar(act, t, rest)
                split_scalar(act, t)
                split_scalar(act, t, 1024)
                split_scalar(act, t, 1024)
                for _ in range(4):
                    used(t)
                t.add(y=2)
                mlp_turn_scalar(act, t, rest)
            for _ in range(2):
                used(t)
            t.add(y=2)

        def mlp_vector(dve, t, n, rest, weight, ada=None):
            split_vector(dve, t)
            split_vector(dve, t)
            split_vector(dve, t)
            h_vector(dve, t, 512)
            split_vector(dve, t)
            for _ in range(4):
                used(t)
            t.add(mlp=1)
            if ada is not None:
                stage_vector(dve, t, weight(0))
                with ada_loop(dve, t, 3, 4) as (a, q):
                    stage_vector(dve, t, weight(a * 4 + q + 1), (ada, a, q))
                with t.loop(dve, n - 14, per_stage(False)) as i:
                    stage_vector(dve, t, weight(i + 13))
            else:
                with t.loop(dve, n - 1, per_stage(False)) as i:
                    stage_vector(dve, t, weight(i))
            if rest:
                mlp_turn_vector(dve, t, 512)
                split_vector(dve, t)
                split_vector(dve, t)
                h_vector(dve, t, rest)
                y_vector(dve, t, 0, weight(n - 1), 3)
                split_vector(dve, t, 1024)
                y_vector(dve, t, 1, weight(n - 1), 4)
                split_vector(dve, t, 1024)
                for _ in range(4):
                    used(t)
                t.add(mlp=1)
            mlp_turn_vector(dve, t, rest if rest else 512)
            last_weight = weight(n if rest else n - 1)
            dve.drain()
            y_vector(dve, t, 0, last_weight, 1)
            y_vector(dve, t, 1, last_weight, 2)
            for _ in range(2):
                used(t)
            dve.drain()

        W_IN = [474] * 8 + [468]
        q_mla = heads[:, 0:2, :]
        k_mla = heads[:, 2:4, :]
        CQ, CKV, KR = MLA, MLA + DQ, MLA + DQ + DKV

        def attention_sync(sp, t, l):
            project_sync(sp, t, A["w_in"][l], 0, W_IN)
            load_piece(sp, t, blocks_of(A["w_uq"][l]))
            load_piece(sp, t, blocks_of(A["w_ukv"][l]))
            t.add(proj=2)
            project_sync(sp, t, A["w_out"][l], 0, [512, 512])

        def input_blocks():
            def src(b, tt):
                c = b * P if b < 4 else FOX + (b - 4) * P if b < 8 else DIL + (b - 8) * P
                return proj[:, tt, c:c + P]

            reads, _ = pairs(src, lambda b: feat[:, b, :], 20)
            moves = [[(feat[:, b:b + 2, :].rearrange("p b s -> p (b s)"), P, 0, 2 * S, None)]
                     for b in range(0, 20, 2)]
            return reads, moves

        def mla_blocks():
            def src(b, tt):
                buf = q_mla if b < 4 else k_mla
                return buf[:, tt, (b % 4) * 96:(b % 4 + 1) * 96]

            reads, _ = pairs(src, lambda b: feat[0:96, 20 + b, :], 8)
            moves = [[(feat[0:96, 20 + b:22 + b, :].rearrange("p b s -> p (b s)"), 96, 0, 2 * S, None)]
                     for b in range(0, 8, 2)]
            return reads, moves

        def latent_blocks(l):
            src = lambda b, tt: proj[:, tt, CQ + b * P:CQ + (b + 1) * P]
            gain = lambda b: g_cq[:, l, b:b + 1] if b < 2 else g_ckv[:, bass.ds(l, 1)]
            return turn_groups(src, latent_h, latent_l, 3, gain)

        def attention_prepare_tensor(pe, t):
            x_transpose_tensor(pe, t, X)
            project_tensor(pe, t, x_lhs, W_IN)
            projected(pe, t)
            pe.wait_ge(params_ready, 1)
            pe.wait_ge(dve_did, t.dve_step.at(2))
            for tt in range(NT):
                last = nc.tensor.matmul(ps[0:4, 0, 0:S], small[:, 6, 4 * tt:4 * tt + 4], cum[:, tt, :],
                                        start=(tt == 0), stop=(tt == NT - 1))
            last.then_inc(pe_did, 1)
            pe.wait_ge(dve_did, t.dve_step.at(4))
            turn_tensor(pe, t, latent_blocks(0)[0])
            t.add(pe_step=1, act_step=3, dve_step=4)
            pe.wait_ge(dve_did, t.dve_step.at(1))
            for j, (b0, nb, n) in enumerate(((0, 2, 384), (2, 1, 512))):
                split_arrived(pe, t)
                wh, wl = parts(t, n)
                for tt in range(NT):
                    s = slice(tt * P, (tt + 1) * P)
                    for b in range(nb):
                        last = product(ps[:, 2 * j + tt, 0:n], (latent_h[:, b0 + b, s], latent_l[:, b0 + b, s]),
                                       (wh[:, b, :], wl[:, b, :]), start=(b == 0), stop=(b == nb - 1))
                last.then_inc(piece_done, 1)
                t.add(raw=1, piece=1, proj=1)
            transpose_tensor(pe, t, input_blocks()[0])
            pe.wait_ge(dve_did, t.dve_step.at(2))
            transpose_tensor(pe, t, mla_blocks()[0])
            transposed(pe, t)
            t.add(dve_step=2)

        def attention_prepare_scalar(act, t, l):
            project_first(act, t, split_scalar, W_IN)
            turn_scalar(act, t, x_groups(X)[1])
            project_move(act, t, split_scalar, 0, W_IN, to_proj(act, 0, 0, W_IN))
            for n in (2 * 384, 512):
                split_scalar(act, t, n)
            projected(act, t)
            act.wait_ge(params_ready, 1)
            for i, (c, n) in enumerate(((CQ, DQ), (CKV, DKV))):
                for tt in range(NT):
                    last = nc.scalar.activation(temp[:, 0:n], proj[:, tt, c:c + n], ACT.Square,
                                                accum_out=small[:, 7, 2 * i + tt:2 * i + tt + 1])
                    act.drain()
            act.drain().then_inc(act_did, 1)
            t.add(act_step=1)
            softplus_scalar(act, t, 8)
            t.add(dve_step=2)
            rsqrt_scalar(act, t, 4)
            t.add(dve_step=1)
            turn_scalar(act, t, latent_blocks(l)[1])
            t.add(pe_step=1)
            for dst, n in ((q_mla[:, 0, :], 384), (kv[:, 0, :], 512)):
                products_ready(act, t)
                nc.scalar.copy(dst, ps[:, 0 if n == 384 else 2, 0:n]).then_inc(proj_act, 1)
                used(t)
                t.add(proj=1)
            act.wait_ge(dve_did, t.dve_step.at(1))
            transposed_move_scalar(act, t, input_blocks()[1])
            transposed_move_scalar(act, t, mla_blocks()[1])
            t.add(dve_step=2)

        def rotate(dve, x1, x2, cos, sin, shape):
            n = int(np.prod(shape[1:]))
            names = "abc"[:len(shape) - 1]
            sizes = dict(zip(names, shape[1:]))
            pattern = f"p ({' '.join(names)}) -> p {' '.join(names)}"
            t1 = temp[:, 0:n].rearrange(pattern, **sizes)
            t2 = temp[:, 1536:1536 + n].rearrange(pattern, **sizes)
            nc.vector.tensor_tensor(t1, x1, sin, ALU.mult)
            nc.vector.tensor_tensor(t2, x2, sin, ALU.mult)
            dve.drain()
            nc.vector.tensor_tensor(x1, x1, cos, ALU.mult)
            nc.vector.tensor_tensor(x2, x2, cos, ALU.mult)
            dve.drain()
            nc.vector.tensor_tensor(x1, x1, t2, ALU.subtract)
            nc.vector.tensor_tensor(x2, x2, t1, ALU.add)
            dve.drain()

        def attention_prepare_vector(dve, t, l):
            project_first(dve, t, split_vector, W_IN)
            turn_vector(dve, t, x_groups(X)[1])
            project_move(dve, t, split_vector, 1, W_IN, to_proj(dve, 1, 0, W_IN))
            for n in (2 * 384, 512):
                split_vector(dve, t, n)
            projected(dve, t)
            dve.wait_ge(params_ready, 1)
            t.add(act_step=1)
            u = small[:, 0, 0:8].rearrange("p (t h) -> p t h", t=NT)
            nc.vector.tensor_tensor(u, proj[:, :, FOX + 768:FOX + 772],
                                    b_forget[:, l, :].unsqueeze(1).to_broadcast([P, NT, 4]), ALU.add)
            dve.drain()
            nc.vector.tensor_scalar(small[:, 0, 0:8], small[:, 0, 0:8], -1.0, None, ALU.mult)
            dve.drain()
            softplus_vector(dve, t, 8)
            nc.vector.tensor_scalar(small[:, 6, 0:8], small[:, 5, 0:8], -1.0, None,
                                    ALU.mult).then_inc(dve_did, 1)
            nc.vector.tensor_scalar(rs[:, 0, 0:2], small[:, 7, 0:2], 1.0 / DQ, 1e-6, ALU.mult, ALU.add)
            nc.vector.tensor_scalar(rs[:, 0, 2:4], small[:, 7, 2:4], 1.0 / DKV, 1e-6, ALU.mult, ALU.add)
            dve.drain().then_inc(dve_did, 1)
            t.add(dve_step=2, act_step=1)
            dve.wait_ge(act_did, t.act_step.at())
            for i, (c, n) in enumerate(((CQ, DQ), (CKV, DKV))):
                for tt in range(NT):
                    nc.vector.tensor_scalar(proj[:, tt, c:c + n], proj[:, tt, c:c + n],
                                            rs[:, 2, 2 * i + tt:2 * i + tt + 1], None, ALU.mult)
            dve.drain().then_inc(dve_did, 1)
            t.add(dve_step=1)
            turn_vector(dve, t, latent_blocks(l)[1])
            dve.wait_ge(pe_did, t.pe_step.at(1))
            t.add(pe_step=1)
            nc.vector.tensor_scalar(rowT[0:4, 0, :], ps[0:4, 0, 0:S], 8.0, None, ALU.mult)
            nc.vector.tensor_scalar(rowT[0:4, 1, :], ps[0:4, 0, 0:S], -8.0, None, ALU.mult)
            v = proj[:, :, DIL:DIL + 1536].rearrange("p t (h d) -> p t h d", d=HD)
            for tt in range(NT):
                rotate(dve, v[:, tt, :, 0:32], v[:, tt, :, 32:64],
                       rope64[:, tt, 0:32].unsqueeze(1).to_broadcast([P, 24, 32]),
                       rope64[:, tt, 32:64].unsqueeze(1).to_broadcast([P, 24, 32]), [P, 24, 32])
            dve.drain().then_inc(dve_did, 1)
            t.add(dve_step=1)
            for dst, n in ((q_mla[:, 1, :], 384), (kv[:, 1, :], 512)):
                products_ready(dve, t)
                nc.vector.tensor_copy(dst, ps[:, 1 if n == 384 else 3, 0:n]).then_inc(proj_dve, 1)
                used(t)
                t.add(proj=1)
            projected(dve, t)
            transposed_move_vector(dve, t, input_blocks()[1])
            kr = proj[:, :, KR:KR + DR]
            rotate(dve, kr[:, :, 0:16], kr[:, :, 16:32], rope32[:, :, 0:16], rope32[:, :, 16:32], [P, NT, 16])
            for tt in range(NT):
                qr = q_mla[:, tt, :].rearrange("p (h d) -> p h d", d=96)
                rotate(dve, qr[:, :, 64:80], qr[:, :, 80:96],
                       rope32[:, tt, 0:16].unsqueeze(1).to_broadcast([P, 4, 16]),
                       rope32[:, tt, 16:32].unsqueeze(1).to_broadcast([P, 4, 16]), [P, 4, 16])
                kc = k_mla[:, tt, :].rearrange("p (h d) -> p h d", d=96)
                nc.vector.tensor_copy(kc[:, :, 0:64], kv[:, tt, :].rearrange("p (h d) -> p h d", d=P)[:, :, 0:64])
                nc.vector.tensor_copy(kc[:, :, 64:96], kr[:, tt, :].unsqueeze(1).to_broadcast([P, 4, 32]))
            dve.drain().then_inc(dve_did, 1)
            t.add(dve_step=1)
            transposed_move_vector(dve, t, mla_blocks()[1])

        SBK = 4 * 384
        sb_z = temp[:, 0:SBK].rearrange("p (h n) -> p h n", n=384)
        sb_sp = temp[:, SBK:2 * SBK].rearrange("p (h n) -> p h n", n=384)
        sb_w = heads[:, 0:4, :]

        def pv_tensor(out_ps, pT, v):
            n = v(0).shape[-1]
            nc.tensor.matmul(out_ps[:, 0:n], pT[:, 0:P], v(0), start=True, stop=True)
            nc.tensor.matmul(out_ps[:, n:2 * n], pT[:, P:2 * P], v(0), start=True, stop=False)
            return nc.tensor.matmul(out_ps[:, n:2 * n], pT[:, 2 * P:3 * P], v(1), start=False, stop=True)

        def stick_tensor(pe, t):
            for h in range(4):
                b = (h % 2) * HD
                q, k = feat[b:b + HD, h // 2, :], feat[b:b + HD, 2 + h // 2, :]
                nc.tensor.matmul(ps[:, h, 0:S], k[:, 0:P], q, start=True, stop=True)
                last = nc.tensor.matmul(ps[:, h, S:384], k[:, P:S], q[:, P:S], start=True, stop=True)
            last.then_inc(pe_did, 1)
            pe.wait_ge(dve_did, t.dve_step.at(2))
            for h in range(4):
                nc.tensor.matmul(ps[:, 4 + h, 0:S], later[:, :], sb_sp[:, h, 0:S], start=True, stop=False)
                nc.tensor.matmul(ps[:, 4 + h, P:S], ones[:, :], sb_sp[:, h, S:384], start=False, stop=True)
                last = nc.tensor.matmul(ps[:, 4 + h, S:384], later[:, :], sb_sp[:, h, S:384],
                                        start=True, stop=True)
            last.then_inc(pe_did, 1)
            pe.wait_ge(act_did, t.act_step.at(2))
            for h in range(4):
                last = pv_tensor(ps[:, 7, h * P:(h + 1) * P], sb_w[:, h, :],
                                 lambda tt: proj[:, tt, 512 + h * HD:512 + (h + 1) * HD])
            last.then_inc(pe_did, 1)
            t.add(pe_step=3, act_step=2, dve_step=3)

        def stick_scalar(act, t):
            act.wait_ge(dve_did, t.dve_step.at(1))
            nc.scalar.activation(sb_w, sb_w, ACT.Exp, scale=-1.0)
            act.drain()
            nc.scalar.activation(sb_w, sb_w, ACT.Ln, bias=1.0).then_inc(act_did, 1)
            act.wait_ge(dve_did, t.dve_step.at(3))
            nc.scalar.activation(sb_w, sb_w, ACT.Exp).then_inc(act_did, 1)
            t.add(pe_step=3, act_step=2, dve_step=3)

        def stick_vector(dve, t):
            dve.wait_ge(pe_did, t.pe_step.at(1))
            for h in range(4):
                nc.vector.scalar_tensor_tensor(sb_z[:, h, :], ps[:, h, 0:384], HD ** -0.5, masks[:, 4, :],
                                               ALU.mult, ALU.add)
            dve.drain()
            nc.vector.scalar_tensor_tensor(sb_w, sb_z, -1.0, sb_z, ALU.mult, ALU.max).then_inc(dve_did, 1)
            dve.wait_ge(act_did, t.act_step.at(1))
            nc.vector.scalar_tensor_tensor(sb_sp, sb_z, 0.0, sb_w, ALU.max, ALU.add).then_inc(dve_did, 1)
            dve.wait_ge(pe_did, t.pe_step.at(2))
            for h in range(4):
                last = nc.vector.tensor_tensor(sb_w[:, h, :], sb_z[:, h, :], ps[:, 4 + h, 0:384], ALU.subtract)
            last.then_inc(dve_did, 1)
            dve.wait_ge(pe_did, t.pe_step.at(3))
            nc.vector.tensor_copy(heads_out[:, :, 0:4, :],
                                  ps[:, 7, :].rearrange("p (h t d) -> p t h d", h=4, t=NT))
            t.add(pe_step=3, act_step=2, dve_step=3)

        def head_list():
            out = []
            for h in range(4):
                out.append(dict(q=4 + h // 2, k=6 + h // 2, base=(h % 2) * HD, n=HD, scale=HD ** -0.5, mask=0,
                                forget=h, v=lambda tt, h=h: proj[:, tt, FOX + 512 + h * HD:FOX + 512 + (h + 1) * HD],
                                out=heads_out[:, :, 4 + h, :]))
            for h in range(4):
                out.append(dict(q=20 + h, k=24 + h, base=0, n=96, scale=96 ** -0.5, mask=0, forget=None,
                                v=lambda tt, h=h: kv[:, tt, h * P + 64:(h + 1) * P],
                                out=heads_out[:, :, 8 + h, :]))
            for n in range(12):
                out.append(dict(q=8 + n // 2, k=14 + n // 2, base=(n % 2) * HD, n=HD, scale=HD ** -0.5,
                                mask=1 + n // 4, forget=None,
                                v=lambda tt, n=n: proj[:, tt, DIL + 1536 + n * HD:DIL + 1536 + (n + 1) * HD],
                                out=dil_out[:, n // 4, :, n % 4, :]))
            return out

        HEADS = head_list()
        NH = len(HEADS)
        logits = lambda i: heads[:, i % 2, :]
        probs = lambda i: heads[:, 2 + i % 2, :]
        probsT = lambda i: heads[:, 4 + i % 2, :]

        def softmax_heads_tensor(pe, t):
            def scores(i):
                hd = HEADS[i]
                if i >= 2:
                    pe.wait_ge(logits_ready, t.head.at(i - 1))
                b, n, f = hd["base"], hd["n"], hd["forget"]
                q, k = feat[b:b + n, hd["q"], :], feat[b:b + n, hd["k"], :]
                for tt, (c0, nk) in enumerate(((0, P), (P, S))):
                    out = ps[:, i % 2, c0:c0 + nk]
                    last = nc.tensor.matmul(out, q[:, tt * P:(tt + 1) * P], k[:, 0:nk],
                                            start=True, stop=(f is None))
                    if f is not None:
                        pick = ident[0:4, f:f + 1]
                        nc.tensor.matmul(out, rowT[0:4, 0, tt * P:(tt + 1) * P],
                                         pick.to_broadcast([4, nk]), start=False, stop=False)
                        last = nc.tensor.matmul(out, pick.to_broadcast([4, P]), rowT[0:4, 1, 0:nk],
                                                start=False, stop=True)
                last.then_inc(scores_ready, 1)

            def turn(i):
                pe.wait_ge(probs_ready, t.head.at(i + 1))
                if i >= 2:
                    pe.wait_ge(probsT_ready, t.head.at(i - 1))
                for c in range(3):
                    last = nc.tensor.transpose(ps[:, 2 + i % 2, c * P:(c + 1) * P],
                                               probs(i)[:, c * P:(c + 1) * P], ident[:, :])
                last.then_inc(probs_turned, 1)

            def output(i):
                pe.wait_ge(probsT_ready, t.head.at(i + 1))
                if i >= 2:
                    pe.wait_ge(output_used, t.head.at(i - 1))
                pv_tensor(ps[:, 6 + i % 2, 0:2 * HD], probsT(i), HEADS[i]["v"]).then_inc(output_ready, 1)

            scores(0)
            scores(1)
            turn(0)
            for i in range(NH):
                if i + 2 < NH:
                    scores(i + 2)
                if i + 1 < NH:
                    turn(i + 1)
                output(i)
            t.add(head=NH)

        def softmax_heads_scalar(act, t):
            def exponentials(i):
                act.wait_ge(logits_ready, t.head.at(i + 1))
                if i >= 2:
                    act.wait_ge(probs_turned, t.head.at(i - 1))
                for tt, (c0, c1) in enumerate(((0, P), (P, 384))):
                    last = nc.scalar.activation(probs(i)[:, c0:c1], logits(i)[:, c0:c1], ACT.Exp,
                                                bias=nmax[:, i, tt:tt + 1], accum_out=den[:, i, tt:tt + 1])
                last.then_inc(probs_ready, 1)

            def move(i):
                act.wait_ge(probs_turned, t.head.at(i + 1))
                if i >= 2:
                    act.wait_ge(output_ready, t.head.at(i - 1))
                nc.scalar.copy(probsT(i), ps[:, 2 + i % 2, 0:384]).then_inc(probsT_ready, 1)

            exponentials(0)
            for i in range(NH):
                if i + 1 < NH:
                    exponentials(i + 1)
                move(i)
            t.add(head=NH)

        def softmax_heads_vector(dve, t):
            def mask(i):
                dve.wait_ge(scores_ready, t.head.at(i + 1))
                if i >= 2:
                    dve.wait_ge(probs_ready, t.head.at(i - 1))
                nc.vector.scalar_tensor_tensor(logits(i), ps[:, i % 2, 0:384], HEADS[i]["scale"],
                                               masks[:, HEADS[i]["mask"], :], ALU.mult, ALU.add)
                dve.drain()
                for tt, (c0, c1) in enumerate(((0, P), (P, 384))):
                    last = nc.vector.tensor_reduce(nmax[:, i, tt:tt + 1], logits(i)[:, c0:c1], AX, ALU.max,
                                                   negate=True)
                last.then_inc(logits_ready, 1)

            def use(i):
                dve.wait_ge(output_ready, t.head.at(i + 1))
                nc.vector.reciprocal(rden[:, i, :], den[:, i, :])
                dve.drain()
                nc.vector.tensor_tensor(HEADS[i]["out"], ps[:, 6 + i % 2, 0:2 * HD].rearrange("p (t d) -> p t d", t=NT),
                                        rden[:, i, :].unsqueeze(2).to_broadcast([P, NT, HD]),
                                        ALU.mult).then_inc(output_used, 1)

            mask(0)
            mask(1)
            for i in range(NH):
                if i + 2 < NH:
                    mask(i + 2)
                use(i)
            t.add(head=NH)

        OUT = [512, 512]
        lse3 = lse[:, 0:3, :].rearrange("p b (h t) -> p b h t", t=NT)
        DIL0 = NH - 12

        def head_blocks(l):
            src = lambda b, tt: wide[:, tt * D + b * P:tt * D + (b + 1) * P]
            return turn_groups(src, OTh, OTl, KD, lambda b: g_head[:, l, b:b + 1])

        o_lhs = lambda b, tt: (OTh[:, b, tt * P:(tt + 1) * P], OTl[:, b, tt * P:(tt + 1) * P])

        def attention_finish_tensor(pe, t, l):
            pe.wait_ge(dve_did, t.dve_step.at(5))
            turn_tensor(pe, t, head_blocks(0)[0])
            project_tensor(pe, t, o_lhs, OUT)
            t.add(act_step=4, dve_step=5)

        def attention_finish_scalar(act, t, l):
            project_first(act, t, split_scalar, OUT)
            act.drain()
            nc.scalar.activation(lse[:, 0:3, :].rearrange("p b n -> p (b n)"),
                                 den[:, DIL0:NH, :].rearrange("p h t -> p (h t)"), ACT.Ln).then_inc(act_did, 1)
            act.wait_ge(dve_did, t.dve_step.at(1))
            nc.scalar.activation(lse[:, 0:3, :], lse[:, 0:3, :], ACT.Exp).then_inc(act_did, 1)
            act.wait_ge(dve_did, t.dve_step.at(3))
            nc.scalar.activation(temp[:, 0:2048], wide[:, 0:2048], ACT.Square).then_inc(act_did, 1)
            t.add(act_step=3, dve_step=4)
            rsqrt_scalar(act, t, 32)
            t.add(dve_step=1)
            turn_scalar(act, t, head_blocks(l)[1])

            def take(j, src):
                return nc.scalar.copy(Y[:, 0, j * 512:(j + 1) * 512], src)

            project_move(act, t, split_scalar, 0, OUT, take)
            mlp_first(act, t, split_scalar)

        def attention_finish_vector(dve, t, l):
            m, total = lse[:, 3, :], lse[:, 4, :]
            project_first(dve, t, split_vector, OUT)
            dve.wait_ge(act_did, t.act_step.at(1))
            nm = nmax[:, DIL0:NH, :].rearrange("p (b h) t -> p b (h t)", b=3)
            nc.vector.tensor_tensor(lse[:, 0:3, :], lse[:, 0:3, :], nm, ALU.subtract)
            dve.drain()
            nc.vector.tensor_tensor(m, lse[:, 0, :], lse[:, 1, :], ALU.max)
            dve.drain()
            nc.vector.tensor_tensor(m, m, lse[:, 2, :], ALU.max)
            dve.drain()
            nc.vector.tensor_tensor(lse[:, 0:3, :], lse[:, 0:3, :], m.unsqueeze(1).to_broadcast([P, 3, 8]),
                                    ALU.subtract).then_inc(dve_did, 1)
            dve.wait_ge(act_did, t.act_step.at(2))
            nc.vector.tensor_tensor(total, lse[:, 0, :], lse[:, 1, :], ALU.add)
            dve.drain()
            nc.vector.tensor_tensor(total, total, lse[:, 2, :], ALU.add)
            dve.drain()
            nc.vector.reciprocal(total, total)
            dve.drain()
            nc.vector.tensor_tensor(lse[:, 0:3, :], lse[:, 0:3, :], total.unsqueeze(1).to_broadcast([P, 3, 8]),
                                    ALU.mult)
            dve.drain().then_inc(dve_did, 1)
            for b in range(3):
                w = lse3[:, b, :, :].rearrange("p h t -> p t h").unsqueeze(3).to_broadcast([P, NT, 4, HD])
                nc.vector.tensor_tensor(dil_out[:, b], dil_out[:, b], w, ALU.mult)
            dve.drain()
            nc.vector.tensor_tensor(dil_out[:, 0], dil_out[:, 0], dil_out[:, 1], ALU.add)
            dve.drain()
            nc.vector.tensor_tensor(heads_out[:, :, 12:16, :], dil_out[:, 0], dil_out[:, 2], ALU.add)
            dve.drain().then_inc(dve_did, 1)
            dve.wait_ge(act_did, t.act_step.at(3))
            nc.vector.tensor_reduce(small[:, 7, 0:32], temp[:, 0:2048].rearrange("p (n d) -> p n d", d=HD),
                                    AX, ALU.add)
            dve.drain()
            nc.vector.tensor_scalar(rs[:, 0, 0:32], small[:, 7, 0:32], 1.0 / HD, 1e-6, ALU.mult,
                                    ALU.add).then_inc(dve_did, 1)
            dve.wait_ge(act_did, t.act_step.at(4))
            w3 = wide[:, 0:2048].rearrange("p (n d) -> p n d", d=HD)
            nc.vector.tensor_tensor(w3, w3, rs[:, 2, 0:32].unsqueeze(2).to_broadcast([P, 32, HD]), ALU.mult)
            dve.drain().then_inc(dve_did, 1)
            t.add(act_step=4, dve_step=5)
            turn_vector(dve, t, head_blocks(l)[1])

            def take(j, src):
                s = slice(j * 512, (j + 1) * 512)
                return nc.vector.scalar_tensor_tensor(Y[:, 1, s], X[:, 1, s], ALPHA, src, ALU.mult, ALU.add)

            project_move(dve, t, split_vector, 1, OUT, take)
            projected(dve, t)
            nc.vector.scalar_tensor_tensor(Y[:, 0, :], X[:, 0, :], ALPHA, Y[:, 0, :], ALU.mult, ALU.add)
            mlp_first(dve, t, split_vector)

        def route_tensor(pe, t, l):
            x_transpose_tensor(pe, t, X)
            for tt in range(NT):
                for b in range(KD):
                    last = product(ps[:, tt, 0:20], x_lhs(b, tt), (wr_h[:, l, b, :], wr_l[:, l, b, :]),
                                   start=(b == 0), stop=(b == KD - 1))
            last.then_inc(pe_did, 1)
            t.add(pe_step=1, act_step=2, dve_step=2)
            pe.wait_ge(dve_did, t.dve_step.at())

        def route_scalar(act, t):
            turn_scalar(act, t, x_groups(X)[1])
            g = small[:, 1, 0:8]
            act.wait_ge(dve_did, t.dve_step.at(1))
            nc.scalar.activation(g, g, ACT.Exp).then_inc(act_did, 1)
            d = small[:, 2, 0:2]
            act.wait_ge(dve_did, t.dve_step.at(2))
            nc.scalar.activation(d, d, ACT.Exp).then_inc(act_did, 1)
            t.add(pe_step=1, act_step=2, dve_step=2)

        def route_vector(dve, t, l):
            turn_vector(dve, t, x_groups(X)[1])
            view = lambda i, n: small[:, i, 0:NT * n].rearrange("p (t n) -> p t n", t=NT)
            lg = view(0, 20)
            glog, elog = lg[:, :, 0:4], lg[:, :, 4:20]
            gexp, d = view(1, 4), view(2, 1)
            top, first, second = view(3, 1), view(4, 1), view(5, 1)
            group = view(6, 4)
            score, one, other = view(7, 16), view(8, 16), view(9, 16)
            gsum = view(10, 1)
            wide_ = lambda a, n: a.to_broadcast([P, NT, n])
            ranks = lambda n: rank[:, 0:n].unsqueeze(1).to_broadcast([P, NT, n])
            TT, TS = nc.vector.tensor_tensor, nc.vector.tensor_scalar

            def choose(dst, values, best, n):
                TT(dst, values, wide_(best, n), ALU.is_ge)
                dve.drain()
                TT(dst, dst, ranks(n), ALU.mult)
                dve.drain()
                nc.vector.tensor_reduce(top, dst, AX, ALU.max)
                dve.drain()
                TT(dst, dst, wide_(top, n), ALU.is_equal)
                dve.drain()

            dve.wait_ge(pe_did, t.pe_step.at(1))
            TT(lg, ps[:, 0:2, 0:20], b_router[:, l, :].unsqueeze(1).to_broadcast([P, NT, 20]), ALU.add)
            dve.drain()
            nc.vector.tensor_reduce(first, glog, AX, ALU.max)
            dve.drain()
            choose(group, glog, first, 4)
            TT(gexp, glog, wide_(first, 4), ALU.subtract).then_inc(dve_did, 1)
            dve.wait_ge(act_did, t.act_step.at(1))
            nc.vector.tensor_reduce(gsum, gexp, AX, ALU.add)
            TS(group, group, -NEG, NEG, ALU.mult, ALU.add)
            dve.drain()
            for tt in range(NT):
                e = elog[:, tt, :].rearrange("p (g e) -> p g e", e=4)
                TT(e, e, group[:, tt, :].unsqueeze(2).to_broadcast([P, 4, 4]), ALU.add)
            dve.drain()
            nc.vector.tensor_reduce(first, elog, AX, ALU.max)
            dve.drain()
            choose(one, elog, first, 16)
            nc.vector.scalar_tensor_tensor(elog, one, 2 * NEG, elog, ALU.mult, ALU.add)
            dve.drain()
            nc.vector.tensor_reduce(second, elog, AX, ALU.max)
            dve.drain()
            choose(other, elog, second, 16)
            TT(d, second, first, ALU.subtract).then_inc(dve_did, 1)
            dve.wait_ge(act_did, t.act_step.at(2))
            TS(first, d, 1.0, None, ALU.add)
            dve.drain()
            TT(first, first, gsum, ALU.mult)
            dve.drain()
            nc.vector.reciprocal(first, first)
            dve.drain()
            TT(second, first, d, ALU.mult)
            dve.drain()
            TT(one, one, wide_(first, 16), ALU.mult)
            TT(other, other, wide_(second, 16), ALU.mult)
            dve.drain()
            TT(gate[:, :, :], one, other, ALU.add)
            TS(Y[:, :, :], X[:, :, :], ALPHA, None, ALU.mult)
            dve.drain()
            t.add(pe_step=1, act_step=2, dve_step=2)

        def first_layer_sync(sp, t, l):
            attention_sync(sp, t, l)
            mlp_sync(sp, t, E, 0, lambda e: A["w1"][l, e], lambda e: A["w3"][l, e], lambda e: A["w2"][l, e],
                     ada=l)

        def first_layer_tensor(pe, t, l):
            attention_prepare_tensor(pe, t)
            stick_tensor(pe, t)
            softmax_heads_tensor(pe, t)
            attention_finish_tensor(pe, t, l)
            layer_norm_tensor(pe, t, l, LN1G)
            route_tensor(pe, t, l)
            mlp_tensor(pe, t, E, 0, True)
            layer_norm_tensor(pe, t, l, LN2G)

        def first_layer_scalar(act, t, l):
            attention_prepare_scalar(act, t, l)
            stick_scalar(act, t)
            softmax_heads_scalar(act, t)
            attention_finish_scalar(act, t, l)
            layer_norm_scalar(act, t)
            route_scalar(act, t)
            mlp_scalar(act, t, E, 0, True)
            layer_norm_scalar(act, t)

        def first_layer_vector(dve, t, l):
            attention_prepare_vector(dve, t, l)
            stick_vector(dve, t)
            softmax_heads_vector(dve, t)
            attention_finish_vector(dve, t, l)
            layer_norm_vector(dve, t)
            route_vector(dve, t, l)
            mlp_vector(dve, t, E, 0, lambda e: lambda tt: gate[:, tt, bass.ds(e, 1)], l)
            layer_norm_vector(dve, t)

        scale1 = temp[:, 0:D]
        flat = proj_all[:, :]
        post = flat[:, 2 * N_IN - D:2 * N_IN]

        def squares_scalar(act, t, buf):
            act.wait_ge(dve_did, t.dve_step.at())
            for tt in range(NT):
                nc.scalar.activation(temp[:, (1 + tt) * D:(2 + tt) * D], buf[:, tt, :], ACT.Square,
                                     accum_out=small[:, 7, tt:tt + 1])
            act.drain().then_inc(act_did, 1)
            t.add(act_step=1, dve_step=1)
            rsqrt_scalar(act, t, NT)

        def root_vector(dve, t, n, width, add=1e-6):
            t.add(act_step=1)
            dve.wait_ge(act_did, t.act_step.at())
            nc.vector.tensor_scalar(rs[:, 0, 0:n], small[:, 7, 0:n], 1.0 / width, add, ALU.mult,
                                    ALU.add).then_inc(dve_did, 1)
            t.add(dve_step=1, act_step=1)
            dve.wait_ge(act_did, t.act_step.at())

        BANKS = lambda k: ps[:, 2 * k:2 * k + 2, :].rearrange("p b n -> p (b n)")
        SCALE, GAIN, GATE, POST_GAIN, SHIFT = (BANKS(k) for k in (0, 1, 3, 2, 0))
        carried = wide[:, 0:NT * D].rearrange("p (t d) -> p t d", t=NT)

        def before_tensor(pe, t, l, s):
            projected(pe, t)
            pe.wait_ge(row_used, t.row.at(1))
            for k, r in ((0, ADAB + 3 * s + 1), (1, PRE + s), (3, ADAB + 3 * s + 2), (2, POST + s), (0, ADAB + 3 * s)):
                if k == 3:
                    pe.wait_ge(y_used, t.y.at(0, 2) + 2)
                if r == ADAB + 3 * s:
                    pe.wait_ge(row_used, t.row.at(-1))
                for h in range(2):
                    last = nc.tensor.matmul(ps[:, 2 * k + h, :], ident[:, r:r + 1].to_broadcast([P, P]),
                                            rows[:, l, h * 512:(h + 1) * 512], start=True, stop=True)
                last.then_inc(row_ready, 1)
                t.add(row=1)
            t.add(act_step=2, dve_step=2)
            x_transpose_tensor(pe, t, Y)

        def before_scalar(act, t, first):
            squares_scalar(act, t, X)
            first(act, t, split_scalar)
            t.add(dve_step=1, row=5)
            turn_scalar(act, t, x_groups(Y)[1])

        def scale_vector(dve, t):
            dve.wait_ge(row_ready, t.row.at(1))
            nc.vector.tensor_copy(scale1, SCALE).then_inc(row_used, 1)
            dve.drain()
            dve.wait_ge(row_ready, t.row.at(2))
            nc.vector.scalar_tensor_tensor(scale1, scale1, 1.0, GAIN, ALU.add, ALU.mult).then_inc(row_used, 1)
            t.add(row=2)
            dve.drain()

        def before_vector(dve, t, weight, clear, first):
            STT, TT = nc.vector.scalar_tensor_tensor, nc.vector.tensor_tensor
            for tt in range(NT):
                TT(carried[:, tt, :], X[:, tt, :], scale1, ALU.mult)
            dve.wait_ge(row_ready, t.row.at(1))
            nc.vector.tensor_copy(post, GATE).then_inc(row_used, 1)
            dve.drain()
            dve.wait_ge(row_ready, t.row.at(2))
            STT(post, post, weight, POST_GAIN, ALU.mult, ALU.mult).then_inc(row_used, 1)
            t.add(row=2)
            dve.drain()
            root_vector(dve, t, NT, D)
            dve.wait_ge(row_ready, t.row.at(1))
            for tt in range(NT):
                last = STT(Y[:, tt, :], carried[:, tt, :], rs[:, 2, tt:tt + 1], SHIFT, ALU.mult, ALU.add)
            last.then_inc(row_used, 1)
            dve.drain().then_inc(dve_did, 1)
            t.add(dve_step=1, row=1)
            first(dve, t, split_vector)
            turn_vector(dve, t, x_groups(Y)[1])
            if clear:
                nc.vector.memset(Y[:, :, :], 0.0)
                dve.drain()

        def after_tensor(pe, t):
            t.add(act_step=2, dve_step=3)

        def after_scalar(act, t):
            t.add(dve_step=1)
            squares_scalar(act, t, Y)
            t.add(dve_step=1)

        def after_vector(dve, t, more):
            dve.drain().then_inc(dve_did, 1)
            t.add(dve_step=1)
            for tt in range(NT):
                nc.vector.tensor_tensor(carried[:, tt, :], Y[:, tt, :], post, ALU.mult)
            if more:
                scale_vector(dve, t)
            dve.drain()
            root_vector(dve, t, NT, D)
            for tt in range(NT):
                nc.vector.scalar_tensor_tensor(X[:, tt, :], carried[:, tt, :], rs[:, 2, tt:tt + 1], X[:, tt, :],
                                               ALU.mult, ALU.add)
            dve.drain().then_inc(dve_did, 1)
            t.add(dve_step=1)

        FULL, REST = DFF // 512, DFF % 512

        def ffn_sync(sp, t, l, f):
            w1, w3, w2 = A["ffn_w1_2"][l, f], A["ffn_w3_2"][l, f], A["ffn_w2_2"][l, f]
            mlp_sync(sp, t, FULL, REST, lambda i: w1[:, bass.ds(i * 512, 512)],
                     lambda i: w3[:, bass.ds(i * 512, 512)], lambda i: w2[bass.ds(i * 512, 512), :],
                     w1[:, FULL * 512:DFF], w3[:, FULL * 512:DFF], w2[FULL * 512:DFF, :])

        one_weight = lambda i: lambda tt: 1.0

        ML_QK, ML_V = ML_HEADS * ML_DK, ML_HEADS * ML_DV
        ML_W = [512] * 6 + [8]
        ML_GATE = 2 * ML_QK + 2 * ML_V
        mlp_proj = flat[:, 0:NT * (ML_GATE + 8)].rearrange("p (t n) -> p t n", t=NT)
        gates_i, gates_f, F_tok, a_tok = (small[:, 8 + i, 0:8] for i in range(4))
        by_tile = lambda a: a.rearrange("p (t h) -> p t h", t=NT)
        ml_out = wide[:, 0:2 * D].rearrange("p (t n) -> p t n", t=NT)

        def to_buffer(buf, tt, widths):
            starts = [sum(widths[:j]) for j in range(len(widths))]

            def take(j, src):
                dst = buf[:, tt, starts[j]:starts[j] + widths[j]]
                return nc.scalar.copy(dst, src) if tt == 0 else nc.vector.tensor_copy(dst, src)

            return take

        def qk_blocks():
            src = lambda b, tt: mlp_proj[:, tt, b * P:(b + 1) * P]
            reads, _ = pairs(src, lambda b: feat[:, b, :], 8)
            return reads, [[(feat[:, b:b + 2, :].rearrange("p b s -> p (b s)"), P, 0, 2 * S, None)]
                           for b in range(0, 8, 2)]

        def ml_blocks():
            return turn_groups(lambda b, tt: ml_out[:, tt, b * P:(b + 1) * P], OTh, OTl, KD,
                               lambda b: ml_norm[:, b:b + 1])

        def mlstm_sync(sp, t):
            project_sync(sp, t, A["ml_w_in_2"][0], 0, ML_W)
            project_sync(sp, t, A["ml_w_out_2"][0], 0, OUT)

        def mlstm_tensor(pe, t):
            project_tensor(pe, t, x_lhs, ML_W)
            projected(pe, t)
            transpose_tensor(pe, t, qk_blocks()[0])
            transposed(pe, t)
            pe.wait_ge(dve_did, t.dve_step.at(2))
            for tt in range(NT):
                for st in range(NT):
                    last = nc.tensor.matmul(ps[:, 0, 4 * tt:4 * tt + 4], cum[:, st, tt * P:(tt + 1) * P],
                                            small[:, 6, 4 * st:4 * st + 4], start=(st == 0), stop=(st == NT - 1))
            last.then_inc(pe_did, 1)
            pe.wait_ge(dve_did, t.dve_step.at(3))
            for tt in range(NT):
                last = nc.tensor.transpose(ps[0:4, 1, tt * P:(tt + 1) * P], a_tok[:, 4 * tt:4 * tt + 4], ident[:, :])
            last.then_inc(pe_did, 1)
            pe.wait_ge(dve_did, t.dve_step.at(4))
            t.add(pe_step=2, act_step=1, dve_step=4)
            for h in range(ML_HEADS):
                q, k = feat[:, h, :], feat[:, 4 + h, :]
                pick = ident[0:4, h:h + 1].to_broadcast([4, P])
                for tt, (c0, nk) in enumerate(((0, P), (P, S))):
                    nc.tensor.matmul(ps[:, 0, c0:c0 + nk], pick, rowT[0:4, 0, 0:nk], start=True, stop=True)
                    last = nc.tensor.matmul(ps[:, 1, c0:c0 + nk], q[:, tt * P:(tt + 1) * P], k[:, 0:nk],
                                            start=True, stop=True)
                last.then_inc(pe_did, 1)
                pe.wait_ge(dve_did, t.dve_step.at(2))
                for c in range(3):
                    last = nc.tensor.transpose(ps[:, 2, c * P:(c + 1) * P], heads[:, 2, c * P:(c + 1) * P],
                                               ident[:, :])
                last.then_inc(pe_did, 1)
                pe.wait_ge(act_did, t.act_step.at(2))
                pv_tensor(ps[:, 3, :], heads[:, 4, :],
                          lambda tt: mlp_proj[:, tt, 2 * ML_QK + h * ML_DV:2 * ML_QK + (h + 1) * ML_DV]
                          ).then_inc(pe_did, 1)
                t.add(pe_step=3, act_step=2, dve_step=3)
                pe.wait_ge(dve_did, t.dve_step.at())
            t.add(act_step=3, dve_step=3)
            pe.wait_ge(dve_did, t.dve_step.at())
            turn_tensor(pe, t, ml_blocks()[0])
            project_tensor(pe, t, o_lhs, OUT)

        def mlstm_scalar(act, t):
            project_move(act, t, split_scalar, 0, ML_W, to_buffer(mlp_proj, 0, ML_W))
            project_first(act, t, split_scalar, OUT)
            transposed_move_scalar(act, t, qk_blocks()[1])
            softplus_scalar(act, t, 8)
            t.add(pe_step=2, dve_step=3)
            for h in range(ML_HEADS):
                act.wait_ge(dve_did, t.dve_step.at(1))
                for tt, (c0, c1) in enumerate(((0, P), (P, 384))):
                    nc.scalar.activation(heads[:, 1, c0:c1], heads[:, 0, c0:c1], ACT.Exp,
                                         bias=nmax[:, h, tt:tt + 1])
                nc.scalar.activation(rden[:, h, :], den[:, h, :], ACT.Exp)
                act.drain().then_inc(act_did, 1)
                act.wait_ge(pe_did, t.pe_step.at(2))
                nc.scalar.copy(heads[:, 4, :], ps[:, 2, 0:384]).then_inc(act_did, 1)
                t.add(pe_step=3, act_step=2, dve_step=3)
            projected(act, t)
            act.wait_ge(dve_did, t.dve_step.at())
            o = mlp_proj[:, :, 2 * ML_QK + ML_V:ML_GATE]
            nc.scalar.activation(o, o, ACT.Sigmoid)
            nc.scalar.activation(temp[:, 0:2 * D], wide[:, 0:2 * D], ACT.Square)
            act.drain().then_inc(act_did, 1)
            t.add(act_step=1, dve_step=1)
            rsqrt_scalar(act, t, 8)
            t.add(act_step=1, dve_step=2)
            act.drain().then_inc(act_did, 1)
            turn_scalar(act, t, ml_blocks()[1])
            project_move(act, t, split_scalar, 0, OUT, lambda j, src: nc.scalar.copy(Y[:, 0, j * 512:(j + 1) * 512], src))

        def mlstm_vector(dve, t):
            project_move(dve, t, split_vector, 1, ML_W, to_buffer(mlp_proj, 1, ML_W))
            project_first(dve, t, split_vector, OUT)
            projected(dve, t)
            transposed_move_vector(dve, t, qk_blocks()[1])
            TT = nc.vector.tensor_tensor
            gates = mlp_proj[:, :, ML_GATE:ML_GATE + 8]
            for g, dst in ((0, gates_i), (1, gates_f)):
                TT(by_tile(dst), gates[:, :, 4 * g:4 * g + 4],
                   b_gate[:, 4 * g:4 * g + 4].unsqueeze(1).to_broadcast([P, NT, 4]), ALU.add)
            dve.drain()
            nc.vector.tensor_scalar(small[:, 0, 0:8], gates_f, -1.0, None, ALU.mult)
            dve.drain()
            softplus_vector(dve, t, 8)
            nc.vector.tensor_scalar(small[:, 6, 0:8], small[:, 5, 0:8], -1.0, None,
                                    ALU.mult).then_inc(dve_did, 1)
            dve.wait_ge(pe_did, t.pe_step.at(1))
            nc.vector.tensor_copy(F_tok, ps[:, 0, 0:8])
            dve.drain()
            TT(a_tok, gates_i, F_tok, ALU.subtract).then_inc(dve_did, 1)
            dve.wait_ge(pe_did, t.pe_step.at(2))
            nc.vector.tensor_copy(rowT[0:4, 0, :], ps[0:4, 1, 0:S]).then_inc(dve_did, 1)
            t.add(pe_step=2, dve_step=3)
            for h in range(ML_HEADS):
                dve.wait_ge(pe_did, t.pe_step.at(1))
                TT(heads[:, 0, :], ps[:, 0, 0:384], masks[:, 0, :], ALU.add)
                dve.drain()
                for tt, (c0, c1) in enumerate(((0, P), (P, 384))):
                    nc.vector.tensor_reduce(nmax[:, h, tt:tt + 1], heads[:, 0, c0:c1], AX, ALU.max, negate=True)
                dve.drain()
                nc.vector.tensor_scalar(nmax[:, h, :], nmax[:, h, :], 0.0, None, ALU.min)
                dve.drain()
                TT(den[:, h, :], nmax[:, h, :], by_tile(F_tok)[:, :, h], ALU.subtract)
                dve.drain().then_inc(dve_did, 1)
                dve.wait_ge(act_did, t.act_step.at(1))
                nc.vector.scalar_tensor_tensor(heads[:, 2, :], ps[:, 1, 0:384], ML_DK ** -0.5, heads[:, 1, :],
                                               ALU.mult, ALU.mult)
                dve.drain()
                for tt, (c0, c1) in enumerate(((0, P), (P, 384))):
                    nc.vector.tensor_reduce(den[:, h, tt:tt + 1], heads[:, 2, c0:c1], AX, ALU.add)
                dve.drain().then_inc(dve_did, 1)
                nc.vector.scalar_tensor_tensor(den[:, h, :], den[:, h, :], -1.0, den[:, h, :], ALU.mult, ALU.max)
                dve.drain()
                TT(den[:, h, :], den[:, h, :], rden[:, h, :], ALU.max)
                dve.drain()
                nc.vector.reciprocal(den[:, h, :], den[:, h, :])
                dve.wait_ge(pe_did, t.pe_step.at(3))
                dve.drain()
                for tt in range(NT):
                    nc.vector.tensor_scalar(ml_out[:, tt, h * ML_DV:(h + 1) * ML_DV],
                                            ps[:, 3, tt * ML_DV:(tt + 1) * ML_DV], den[:, h, tt:tt + 1], None,
                                            ALU.mult)
                dve.drain().then_inc(dve_did, 1)
                t.add(pe_step=3, act_step=2, dve_step=3)
            t.add(act_step=1)
            dve.wait_ge(act_did, t.act_step.at())
            nc.vector.tensor_reduce(small[:, 7, 0:8], temp[:, 0:2 * D].rearrange("p (n d) -> p n d", d=ML_DV),
                                    AX, ALU.add)
            dve.drain()
            nc.vector.tensor_scalar(rs[:, 0, 0:8], small[:, 7, 0:8], 1.0 / ML_DV, 1e-6, ALU.mult,
                                    ALU.add).then_inc(dve_did, 1)
            t.add(act_step=1, dve_step=1)
            dve.wait_ge(act_did, t.act_step.at())
            w3 = wide[:, 0:2 * D].rearrange("p (n d) -> p n d", d=ML_DV)
            TT(w3, w3, rs[:, 2, 0:8].unsqueeze(2).to_broadcast([P, 8, ML_DV]), ALU.mult)
            dve.drain().then_inc(dve_did, 1)
            t.add(act_step=1, dve_step=2)
            TT(ml_out, ml_out, mlp_proj[:, :, 2 * ML_QK + ML_V:ML_GATE], ALU.mult)
            dve.drain().then_inc(dve_did, 1)
            turn_vector(dve, t, ml_blocks()[1])
            project_move(dve, t, split_vector, 1, OUT, lambda j, src: nc.vector.tensor_copy(Y[:, 1, j * 512:(j + 1) * 512], src))
            projected(dve, t)

        MB_CB = 24
        Z_W = [512] * 4
        mb_z = flat[:, 0:NT * MB_DI].rearrange("p (t n) -> p t n", t=NT)
        xs = wide[:, :].rearrange("p (t n) -> p t n", t=NT)
        bc = temp[:, 0:4 * 384].rearrange("p (g n) -> p g n", n=384)
        conv_acc = temp[:, 1536:3072].rearrange("p (a n) -> p a n", n=S)
        dt_tok, dtA, a_mid = (small[:, 8 + i, :] for i in range(3))
        dt_bias, A_log, D_skip = (mb_head[:, i, :] for i in range(3))
        tok32 = lambda a: a.rearrange("p (t h) -> p t h", t=NT)

        def xs_blocks():
            reads, moves = [], []
            for tt in range(NT):
                for b in range(0, 16, 4):
                    reads.append([(P, i * P, feat[:, b + i, tt * P:(tt + 1) * P]) for i in range(4)])
                    moves.append([(xs[:, tt, b * P:(b + 4) * P], P, 0, 512, None)])
            return reads, moves

        def mb_blocks():
            return turn_groups(lambda b, tt: xs[:, tt, b * P:(b + 1) * P], MTh, MTl, 16,
                               lambda b: mb_norm[:, b:b + 1])

        def mamba_sync(sp, t):
            w = A["mb_w_in_2"][0]
            project_sync(sp, t, w, 0, Z_W)
            for j in range(MB_CB // 2):
                load_piece(sp, t, blocks_of(w[:, MB_DI + j * 256:MB_DI + (j + 1) * 256]))
            project_sync(sp, t, w, 2 * MB_DI + 2 * MB_G * P, [32])
            project_sync(sp, t, A["mb_w_out_2"][0], 0, OUT)

        def mamba_tensor(pe, t):
            project_tensor(pe, t, x_lhs, Z_W)
            projected(pe, t)
            for j in range(MB_CB // 2):
                if j >= 4:
                    pe.wait_ge(conv_read, 2 * (j - 3))
                split_arrived(pe, t)
                wh, wl = parts(t, 256)
                for i in range(2):
                    s = slice(i * P, (i + 1) * P)
                    for b in range(KD):
                        last = product(ps[:, j % 4, i * S:(i + 1) * S], (wh[:, b, s], wl[:, b, s]),
                                       (XTh[:, b, :], XTl[:, b, :]), start=(b == 0), stop=(b == KD - 1))
                last.then_inc(piece_done, 1)
                t.add(raw=1, piece=1)
            pe.wait_ge(conv_read, MB_CB)
            project_tensor(pe, t, x_lhs, [32])
            pe.wait_ge(conv_done, MB_CB)
            transpose_tensor(pe, t, xs_blocks()[0])
            transposed(pe, t)
            projected(pe, t)
            for g in range(MB_G):
                Bg, Cg = feat[:, 16 + g, :], feat[:, 20 + g, :]
                nc.tensor.matmul(ps[:, g, 0:S], Bg[:, 0:P], Cg, start=True, stop=True)
                last = nc.tensor.matmul(ps[:, g, S:384], Bg[:, P:S], Cg[:, P:S], start=True, stop=True)
            last.then_inc(pe_did, 1)
            pe.wait_ge(dve_did, t.dve_step.at(3))
            dA = tok32(dtA)
            for tt in range(NT):
                for st in range(NT):
                    nc.tensor.matmul(ps[:, 6, 32 * tt:32 * tt + 32], mid[:, st, tt * P:(tt + 1) * P],
                                     dA[:, st, :], start=(st == 0), stop=(st == NT - 1))
            for st in range(NT):
                last = nc.tensor.matmul(ps[0:32, 7, 0:S], dA[:, st, :], mid[:, st, :],
                                        start=(st == 0), stop=(st == NT - 1))
            last.then_inc(pe_did, 1)
            pe.wait_ge(dve_did, t.dve_step.at(4))
            t.add(pe_step=2, act_step=2, dve_step=4)

            def row(h):
                if h >= 4:
                    pe.wait_ge(decay_ready, h - 3)
                nc.tensor.matmul(ps[:, h % 4, 0:S], ident[0:32, h:h + 1].to_broadcast([32, P]),
                                 rowT[0:32, 0, :], start=True, stop=True).then_inc(decay_row, 1)

            def output(h):
                pe.wait_ge(weights_ready, h + 1)
                if h >= 2:
                    pe.wait_ge(state_used, h - 1)
                pv_tensor(ps[:, 6 + h % 2, 0:2 * HD], heads[:, 4 + h % 2, :],
                          lambda tt: xs[:, tt, h * HD:(h + 1) * HD]).then_inc(state_out, 1)

            for h in range(3):
                row(h)
            for h in range(MB_H):
                if h + 3 < MB_H:
                    row(h + 3)
                output(h)
            t.add(act_step=3, dve_step=4)
            pe.wait_ge(dve_did, t.dve_step.at())
            turn_tensor(pe, t, mb_blocks()[0])
            m_lhs = lambda b, tt: (MTh[:, b, tt * P:(tt + 1) * P], MTl[:, b, tt * P:(tt + 1) * P])
            project_tensor(pe, t, m_lhs, OUT, depth=4)

        def mamba_scalar(act, t):
            project_move(act, t, split_scalar, 0, Z_W, to_buffer(mb_z, 0, Z_W))
            split_scalar(act, t)
            split_scalar(act, t)
            for j in range(MB_CB // 2):
                split_scalar(act, t, PIECE if j < MB_CB // 2 - 2 else KH * 32)
                for b in (2 * j, 2 * j + 1):
                    act.wait_ge(conv_read, b + 1)
                    nc.scalar.activation(feat[:, b, :], conv_acc[:, b % 6, :], ACT.Silu,
                                         bias=conv_b[:, b:b + 1]).then_inc(conv_done, 1)
                used(t)
            projected(act, t)
            nc.scalar.activation(mb_z, mb_z, ACT.Silu)
            project_move(act, t, split_scalar, 0, [32], lambda j, src: nc.scalar.copy(tok32(dt_tok)[:, 0, :], src))
            project_first(act, t, split_scalar, OUT)
            transposed_move_scalar(act, t, xs_blocks()[1])
            softplus_scalar(act, t, 64)
            act.drain()
            nc.scalar.activation(A_log, A_log, ACT.Exp).then_inc(act_did, 1)
            t.add(pe_step=2, act_step=1, dve_step=3)
            for h in range(MB_H):
                act.wait_ge(decay_ready, h + 1)
                if h >= 2:
                    act.wait_ge(weights_ready, h - 1)
                nc.scalar.activation(heads[:, 2 + h % 2, :], heads[:, h % 2, :], ACT.Exp).then_inc(decays, 1)
            act.wait_ge(dve_did, t.dve_step.at(1))
            for i in range(NT):
                for g in range(4):
                    last = nc.scalar.activation(temp[:, 0:512], xs[:, i, g * 512:(g + 1) * 512], ACT.Square,
                                                accum_out=small[:, 7, 4 * i + g:4 * i + g + 1])
                    act.drain()
            act.drain().then_inc(act_did, 1)
            t.add(act_step=1, dve_step=2)
            rsqrt_scalar(act, t, 8)
            t.add(act_step=1, dve_step=2)
            act.drain().then_inc(act_did, 1)
            turn_scalar(act, t, mb_blocks()[1])
            project_move(act, t, split_scalar, 0, OUT,
                         lambda j, src: nc.scalar.copy(Y[:, 0, j * 512:(j + 1) * 512], src), depth=4)

        def mamba_vector(dve, t):
            TT, STT = nc.vector.tensor_tensor, nc.vector.scalar_tensor_tensor
            project_move(dve, t, split_vector, 1, Z_W, to_buffer(mb_z, 1, Z_W))
            split_vector(dve, t)
            split_vector(dve, t)
            for j in range(MB_CB // 2):
                split_vector(dve, t, PIECE if j < MB_CB // 2 - 2 else KH * 32)
                products_ready(dve, t)
                for i in range(2):
                    b = 2 * j + i
                    src = ps[:, j % 4, i * S:(i + 1) * S]
                    acc = conv_acc[:, b % 6, :]
                    if b >= 6:
                        dve.wait_ge(conv_done, b - 5)
                    nc.vector.tensor_scalar(acc, src, conv_w[:, 3, b:b + 1], None, ALU.mult)
                    for d in (1, 2, 3):
                        dve.drain()
                        last = STT(acc[:, d:S], src[:, 0:S - d], conv_w[:, 3 - d, b:b + 1], acc[:, d:S],
                                   ALU.mult, ALU.add)
                    last.then_inc(conv_read, 1)
                used(t)
            project_move(dve, t, split_vector, 1, [32], lambda j, src: nc.vector.tensor_copy(tok32(dt_tok)[:, 1, :], src))
            projected(dve, t)
            project_first(dve, t, split_vector, OUT)
            transposed_move_vector(dve, t, xs_blocks()[1])
            TT(tok32(small[:, 0, :]), tok32(dt_tok), dt_bias.unsqueeze(1).to_broadcast([P, NT, 32]), ALU.add)
            dve.drain()
            softplus_vector(dve, t, 64)
            t.add(act_step=1)
            dve.wait_ge(act_did, t.act_step.at())
            nc.vector.tensor_copy(dt_tok, small[:, 5, :])
            STT(tok32(dtA), tok32(small[:, 5, :]), -1.0, A_log.unsqueeze(1).to_broadcast([P, NT, 32]),
                ALU.mult, ALU.mult).then_inc(dve_did, 1)
            dve.wait_ge(pe_did, t.pe_step.at(1))
            nc.vector.tensor_copy(bc, ps[:, 0:4, 0:384])
            dve.drain().then_inc(dve_did, 1)
            dve.wait_ge(pe_did, t.pe_step.at(2))
            nc.vector.tensor_copy(a_mid, ps[:, 6, 0:64])
            nc.vector.tensor_copy(rowT[0:32, 0, :], ps[0:32, 7, 0:S])
            dve.drain().then_inc(dve_did, 1)
            t.add(pe_step=2, dve_step=3)
            am, dts = tok32(a_mid), tok32(dt_tok)

            def exponent(h):
                dve.wait_ge(decay_row, h + 1)
                if h >= 2:
                    dve.wait_ge(decays, h - 1)
                for st, (c0, c1) in enumerate(((0, S), (S, 384))):
                    last = STT(heads[:, h % 2, c0:c1], ps[:, h % 4, st * P:S], am[:, st, h:h + 1],
                               masks[:, 5, c0:c1], ALU.subtract, ALU.add)
                last.then_inc(decay_ready, 1)

            def weights(h):
                dve.wait_ge(decays, h + 1)
                if h >= 2:
                    dve.wait_ge(state_out, h - 1)
                for st, (c0, c1) in enumerate(((0, S), (S, 384))):
                    last = STT(heads[:, 4 + h % 2, c0:c1], heads[:, 2 + h % 2, c0:c1], dts[:, st, h:h + 1],
                               bc[:, h // (MB_H // MB_G), c0:c1], ALU.mult, ALU.mult)
                last.then_inc(weights_ready, 1)

            def use(h):
                dve.wait_ge(state_out, h + 1)
                x = xs[:, :, h * HD:(h + 1) * HD]
                STT(x, x, D_skip[:, h:h + 1], ps[:, 6 + h % 2, 0:2 * HD].rearrange("p (t d) -> p t d", t=NT),
                    ALU.mult, ALU.add).then_inc(state_used, 1)

            exponent(0)
            for h in range(MB_H):
                if h + 1 < MB_H:
                    exponent(h + 1)
                weights(h)
                if h >= 1:
                    use(h - 1)
            use(MB_H - 1)
            dve.drain()
            TT(xs, xs, mb_z, ALU.mult)
            dve.drain().then_inc(dve_did, 1)
            t.add(act_step=1, dve_step=1)
            dve.wait_ge(act_did, t.act_step.at())
            nc.vector.tensor_scalar(rs[:, 0, 0:8], small[:, 7, 0:8], 1.0 / 512, 1e-6, ALU.mult,
                                    ALU.add).then_inc(dve_did, 1)
            t.add(act_step=1, dve_step=1)
            dve.wait_ge(act_did, t.act_step.at())
            w3 = wide[:, :].rearrange("p (n d) -> p n d", d=512)
            TT(w3, w3, rs[:, 2, 0:8].unsqueeze(2).to_broadcast([P, 8, 512]), ALU.mult)
            dve.drain().then_inc(dve_did, 1)
            dve.drain().then_inc(dve_did, 1)
            t.add(act_step=1, dve_step=2)
            turn_vector(dve, t, mb_blocks()[1])
            project_move(dve, t, split_vector, 1, OUT,
                         lambda j, src: nc.vector.tensor_copy(Y[:, 1, j * 512:(j + 1) * 512], src), depth=4)
            projected(dve, t)

        def loads():
            a = A
            bcast = lambda v: v.partition_broadcast(P)
            out = [
                (masks[:, :, :], a["c_masks"]), (rope64[:, :, :], a["c_rope64"]), (rope32[:, :, :], a["c_rope32"]),
                (cum[:, :, :], a["c_cum"]), (mid[:, :, :], a["c_mid"]),
                (later[:, :], a["c_later"]), (rank[:, :], a["c_rank"]),
                (b_forget[:, :, :], bcast(a["b_forget"])),
                (b_router[:, :, 0:4], bcast(a["b_group"])), (b_router[:, :, 4:20], bcast(a["b_expert"])),
                (b_gate[:, :], bcast(a["ml_b_gate_2"][0])),
                (mb_head[:, 0, :], bcast(a["mb_dt_bias_2"][0])), (mb_head[:, 1, :], bcast(a["mb_A_log_2"][0])),
                (mb_head[:, 2, :], bcast(a["mb_D_2"][0])),
                (g_cq[:, :, :], a["g_cq"].rearrange("l (b p) -> p l b", p=P)),
                (g_ckv[:, :], a["g_ckv"].rearrange("l p -> p l")),
                (g_head[:, :, :], a["g_head"].rearrange("l (b h) d -> (h d) l b", h=2)),
                (ml_norm[:, :], a["ml_norm_w_2"][0].rearrange("(b p) -> p b", p=P)),
                (mb_norm[:, :], a["mb_norm_w_2"][0].rearrange("(b p) -> p b", p=P)),
                (conv_b[:, :], a["mb_conv_b_2"][0].rearrange("(b p) -> p b", p=P)),
            ]
            for j in range(4):
                out.append((conv_w[:, j, :], a["mb_conv_w_2"][0, j].rearrange("(b p) -> p b", p=P)))
            for l in range(L):
                out.append((w_router[:, l, :, 0:4], a["w_group"][l].rearrange("(b p) n -> p b n", p=P)))
                out.append((w_router[:, l, :, 4:20], a["w_expert"][l].rearrange("(b p) n -> p b n", p=P)))
            for i, n in enumerate(("ln1_g", "ln1_b", "ln2_g", "ln2_b")):
                out.append((rows[i:i + 1, :, :], a[n].unsqueeze(0)))
            for r, n in ((PRE, "norm_pre_2"), (POST, "norm_post_2")):
                out.append((rows[r:r + 3, :, :], a[n].rearrange("l s d -> s l d")))
            out.append((rows[ADAB:ADAB + 9, :, :], a["ada_b_2"].rearrange("l (r d) -> r l d", d=D)))
            return out

        LOADS = loads()
        assert len(LOADS) == N_LOADS, len(LOADS)
        ctx.enter_context(nc.allow_non_contiguous_dma(reason="small parameters, one feature a partition"))
        block = ctx.enter_context(nc.Block())

        SECOND = [(l, s) for l in range(L) for s in range(3)]

        def first_pieces(l, s):
            if s != 1:
                return mlp_first
            return lambda eng, t, split: project_first(eng, t, split, ML_W if l == 0 else Z_W)

        @block.sync
        def _(sp):
            t = Tallies()
            with t.loop(sp, L, SYNC_LAYER) as l:
                first_layer_sync(sp, t, l)
            for l, s in SECOND:
                if s != 1:
                    ffn_sync(sp, t, l, s // 2)
                elif l == 0:
                    mlstm_sync(sp, t)
                else:
                    mamba_sync(sp, t)
            sp.wait_ge(dve_did, END_STEPS)
            sp.dma_start(out[0].rearrange("(t p) d -> p t d", p=P), X[:, :, :]).then_inc(stored, 16)
            sp.wait_ge(stored, 16)

        @block.gpsimd
        def _(pool):
            t = Tallies()
            nc.gpsimd.memset(rows[:, :, :], 0.0).then_inc(ones_set, 1)
            nc.gpsimd.memset(ones[:, :], 1.0).then_inc(ones_set, 1)
            pool.wait_ge(ones_set, 2)
            for dst, src in LOADS:
                pool.dma_start(dst, src).then_inc(loaded, 16)
            pool.wait_ge(loaded, 16 * N_LOADS)
            flat = lambda w: w[:, :, :, :].rearrange("p l k n -> p (l k n)")
            nc.gpsimd.tensor_copy(flat(wr_h), flat(w_router))
            pool.drain()
            nc.gpsimd.tensor_tensor(flat(wr_l), flat(w_router), flat(wr_h).bitcast(F32), ALU.subtract)
            pool.drain().then_inc(params_ready, 1)
            pool.sem_inc(ada_read, 3)
            pool.wait_ge(act_did, 1)
            with t.loop(pool, L, POOL_LAYER):
                with ada_loop(pool, t, 3, 4, dict(ada=1)) as (a, q):
                    ada_pool(pool, t, q)

        @block.tensor
        def _(pe):
            t = Tallies()
            pe.sem_inc(piece_done, SPLIT)
            t.add(dve_step=1, act_step=1)
            pe.wait_ge(ident_loaded, 16)
            pe.wait_ge(dve_did, 1)
            with t.loop(pe, L, LAYER) as l:
                first_layer_tensor(pe, t, l)
            for l, s in SECOND:
                before_tensor(pe, t, l, s)
                if s != 1:
                    mlp_tensor(pe, t, FULL, REST)
                elif l == 0:
                    mlstm_tensor(pe, t)
                else:
                    mamba_tensor(pe, t)
                after_tensor(pe, t)
            done["pe"] = t.counts()

        @block.scalar
        def _(act):
            t = Tallies()
            act.dma_start(X[:, :, :], A["x"][0].rearrange("(t p) d -> p t d", p=P)).then_inc(x_loaded, 16)
            act.dma_start(ident[:, :], A["c_ident"]).then_inc(ident_loaded, 16)
            act.dma_start(c_feat[:, :], A["c_2"][0].rearrange("(b p) -> p b", p=P)).then_inc(c_loaded, 16)
            for s in (proj_act, tr_act):
                act.sem_inc(s, 1)
            t.add(dve_step=1)
            act.wait_ge(c_loaded, 16)
            nc.scalar.activation(c_feat[:, :], c_feat[:, :], ACT.Silu)
            act.drain().then_inc(act_did, 1)
            t.add(act_step=1)
            with t.loop(act, L, LAYER) as l:
                first_layer_scalar(act, t, l)
            for l, s in SECOND:
                before_scalar(act, t, first_pieces(l, s))
                if s != 1:
                    mlp_scalar(act, t, FULL, REST)
                elif l == 0:
                    mlstm_scalar(act, t)
                else:
                    mamba_scalar(act, t)
                after_scalar(act, t)
            done["act"] = t.counts()

        @block.vector
        def _(dve):
            t = Tallies()
            for s, n in ((proj_dve, 1), (tr_dve, 1), (row_used, 1), (h_ready, 1), (hT_ready, 1),
                         (y_used, 2), (turned_lo, 2), (ada_used, 4), (raw_used, RAW)):
                dve.sem_inc(s, n)
            dve.wait_ge(x_loaded, 16)
            dve.drain().then_inc(dve_did, 1)
            t.add(dve_step=1, act_step=1)
            with t.loop(dve, L, LAYER) as l:
                first_layer_vector(dve, t, l)
            scale_vector(dve, t)
            for l, s in SECOND:
                before_vector(dve, t, 0.5 if s != 1 else 1.0, s != 1, first_pieces(l, s))
                if s != 1:
                    mlp_vector(dve, t, FULL, REST, one_weight)
                elif l == 0:
                    mlstm_vector(dve, t)
                else:
                    mamba_vector(dve, t)
                after_vector(dve, t, (l, s) != SECOND[-1])
            done["dve"] = t.counts()

        assert done["pe"] == done["act"] == done["dve"], done
        assert done["dve"][TALLIES.index("dve_step")] == END_STEPS, done

    return nc


def kernel(**inputs):
    import concourse.bacc as bacc
    from concourse.bass_utils import run_bass_kernel_spmd

    arrays = {name: np.ascontiguousarray(a) for name, a in inputs.items()}
    arrays.update(shape_constants(inputs["x"].shape[1]))
    nc = bacc.Bacc("TRN2", target_bir_lowering=False, num_devices=1)
    A = {name: nc.dram_tensor(f"in_{name}", a.shape, F32, kind="ExternalInput").ap()
         for name, a in arrays.items()}
    out = nc.dram_tensor("out", inputs["x"].shape, F32, kind="ExternalOutput").ap()
    build(nc, A, out)
    result = run_bass_kernel_spmd(nc, [{f"in_{name}": a for name, a in arrays.items()}], core_ids=[0])
    return result.results[0]["out"]
```
